# Optimizing a Trainium2 kernel written in Bass

```python
import math
import jax
import jax.numpy as jnp
from jax import lax
import numpy as np

D_MODEL = 1024
BATCH = 1
SEQ = 512
DEPTH = 2

GRID_W = 64
CTX_LEN = 256
N_HEADS_TOTAL = 16
HEAD_DIM = D_MODEL // N_HEADS_TOTAL
N_HEADS_A = 4
N_KV_A = 2
N_HEADS_B = 4
DIFF_DIM = HEAD_DIM // 2
N_HEADS_C = 4
N_KV_C = 2
N_HEADS_D = 4
MIX_WIDTH = (N_HEADS_A + N_HEADS_B + N_HEADS_C + N_HEADS_D) * HEAD_DIM
Q_BLOCK = 128
WINDOW = 128
NA_ROWS = 8
NA_COLS = 16
ROPE_BASE = 10000.0
N_EXPERTS = 16
D_EXPERT = 1024
CAPACITY_FACTOR = 2
EPS = 1e-6
NEG_INF = -1e30
PROJ_WIDTHS = (
    N_HEADS_A * HEAD_DIM, N_KV_A * HEAD_DIM, N_KV_A * HEAD_DIM,
    N_HEADS_B * HEAD_DIM, N_HEADS_B * HEAD_DIM, N_HEADS_B * HEAD_DIM,
    N_HEADS_C * HEAD_DIM, N_KV_C * HEAD_DIM, N_KV_C * HEAD_DIM,
    N_HEADS_D * HEAD_DIM, N_HEADS_D * HEAD_DIM, N_HEADS_D * HEAD_DIM,
)
PROJ_DIM = sum(PROJ_WIDTHS)
SPLIT_POINTS = tuple(int(s) for s in np.cumsum(PROJ_WIDTHS)[:-1])

kernel_name = 'hybrid_dit_parallel_heads_ec_moe'

def rms_norm(x, gain):
    xf = x.astype(jnp.float32)
    y = xf * lax.rsqrt(jnp.mean(xf * xf, axis=-1, keepdims=True) + EPS)
    return (y * gain.astype(jnp.float32)).astype(x.dtype)

def modulate(h, shift, scale):
    return h * (1.0 + scale) + shift

def axial_rope_tables(n_tokens, dim, dtype):
    t = jnp.arange(n_tokens, dtype=jnp.int32)
    rows = (t // GRID_W).astype(jnp.float32)
    cols = (t % GRID_W).astype(jnp.float32)
    n_axis = dim // 4
    inv_freq = ROPE_BASE ** (-jnp.arange(n_axis, dtype=jnp.float32) / n_axis)
    ang = jnp.concatenate([rows[:, None] * inv_freq, cols[:, None] * inv_freq], axis=-1)
    return jnp.cos(ang).astype(dtype), jnp.sin(ang).astype(dtype)

def apply_rope(x, cos, sin):
    shape = (cos.shape[0],) + (1,) * (x.ndim - 3) + (cos.shape[1],)
    cos = cos.reshape(shape)
    sin = sin.reshape(shape)
    xr = x.reshape(x.shape[:-1] + (x.shape[-1] // 2, 2))
    x0, x1 = xr[..., 0], xr[..., 1]
    return jnp.stack([x0 * cos - x1 * sin, x0 * sin + x1 * cos], axis=-1).reshape(x.shape)

def gqa_dense(q, k, v):
    s = jnp.einsum('bqkgd,bskd->bkgqs', q, k).astype(jnp.float32) * (HEAD_DIM ** -0.5)
    p = jax.nn.softmax(s, axis=-1).astype(v.dtype)
    o = jnp.einsum('bkgqs,bskd->bqkgd', p, v)
    return o.reshape(o.shape[0], o.shape[1], -1)

def mixer_axial_gqa(q, k, v, qc, kc, vc, q_gain, k_gain, cos, sin, with_ctx):
    B, L, _ = q.shape
    Lc = kc.shape[1]
    G = N_HEADS_A // N_KV_A
    q = apply_rope(rms_norm(q.reshape(B, L, N_KV_A, G, HEAD_DIM), q_gain), cos, sin)
    k = apply_rope(rms_norm(k.reshape(B, L, N_KV_A, HEAD_DIM), k_gain), cos, sin)
    v = v.reshape(B, L, N_KV_A, HEAD_DIM)
    kc = rms_norm(kc.reshape(B, Lc, N_KV_A, HEAD_DIM), k_gain)
    vc = vc.reshape(B, Lc, N_KV_A, HEAD_DIM)
    k_all = jnp.concatenate([kc, k], axis=1)
    v_all = jnp.concatenate([vc, v], axis=1)
    q_blocks = jnp.moveaxis(q.reshape(B, L // Q_BLOCK, Q_BLOCK, N_KV_A, G, HEAD_DIM), 1, 0)
    out = lax.map(lambda qb: gqa_dense(qb, k_all, v_all), q_blocks)
    out = jnp.moveaxis(out, 0, 1).reshape(B, L, N_HEADS_A * HEAD_DIM)
    out_c = None
    if with_ctx:
        qc = rms_norm(qc.reshape(B, Lc, N_KV_A, G, HEAD_DIM), q_gain)
        out_c = gqa_dense(qc, kc, vc)
    return out, out_c

def mixer_differential(q, k, v, qc, kc, vc, lam_q1, lam_k1, lam_q2, lam_k2, subln_gain, lam_init,
                       cos, sin, with_ctx):
    B, L, _ = q.shape
    Lc = kc.shape[1]
    H = N_HEADS_B
    q = apply_rope(q.reshape(B, L, H, 2, DIFF_DIM), cos, sin)
    k = apply_rope(k.reshape(B, L, H, 2, DIFF_DIM), cos, sin)
    v = v.reshape(B, L, H, HEAD_DIM)
    kc = kc.reshape(B, Lc, H, 2, DIFF_DIM)
    vc = vc.reshape(B, Lc, H, HEAD_DIM)
    lam = (jnp.exp(jnp.sum(lam_q1.astype(jnp.float32) * lam_k1.astype(jnp.float32)))
           - jnp.exp(jnp.sum(lam_q2.astype(jnp.float32) * lam_k2.astype(jnp.float32))) + lam_init)

    def diff_attend(qb, kk, vv):
        s = jnp.einsum('bqhcd,bshcd->bhcqs', qb, kk).astype(jnp.float32) * (DIFF_DIM ** -0.5)
        p = jax.nn.softmax(s, axis=-1)
        a = (p[:, :, 0] - lam * p[:, :, 1]).astype(vv.dtype)
        o = jnp.einsum('bhqs,bshd->bqhd', a, vv)
        o = rms_norm(o, subln_gain) * (1.0 - lam_init)
        return o.reshape(o.shape[0], o.shape[1], H * HEAD_DIM)

    k_all = jnp.concatenate([kc, k], axis=1)
    v_all = jnp.concatenate([vc, v], axis=1)
    q_blocks = jnp.moveaxis(q.reshape(B, L // Q_BLOCK, Q_BLOCK, H, 2, DIFF_DIM), 1, 0)
    out = lax.map(lambda qb: diff_attend(qb, k_all, v_all), q_blocks)
    out = jnp.moveaxis(out, 0, 1).reshape(B, L, H * HEAD_DIM)
    out_c = None
    if with_ctx:
        out_c = diff_attend(qc.reshape(B, Lc, H, 2, DIFF_DIM), kc, vc)
    return out, out_c

def mixer_window_sink(q, k, v, qc, kc, vc, sink, cos, sin, with_ctx):
    B, L, _ = q.shape
    Lc = kc.shape[1]
    G = N_HEADS_C // N_KV_C
    nb = L // Q_BLOCK
    scale = HEAD_DIM ** -0.5
    q = apply_rope(q.reshape(B, L, N_KV_C, G, HEAD_DIM), cos, sin)
    k = apply_rope(k.reshape(B, L, N_KV_C, HEAD_DIM), cos, sin)
    v = v.reshape(B, L, N_KV_C, HEAD_DIM)
    kc = kc.reshape(B, Lc, N_KV_C, HEAD_DIM)
    vc = vc.reshape(B, Lc, N_KV_C, HEAD_DIM)
    sink_kg = sink.reshape(N_KV_C, G).astype(jnp.float32)

    def band(t):
        tp = jnp.pad(t, ((0, 0), (Q_BLOCK, Q_BLOCK), (0, 0), (0, 0)))
        tp = tp.reshape(B, nb + 2, Q_BLOCK, N_KV_C, HEAD_DIM)
        return jnp.concatenate([tp[:, :-2], tp[:, 1:-1], tp[:, 2:]], axis=2)

    kb, vb = band(k), band(v)
    qb = q.reshape(B, nb, Q_BLOCK, N_KV_C, G, HEAD_DIM)
    s_band = jnp.einsum('bnqkgd,bnskd->bnkgqs', qb, kb).astype(jnp.float32) * scale
    s_ctx = jnp.einsum('bnqkgd,bskd->bnkgqs', qb, kc).astype(jnp.float32) * scale
    blk = jnp.arange(nb)[:, None, None] * Q_BLOCK
    qpos = blk + jnp.arange(Q_BLOCK)[None, :, None]
    kpos = blk - Q_BLOCK + jnp.arange(3 * Q_BLOCK)[None, None, :]
    valid = (jnp.abs(kpos - qpos) <= WINDOW) & (kpos >= 0) & (kpos < L)
    s_band = jnp.where(valid[None, :, None, None], s_band, NEG_INF)
    s_sink = jnp.broadcast_to(sink_kg[None, None, :, :, None, None], s_ctx.shape[:-1] + (1,))
    p = jax.nn.softmax(jnp.concatenate([s_sink, s_ctx, s_band], axis=-1), axis=-1)
    p_ctx = p[..., 1:1 + Lc].astype(v.dtype)
    p_band = p[..., 1 + Lc:].astype(v.dtype)
    o = (jnp.einsum('bnkgqs,bskd->bnqkgd', p_ctx, vc)
         + jnp.einsum('bnkgqs,bnskd->bnqkgd', p_band, vb))
    out = o.reshape(B, L, N_HEADS_C * HEAD_DIM)
    out_c = None
    if with_ctx:
        qcg = qc.reshape(B, Lc, N_KV_C, G, HEAD_DIM)
        s = jnp.einsum('bqkgd,bskd->bkgqs', qcg, kc).astype(jnp.float32) * scale
        s_sink_c = jnp.broadcast_to(sink_kg[None, :, :, None, None], s.shape[:-1] + (1,))
        pc = jax.nn.softmax(jnp.concatenate([s_sink_c, s], axis=-1), axis=-1)[..., 1:].astype(v.dtype)
        out_c = jnp.einsum('bkgqs,bskd->bqkgd', pc, vc).reshape(B, Lc, N_HEADS_C * HEAD_DIM)
    return out, out_c

def mixer_neighbourhood(q, k, v, qc, kc, vc, rpb, with_ctx):
    B, L, _ = q.shape
    Lc = kc.shape[1]
    H = N_HEADS_D
    rows = L // GRID_W
    kr = min(NA_ROWS, rows)
    scale = HEAD_DIM ** -0.5
    qg = q.reshape(B, rows, GRID_W, H, HEAD_DIM)
    kg = k.reshape(B, rows, GRID_W, H, HEAD_DIM)
    vg = v.reshape(B, rows, GRID_W, H, HEAD_DIM)
    kc = kc.reshape(B, Lc, H, HEAD_DIM)
    vc = vc.reshape(B, Lc, H, HEAD_DIM)
    r = jnp.arange(rows)
    row_start = jnp.clip(r - kr // 2, 0, rows - kr)
    row_idx = row_start[:, None] + jnp.arange(kr)[None, :]
    k_strip = kg[:, row_idx]
    v_strip = vg[:, row_idx]
    cq = jnp.arange(GRID_W)
    col_start = jnp.clip(cq - NA_COLS // 2, 0, GRID_W - NA_COLS)
    col_valid = (cq[None, :] >= col_start[:, None]) & (cq[None, :] < col_start[:, None] + NA_COLS)
    ri = row_idx - r[:, None] + NA_ROWS - 1
    ci = jnp.clip(cq[None, :] - cq[:, None] + NA_COLS - 1, 0, 2 * NA_COLS - 2)
    bias = rpb[:, ri[:, None, :, None], ci[None, :, None, :]]
    bias = jnp.moveaxis(bias, 0, 1).astype(jnp.float32)
    s = jnp.einsum('brqhd,brkwhd->brhqkw', qg, k_strip).astype(jnp.float32) * scale + bias[None]
    s = jnp.where(col_valid[:, None, :], s, NEG_INF)
    s = s.reshape(B, rows, H, GRID_W, kr * GRID_W)
    s_ctx = jnp.einsum('brqhd,bshd->brhqs', qg, kc).astype(jnp.float32) * scale
    p = jax.nn.softmax(jnp.concatenate([s_ctx, s], axis=-1), axis=-1)
    p_ctx = p[..., :Lc].astype(v.dtype)
    p_nb = p[..., Lc:].reshape(B, rows, H, GRID_W, kr, GRID_W).astype(v.dtype)
    o = (jnp.einsum('brhqkw,brkwhd->brqhd', p_nb, v_strip)
         + jnp.einsum('brhqs,bshd->brqhd', p_ctx, vc))
    out = o.reshape(B, L, H * HEAD_DIM)
    out_c = None
    if with_ctx:
        qcg = qc.reshape(B, Lc, H, HEAD_DIM)
        sc = jnp.einsum('bqhd,bshd->bhqs', qcg, kc).astype(jnp.float32) * scale
        pc = jax.nn.softmax(sc, axis=-1).astype(v.dtype)
        out_c = jnp.einsum('bhqs,bshd->bqhd', pc, vc).reshape(B, Lc, H * HEAD_DIM)
    return out, out_c

def expert_choice_ffn(h, w_router, w_gate, w_up, w_down):
    B, T, D = h.shape
    cap = CAPACITY_FACTOR * T // N_EXPERTS
    aff = jax.nn.softmax(jnp.einsum('btd,de->bte', h, w_router).astype(jnp.float32), axis=-1)
    g, idx = lax.top_k(jnp.swapaxes(aff, 1, 2), cap)
    xe = jax.vmap(lambda hb, ib: hb[ib])(h, idx)
    a = jnp.einsum('becd,edf->becf', xe, w_gate)
    u = jnp.einsum('becd,edf->becf', xe, w_up)
    y = jnp.einsum('becf,efd->becd', jax.nn.silu(a) * u, w_down) * g[..., None].astype(h.dtype)
    return jax.vmap(lambda yb, ib: jnp.zeros((T, D), yb.dtype).at[ib.reshape(-1)].add(yb.reshape(-1, D)))(y, idx)

def setup_inputs(seed: int = 0) -> dict:
    key = jax.random.key(seed)
    ks = jax.random.split(key, 26)
    f32 = jnp.float32
    nrm = lambda k, shape, s: jax.random.normal(k, shape, f32) * s
    return {
        'x': nrm(ks[0], (BATCH, SEQ, D_MODEL), 1.0),
        'c': nrm(ks[1], (BATCH, D_MODEL), 1.0),
        'ctx': nrm(ks[2], (BATCH, CTX_LEN, D_MODEL), 1.0),
        'c_ctx': nrm(ks[3], (D_MODEL,), 1.0),
        'w_ada': nrm(ks[4], (DEPTH, D_MODEL, 6 * D_MODEL), 0.5 * D_MODEL ** -0.5),
        'b_ada': nrm(ks[5], (DEPTH, 6 * D_MODEL), 0.02),
        'g_pre_mix': 1.0 + nrm(ks[6], (DEPTH, D_MODEL), 0.05),
        'g_post_mix': 1.0 + nrm(ks[7], (DEPTH, D_MODEL), 0.05),
        'g_pre_ffn': 1.0 + nrm(ks[8], (DEPTH, D_MODEL), 0.05),
        'g_post_ffn': 1.0 + nrm(ks[9], (DEPTH, D_MODEL), 0.05),
        'w_in': nrm(ks[10], (DEPTH, D_MODEL, PROJ_DIM), D_MODEL ** -0.5),
        'w_out': nrm(ks[11], (DEPTH, MIX_WIDTH, D_MODEL), MIX_WIDTH ** -0.5),
        'q_gain_a': 1.0 + nrm(ks[12], (DEPTH, HEAD_DIM), 0.05),
        'k_gain_a': 1.0 + nrm(ks[13], (DEPTH, HEAD_DIM), 0.05),
        'lam_q1': nrm(ks[14], (DEPTH, DIFF_DIM), 0.1),
        'lam_k1': nrm(ks[15], (DEPTH, DIFF_DIM), 0.1),
        'lam_q2': nrm(ks[16], (DEPTH, DIFF_DIM), 0.1),
        'lam_k2': nrm(ks[17], (DEPTH, DIFF_DIM), 0.1),
        'subln_gain_b': 1.0 + nrm(ks[18], (DEPTH, HEAD_DIM), 0.05),
        'sink_c': nrm(ks[19], (DEPTH, N_HEADS_C), 0.5),
        'rpb_d': nrm(ks[20], (DEPTH, N_HEADS_D, 2 * NA_ROWS - 1, 2 * NA_COLS - 1), 0.5),
        'w_router': nrm(ks[21], (DEPTH, D_MODEL, N_EXPERTS), D_MODEL ** -0.5),
        'w_gate': nrm(ks[22], (DEPTH, N_EXPERTS, D_MODEL, D_EXPERT), D_MODEL ** -0.5),
        'w_up': nrm(ks[23], (DEPTH, N_EXPERTS, D_MODEL, D_EXPERT), D_MODEL ** -0.5),
        'w_down': nrm(ks[24], (DEPTH, N_EXPERTS, D_EXPERT, D_MODEL), D_EXPERT ** -0.5),
    }

def reference(x, c, ctx, c_ctx, w_ada, b_ada, g_pre_mix, g_post_mix, g_pre_ffn, g_post_ffn,
              w_in, w_out, q_gain_a, k_gain_a, lam_q1, lam_k1, lam_q2, lam_k2, subln_gain_b,
              sink_c, rpb_d, w_router, w_gate, w_up, w_down):
    B, L, D = x.shape
    cos_a, sin_a = axial_rope_tables(L, HEAD_DIM, x.dtype)
    cos_b, sin_b = axial_rope_tables(L, DIFF_DIM, x.dtype)
    xc = ctx
    for l in range(DEPTH):
        with_ctx = l < DEPTH - 1
        lam_init = 0.8 - 0.6 * math.exp(-0.3 * l)
        mod = (jax.nn.silu(c) @ w_ada[l] + b_ada[l])[:, None, :]
        mod_c = jax.nn.silu(c_ctx) @ w_ada[l] + b_ada[l]
        sh1, sc1, gt1, sh2, sc2, gt2 = jnp.split(mod, 6, axis=-1)
        sh1c, sc1c, gt1c, sh2c, sc2c, gt2c = jnp.split(mod_c, 6, axis=-1)

        h = modulate(rms_norm(x, g_pre_mix[l]), sh1, sc1)
        hc = modulate(rms_norm(xc, g_pre_mix[l]), sh1c, sc1c)
        p = jnp.split(h @ w_in[l], SPLIT_POINTS, axis=-1)
        pc = jnp.split(hc @ w_in[l], SPLIT_POINTS, axis=-1)
        oa, oa_c = mixer_axial_gqa(p[0], p[1], p[2], pc[0], pc[1], pc[2],
                                   q_gain_a[l], k_gain_a[l], cos_a, sin_a, with_ctx)
        ob, ob_c = mixer_differential(p[3], p[4], p[5], pc[3], pc[4], pc[5],
                                      lam_q1[l], lam_k1[l], lam_q2[l], lam_k2[l], subln_gain_b[l],
                                      lam_init, cos_b, sin_b, with_ctx)
        oc, oc_c = mixer_window_sink(p[6], p[7], p[8], pc[6], pc[7], pc[8],
                                     sink_c[l], cos_a, sin_a, with_ctx)
        od, od_c = mixer_neighbourhood(p[9], p[10], p[11], pc[9], pc[10], pc[11], rpb_d[l], with_ctx)
        o = jnp.concatenate([oa, ob, oc, od], axis=-1) @ w_out[l]
        x = x + gt1 * rms_norm(o, g_post_mix[l])
        if with_ctx:
            o_c = jnp.concatenate([oa_c, ob_c, oc_c, od_c], axis=-1) @ w_out[l]
            xc = xc + gt1c * rms_norm(o_c, g_post_mix[l])

        h = modulate(rms_norm(x, g_pre_ffn[l]), sh2, sc2)
        y = expert_choice_ffn(h, w_router[l], w_gate[l], w_up[l], w_down[l])
        x = x + gt2 * rms_norm(y, g_post_ffn[l])
        if with_ctx:
            hc = modulate(rms_norm(xc, g_pre_ffn[l]), sh2c, sc2c)
            yc = expert_choice_ffn(hc, w_router[l], w_gate[l], w_up[l], w_down[l])
            xc = xc + gt2c * rms_norm(yc, g_post_ffn[l])
    return x


_drawn_inputs = setup_inputs


def setup_inputs(seed=0):
    import zlib

    import numpy as np

    out = dict(_drawn_inputs(seed))
    spreads = {}
    factors = {'q_gain_a': 4.196, 'k_gain_a': 5.514, 'sink_c': 8.0}
    for name, (base, spread) in spreads.items():
        noise = np.random.default_rng([zlib.crc32(name.encode()), seed]).standard_normal(out[name].shape)
        drawn = base * np.exp(spread * noise) if base else spread * noise
        out[name] = jnp.asarray(drawn.astype(out[name].dtype))
    for name, factor in factors.items():
        out[name] = (out[name] * factor).astype(out[name].dtype)
    return out
```

```python
from contextlib import ExitStack
import math

import numpy as np
import concourse.bass as bass
from concourse import mybir

F32 = mybir.dt.float32
U32 = mybir.dt.uint32
ALU = mybir.AluOpType
ACT = mybir.ActivationFunctionType
AX_X = mybir.AxisListType.X

P = 128
D = 1024
KC = D // P
SEQ, CTX = 512, 256
NT, NC = (SEQ + CTX) // P, CTX // P
DEPTH = 2
HD = 64
GRID_W = 64
PROJ = 2560
NE = 16
CAP_X, CAP_C = 2 * SEQ // NE, 2 * CTX // NE
EPS = 1e-6
NEG = -1e30
SCALE = HD ** -0.5
SCALE_B = (HD // 2) ** -0.5
INV_SCALE = 1.0 / SCALE
KiB = 256

GROUPS = [
    [("qa", 0, 256, 0), ("ka", 256, 128, 1024), ("v", 384, 128, 0)],
    [("qb", 0, 256, 256), ("kb", 256, 256, 1152)],
    [("v", 0, 256, 128), ("qc", 256, 256, 512)],
    [("kc", 0, 128, 1408), ("v", 128, 128, 384), ("qd", 256, 256, 768)],
    [("kd", 0, 256, 1536), ("v", 256, 256, 512)],
]
KV_SPAN = [(256, 512), (256, 512), (0, 256), (0, 256), (0, 512)]


def lam_init(l):
    return 0.8 - 0.6 * math.exp(-0.3 * l)


def rope_table():
    t = np.arange(SEQ)
    parts = []
    for dim in (HD, HD // 2):
        n = dim // 4
        inv = (np.float32(10000.0) ** (-np.arange(n, dtype=np.float32) / np.float32(n))).astype(np.float32)
        rows = (t // GRID_W).astype(np.float32)
        cols = (t % GRID_W).astype(np.float32)
        ang = np.concatenate([rows[:, None] * inv, cols[:, None] * inv], axis=-1).astype(np.float32)
        cos, sin = np.cos(ang), np.sin(ang)
        parts += [np.repeat(cos, 2, axis=1), np.stack([-sin, sin], axis=-1).reshape(SEQ, dim)]
    return np.concatenate(parts, axis=1).astype(np.float32)


def attention_plan():
    scores, values = [], []
    for l in range(DEPTH):
        for t in range(0 if l < DEPTH - 1 else NC, NT):
            i = t - NC
            for mixer in "ABCD":
                for h in range(4):
                    for c in range(2 if mixer == "B" else 1):
                        u = dict(l=l, t=t, i=i, mixer=mixer, h=h, c=c, k=len(scores))
                        if i < 0:
                            u["segs"], u["vt"] = [(0, 0, 256)], [0, 1]
                        elif mixer == "C":
                            first, n = max(i - 1, 0), 3 if 0 < i < NT - NC - 1 else 2
                            u["segs"] = [(0, 0, 256), (256, CTX + P * first, 256)]
                            if n == 3:
                                u["segs"].append((512, CTX + P * (first + 2), P))
                            u["vt"] = [0, 1] + [NC + first + j for j in range(n)]
                            u["left"] = i > 0
                            u["right"] = i < NT - NC - 1
                        else:
                            u["segs"], u["vt"] = [(0, 0, 512), (512, 512, 256)], list(range(NT))
                        u["nk"] = len(u["vt"]) * P
                        if mixer in "AC":
                            u["half"], u["qp"] = h // 2, (0 if mixer == "A" else 4) + h % 2
                            u["kp"] = 0 if mixer == "A" else 3
                            u["vcol"] = (0 if mixer == "A" else 384) + HD * (h // 2)
                        else:
                            u["half"], u["qp"] = h % 2, (2 if mixer == "B" else 6) + h // 2
                            u["kp"] = (1 if mixer == "B" else 4) + h // 2
                            u["vcol"] = (128 if mixer == "B" else 512) + HD * h
                        u["ocol"] = 256 * "ABCD".index(mixer) + HD * h
                        scores.append(u)
                        if mixer != "B" or c == 1:
                            u["m"] = len(values)
                            values.append(u)
    wide = diffs = 0
    for v in values:
        wide += v["nk"] > 512
        v["wide"] = wide
        diffs += v["mixer"] == "B"
        v["diffs"] = diffs
    steps = []
    for l in range(DEPTH):
        mine = [u for u in scores if u["l"] == l]
        part = [dict(score=u, turn=[], pv=[]) for u in mine] + [dict(score=None, turn=[], pv=[]) for _ in range(4)]
        for v in values:
            if v["l"] == l:
                lag = 3 if v["mixer"] == "B" else 2
                part[v["k"] - mine[0]["k"] + lag]["turn"].append(v)
                part[v["k"] - mine[0]["k"] + lag + 1]["pv"].append(v)
        steps.append(part)
    return scores, values, steps


SCORES, VALUES, STEPS = attention_plan()
for _part in STEPS:
    for _no, _step in enumerate(_part):
        _step["no"] = _no


def _counts():
    raw_read, done = [], 0
    for l in range(DEPTH):
        for t in range(NT):
            for g in range(5):
                reads = not (g == 2 and l == DEPTH - 1 and t < NC)
                done += reads
                raw_read.append(done if reads else 0)
    p_last = []
    for u in SCORES:
        k = u["k"] - 4
        p_last.append(0 if k < 0 else min(v["m"] for v in VALUES if v["k"] >= k) + 1)
    sinks, done = [], 0
    for u in SCORES:
        done += u["mixer"] == "C"
        sinks.append(done)
    return raw_read, p_last, sinks


RAW_READ, P_LAST, SINKS = _counts()
ROW_TILES = [(l, t) for l in range(DEPTH) for t in range(0 if l < DEPTH - 1 else NC, NT)]
LAYER_ROWS = [[n for n, (l, _) in enumerate(ROW_TILES) if l == k] for k in range(DEPTH)]
LAYER_SCORES = [[u["k"] for u in SCORES if u["l"] == k] for k in range(DEPTH)]
LAYER_VALUES = [[v["m"] for v in VALUES if v["l"] == k] for k in range(DEPTH)]



def hybrid_dit(nc, I, out, xn_dram, y_dram, rp_dram):
    with ExitStack() as ctx:
        def sb(name, shape, dt=F32):
            return ctx.enter_context(nc.sbuf_tensor(name, shape, dt))

        def sem(name):
            return ctx.enter_context(nc.semaphore(name))

        X = sb("X", [P, NT, D])
        ident = sb("ident", [P, P])
        ones = sb("ones", [P, P])
        bandL = sb("bandL", [P, P])
        bandR = sb("bandR", [P, P])
        colmask = sb("colmask", [P, GRID_W])
        rope = sb("rope", [P, NT - NC, 192])
        modcol = sb("modcol", [P, DEPTH, 48, 2])
        gcol = sb("gcol", [P, KC, 8])
        mscale = sb("mscale", [P, DEPTH, 2, 2, KC])
        gate = sb("gate", [P, DEPTH, 2, 2, KC])
        cT = sb("cT", [P, KC, 2])
        qkgain = sb("qkgain", [P, DEPTH, 2, HD])
        subgain = sb("subgain", [P, DEPTH, HD])
        sink8 = sb("sink8", [P, DEPTH, 4])
        nsink8 = sb("nsink8", [P, DEPTH, 4])
        lamv = sb("lamv", [P, DEPTH, 4, 32])
        lamp = sb("lamp", [P, DEPTH, 2, 32])
        lams = sb("lams", [P, DEPTH, 2])
        nlam = sb("nlam", [P, DEPTH])
        halfneg = sb("halfneg", [P, 8])
        st = sb("st", [P, 64])
        wr = sb("wr", [P, KC, NE])
        arena = sb("arena", [P, 170 * KiB])

        def at(kib, shape, dt=None, parts=P):
            n = int(np.prod(shape))
            v = arena[0:parts, int(kib * KiB):int(kib * KiB) + n]
            if len(shape) > 1:
                names = "abcd"[:len(shape)]
                v = v.rearrange(f"p ({' '.join(names)}) -> p {' '.join(names)}",
                                **{x: s for x, s in zip(names[1:], shape[1:])})
            return v

        ada_ring = [at(80 + 16 * s, [KC, 512]) for s in range(3)]
        ada_row = [at(128 + 2 * s, [512], parts=2) for s in range(4)]
        crow, crow2 = at(0, [D], parts=2), at(4, [D], parts=2)
        grow = at(8, [D], parts=8)
        win = at(0, [KC, PROJ])
        qT = at(80, [8, NT * P])
        kT = at(104, [6, NT * P])
        V = at(122, [NT, 768])
        xn = at(140, [D])
        hT = [at(144 + 4 * s, [KC, P]) for s in range(2)]
        raw = [at(152 + 2 * s, [512]) for s in range(2)]
        tmp = [at(156 + 2 * s, [512]) for s in range(3)]
        qk = at(162, [1792])
        rpbT = at(0, [4, 14, GRID_W])
        wout = at(16, [KC, D])
        Ost = at(48, [NT, D])
        Pb = [at(140 + 3 * s, [768]) for s in range(4)]
        PT = [at(152 + 3 * s, [768]) for s in range(2)]
        rp = at(169.5, [P], parts=60)
        OT = [at(140 + 4 * s, [KC, P]) for s in range(2)]
        junk = at(148, [D])
        upd = at(152, [D])
        diag = at(156, [KC, P])
        GB = at(160, [2, D])
        RING = 8
        unit = [at(16 * s, [4096]) for s in range(RING)]
        xe = [at(128 + 4 * s, [D], parts=96) for s in range(2)]
        xeT = [at(136 + 3 * s, [KC, 96]) for s in range(2)]
        hs = at(142, [D], parts=96)
        hsT = at(146, [KC, 96])
        sg = at(149, [2, 512], parts=96)
        ysc = [at(153 + 4 * s, [D], parts=96) for s in range(2)]
        affT = at(161, [NT * P], parts=NE)
        aff2 = at(164, [SEQ], parts=NE)
        fxn = [at(128 + 4 * s, [D]) for s in range(2)]
        fhT = [at(136 + 4 * s, [KC, P]) for s in range(2)]
        yrow = [at(128 + 4 * s, [D]) for s in range(2)]
        yupd = at(136, [D])
        zero = at(165, [D])
        vals = sb("vals", [NE, 96])
        idxu = sb("idxu", [NE, 96], U32)
        idxf = sb("idxf", [NE, 96])
        gT = sb("gT", [96, NE])
        idxT = sb("idxT", [96, NE + 1], U32)
        idc = sb("idc", [96, 4], U32)
        nmx = sb("nmx", [P, 8])
        sumx = sb("sumx", [P, 8])
        skx = sb("skx", [P, 8])
        rx = sb("rx", [P, 8])
        lg = sb("lg", [P, 2, NE])

        ps = ctx.enter_context(nc.psum_tensor("ps", [P, 8, 512], F32))

        def pb(b, n=1):
            return ps[:, b:b + n, :].rearrange("p b n -> p (b n)")

        s_in = sem("s_in")
        s_in2 = sem("s_in2")
        s_x = sem("s_x")
        s_const = sem("s_const")
        s_adaw = [sem(f"s_adaw{s}") for s in range(3)]
        s_csT = sem("s_csT")
        s_cs = sem("s_cs")
        s_adam = sem("s_adam")
        s_adab = [sem(f"s_adab{s}") for s in range(4)]
        s_adar = sem("s_adar")
        s_adat = sem("s_adat")
        s_mod = sem("s_mod")
        s_win = [sem(f"s_win{g}") for g in range(5)]
        s_ss = sem("s_ss")
        s_rs = sem("s_rs")
        s_xn = sem("s_xn")
        s_xt = sem("s_xt")
        s_ht = sem("s_ht")
        s_prj = sem("s_prj")
        s_raw = sem("s_raw")
        s_rawf = sem("s_rawf")
        s_hss = sem("s_hss")
        s_hrs = sem("s_hrs")
        s_qk = sem("s_qk")
        s_qkt = sem("s_qkt")
        s_qkc = sem("s_qkc")
        s_rpi = sem("s_rpi")
        s_rpz = sem("s_rpz")
        s_rpw = sem("s_rpw")
        s_rpl = sem("s_rpl")
        s_bias = sem("s_bias")
        s_wout = sem("s_wout")
        s_sc = sem("s_sc")
        s_mx = sem("s_mx")
        s_ex = sem("s_ex")
        s_sk = sem("s_sk")
        s_cb = sem("s_cb")
        s_tn = sem("s_tn")
        s_ta = sem("s_ta")
        s_tb = sem("s_tb")
        s_pv = sem("s_pv")
        s_o = sem("s_o")
        s_gd = sem("s_gd")
        s_gm = sem("s_gm")
        s_gb = sem("s_gb")
        s_bss = sem("s_bss")
        s_brs = sem("s_brs")
        s_on = sem("s_on")
        s_ot = sem("s_ot")
        s_oc = sem("s_oc")
        s_om = sem("s_om")
        s_oss = sem("s_oss")
        s_ors = sem("s_ors")
        s_xu = sem("s_xu")
        s_wr = sem("s_wr")
        s_fss = sem("s_fss")
        s_frs = sem("s_frs")
        s_fxn = sem("s_fxn")
        s_fst = [sem("s_fst0"), sem("s_fst1")]
        s_ft = sem("s_ft")
        s_fh = sem("s_fh")
        s_fv = sem("s_fv")
        s_lg = sem("s_lg")
        s_lm = sem("s_lm")
        s_le = sem("s_le")
        s_lp = sem("s_lp")
        s_lt = sem("s_lt")
        s_lc = sem("s_lc")
        s_top = sem("s_top")
        s_tt = sem("s_tt")
        s_tc = sem("s_tc")
        s_w = [sem(f"s_w{s}") for s in range(RING)]
        s_wf = sem("s_wf")
        s_idc = sem("s_idc")
        s_g = [sem("s_g0"), sem("s_g1")]
        s_et = sem("s_et")
        s_ec = sem("s_ec")
        s_gu = sem("s_gu")
        s_eg = sem("s_eg")
        s_hs = sem("s_hs")
        s_hst = sem("s_hst")
        s_hsc = sem("s_hsc")
        s_yd = sem("s_yd")
        s_yc = sem("s_yc")
        s_sct = sem("s_sct")
        s_z = sem("s_z")
        s_yl = [sem("s_yl0"), sem("s_yl1")]
        s_yss = sem("s_yss")
        s_yrs = sem("s_yrs")
        s_yu = sem("s_yu")
        s_out = sem("s_out")
        s_vch = sem("s_vch")
        s_vlam = sem("s_vlam")
        s_ach = sem("s_ach")
        s_pch = sem("s_pch")

        block = ctx.enter_context(nc.Block())
        n_small = [0]

        def kind(t):
            return 0 if t < NC else 1

        def first_tile(l):
            return 0 if l < DEPTH - 1 else NC

        N_CLEAR = sum(NT - first_tile(l) for l in range(DEPTH))

        @block.sync
        def _(sp):
            def small(dst, src):
                sp.dma_start(dst, src).then_inc(s_in, 16)
                n_small[0] += 1

            small(crow[0:1, :], I["c_ctx"].rearrange("(a d) -> a d", a=1))
            small(crow[1:2, :], I["c"])
            for g, name in enumerate(("g_pre_mix", "g_post_mix", "g_pre_ffn", "g_post_ffn")):
                small(grow[2 * g:2 * g + 2, :], I[name])

            def ada_load(n):
                if n >= 4:
                    sp.wait_ge(s_adat, n - 3)
                sp.dma_start(ada_row[n % 4], bass.AP(I["b_ada"].tensor, 512 * n, [[0, 2], [1, 512]])
                             ).then_inc(s_adab[n % 4], 16)
                if n >= 3:
                    sp.wait_ge(s_adam, n - 2)
                sp.dma_start(ada_ring[n % 3],
                             I["w_ada"][n // 12].rearrange("(c p) n -> p c n", p=P)[:, :, 512 * (n % 12):512 * (n % 12) + 512]
                             ).then_inc(s_adaw[n % 3], 16)

            for n in range(12):
                ada_load(n)
            sp.dma_start(X[:, 0:NC, :], I["ctx"][0].rearrange("(t p) d -> p t d", p=P)).then_inc(s_x, 16)
            sp.dma_start(X[:, NC:NT, :], I["x"][0].rearrange("(t p) d -> p t d", p=P)).then_inc(s_x, 16)
            sp.wait_ge(s_cs, 3)
            for g in range(5):
                sp.dma_start(win[:, :, 512 * g:512 * g + 512],
                             I["w_in"][0].rearrange("(c p) n -> p c n", p=P)[:, :, 512 * g:512 * g + 512]
                             ).then_inc(s_win[g], 16)
            for n in range(12, 24):
                ada_load(n)

            def in2(dst, src):
                sp.dma_start(dst, src).then_inc(s_in2, 16)

            in2(rope[:], I["rope"].rearrange("(t p) n -> p t n", p=P))
            for l in range(DEPTH):
                in2(qkgain[:, l, 0, :], bass.AP(I["q_gain_a"].tensor, HD * l, [[0, P], [1, HD]]))
                in2(qkgain[:, l, 1, :], bass.AP(I["k_gain_a"].tensor, HD * l, [[0, P], [1, HD]]))
                for j, name in enumerate(("lam_q1", "lam_q2", "lam_k1", "lam_k2")):
                    in2(lamv[:, l, j, :], bass.AP(I[name].tensor, 32 * l, [[0, P], [1, 32]]))
            in2(subgain[:], bass.AP(I["subln_gain_b"].tensor, 0, [[0, P], [1, DEPTH * HD]]))
            in2(sink8[:], bass.AP(I["sink_c"].tensor, 0, [[0, P], [1, DEPTH * 4]]))

            sp.wait_ge(s_const, 2)
            for l in range(DEPTH):
                for t in range(NT - first_tile(l)):
                    sp.dma_start(y_dram[l][P * t:P * t + P, :], zero).then_inc(s_z, 16)

            for l in range(DEPTH):
                rows = LAYER_ROWS[l]
                if l == 0:
                    sp.wait_ge(s_z, 16 * N_CLEAR)
                sp.wait_ge(s_rpz, l + 1)
                sp.dma_start(rp[:, 48:79], I["rpb_d"][l].rearrange("h r c -> (h r) c")).then_inc(s_rpi, 16)
                sp.wait_ge(s_rpi, 16 * (l + 1))
                sp.dma_start(rp_dram[l].rearrange("c (r j) -> r c j", j=P),
                             rp.unsqueeze(1).broadcast_to([60, GRID_W, P])).then_inc(s_rpw, 16)
                sp.wait_ge(s_rpw, 16 * (l + 1))
                sp.wait_ge(s_prj, 5 * NT * (l + 1))
                for up in range(2):
                    for h in range(4):
                        src = bass.AP(rp_dram.tensor, l * GRID_W * 60 * P + 63 + P * (15 * h + 1 - up),
                                      [[60 * P - 1, GRID_W], [P, 14], [1, GRID_W]])
                        sp.dma_start(rpbT[64 * up:64 * up + 64, h], src).then_inc(s_rpl, 16)
                sp.dma_start(wout, I["w_out"][l].rearrange("(c p) n -> p c n", p=P)).then_inc(s_wout, 16)
                sp.dma_start(wr[:], I["w_router"][l].rearrange("(c p) n -> p c n", p=P)).then_inc(s_wr, 16)

                wg = I["w_gate"][l].rearrange("e (c p) f -> e p c f", p=P)
                wu = I["w_up"][l].rearrange("e (c p) f -> e p c f", p=P)
                wd = I["w_down"][l].rearrange("e (c p) n -> e p c n", p=P)

                def load_unit(e, part, slot):
                    if part < 4:
                        src = (wg, wu)[part % 2][e, :, :, 512 * (part // 2):512 * (part // 2) + 512]
                        dst = unit[slot].rearrange("p (c n) -> p c n", n=512)
                    else:
                        src = wd[e, :, 4 * (part - 4):4 * (part - 4) + 4, :]
                        dst = unit[slot].rearrange("p (c n) -> p c n", n=D)
                    sp.dma_start(dst, src).then_inc(s_w[slot], 16)

                sp.wait_ge(s_pv, LAYER_VALUES[l][-1] + 1)
                for n in range(4):
                    load_unit(0, n, (n + 5) % RING)
                sp.wait_ge(s_om, rows[-1] + 1)
                for n in range(4, 8):
                    load_unit(n // 6, n % 6, (n + 5) % RING)
                for n in rows:
                    t = ROW_TILES[n][1] - first_tile(l)
                    sp.wait_ge(s_fxn, n + 1)
                    sp.dma_start(xn_dram[l][P * t:P * t + P, :], fxn[n % 2]).then_inc(s_fst[n % 2], 16)
                for n in range(8, 96):
                    sp.wait_ge(s_wf, 96 * l + n - 7)
                    load_unit(n // 6, n % 6, (n + 5) % RING)
                if l + 1 < DEPTH:
                    sp.wait_ge(s_wf, 96 * (l + 1))
                    for g in range(5):
                        sp.dma_start(win[:, :, 512 * g:512 * g + 512],
                                     I["w_in"][l + 1].rearrange("(c p) n -> p c n", p=P)[:, :, 512 * g:512 * g + 512]
                                     ).then_inc(s_win[g], 16)
                sp.wait_ge(s_sct, 16 * NE * (l + 1))
                for n in rows:
                    t = ROW_TILES[n][1] - first_tile(l)
                    if n >= 2:
                        sp.wait_ge(s_yu, n - 1)
                    sp.dma_start(yrow[n % 2], y_dram[l][P * t:P * t + P, :]).then_inc(s_yl[n % 2], 16)
            for j, n in enumerate(LAYER_ROWS[DEPTH - 1]):
                sp.wait_ge(s_yu, n + 1)
                sp.dma_start(out[0, P * j:P * j + P, :], X[:, NC + j, :]).then_inc(s_out, 16)
            sp.wait_ge(s_out, 16 * (NT - NC))

        @block.gpsimd
        def _(pool):
            chain = [0]

            def link(ins):
                chain[0] += 1
                ins.then_inc(s_pch, 1)
                pool.wait_ge(s_pch, chain[0])

            link(pool.memset(ident[:], 0.0))
            link(pool.memset(ones[:], 1.0))
            link(pool.memset(halfneg[:], -0.5))
            pool.affine_select(out=ident[:], in_=ident[:], compare_op=ALU.not_equal, fill=1.0, base=0,
                               pattern=[[-1, P]], channel_multiplier=1).then_inc(s_const, 1)
            link(pool.memset(zero, 0.0))
            link(pool.memset(colmask[:], 0.0))
            for half in range(2):
                m = colmask[64 * half:64 * half + 64, :]
                link(pool.affine_select(out=m[:, 0:48], in_=m[:, 0:48], compare_op=ALU.is_ge, fill=NEG * INV_SCALE,
                                        base=8, pattern=[[1, 48]], channel_multiplier=-1))
                link(pool.affine_select(out=m[:, 16:64], in_=m[:, 16:64], compare_op=ALU.is_ge, fill=NEG * INV_SCALE,
                                        base=7 - 16, pattern=[[-1, 48]], channel_multiplier=1))
            link(pool.memset(bandL[:], 0.0))
            link(pool.memset(bandR[:], 0.0))
            link(pool.memset(idxT[:], 0))
            link(pool.affine_select(out=bandL[:], in_=bandL[:], compare_op=ALU.is_ge, fill=NEG, base=0,
                                    pattern=[[1, P]], channel_multiplier=-1))
            pool.affine_select(out=bandR[:], in_=bandR[:], compare_op=ALU.is_ge, fill=NEG, base=0,
                               pattern=[[-1, P]], channel_multiplier=1).then_inc(s_const, 1)

            def inverse_root(dst, src, width, n_el, wait, done, value):
                pool.wait_ge(wait, value)
                link(pool.tensor_scalar(dst, src, 1.0 / width, EPS, ALU.mult, ALU.add))
                pool.tensor_tensor(dst, dst, halfneg[:, 0:n_el], ALU.pow).then_inc(done, 1)

            for l in range(DEPTH):
                rows = LAYER_ROWS[l]
                if l > 0:
                    pool.wait_ge(s_yu, LAYER_ROWS[l - 1][-1] + 1)
                pool.memset(rp, 0.0).then_inc(s_rpz, 1)
                inverse_root(st[:, 1:2], st[:, 0:1], D, 1, s_ss, s_rs, NT * l + 1)
                for t in range(NT):
                    n = NT * l + t
                    inverse_root(st[:, 8:14], st[:, 2:8], HD, 6, s_hss, s_hrs, n + 1)
                    if t + 1 < NT:
                        pool.wait_ge(s_xn, n + 1)
                        inverse_root(st[:, 1:2], st[:, 0:1], D, 1, s_ss, s_rs, n + 2)
                inverse_root(st[:, 20:24], st[:, 16:20], HD, 4, s_bss, s_brs, rows[0] + 1)
                for n in rows:
                    if n < rows[-1]:
                        pool.wait_ge(s_on, n + 1)
                        inverse_root(st[:, 20:24], st[:, 16:20], HD, 4, s_bss, s_brs, n + 2)
                    if n > 0:
                        pool.wait_ge(s_xu, n)
                    inverse_root(st[:, 25:26], st[:, 24:25], D, 1, s_oss, s_ors, n + 1)
                for n in rows:
                    if n > 0:
                        pool.wait_ge(s_fxn, n)
                    inverse_root(st[:, 27:28], st[:, 26:27], D, 1, s_fss, s_frs, n + 1)
                M = 96 if l < DEPTH - 1 else CAP_X
                pool.wait_ge(s_tc, 2 * (l + 1))
                pool.wait_ge(s_fst[0], 16 * (rows[-1] // 2 + 1))
                pool.wait_ge(s_fst[1], 16 * ((rows[-1] + 1) // 2))

                def gather(e):
                    E = NE * l + e
                    pool.tensor_copy(idc[0:M, e % 4:e % 4 + 1], idxT[0:M, e:e + 1]).then_inc(s_idc, 1)
                    pool.wait_ge(s_idc, E + 1)
                    if e >= 2:
                        pool.wait_ge(s_et, 2 * (E - 1))
                    pool.indirect_dma_start(out=xe[e % 2][0:M], out_offset=None, in_=xn_dram[l],
                                            in_offset=bass.IndirectOffsetOnAxis(idc[0:M, e % 4:e % 4 + 1], 0)
                                            ).then_inc(s_g[e % 2], 16)

                gather(0)
                for e in range(NE):
                    E = NE * l + e
                    if e + 1 < NE:
                        gather(e + 1)
                    pool.wait_ge(s_yc, E + 1)
                    if e:
                        pool.wait_ge(s_sct, 16 * E)
                    elif l == 0:
                        pool.wait_ge(s_z, 16 * N_CLEAR)
                    pool.indirect_dma_start(out=y_dram[l],
                                            out_offset=bass.IndirectOffsetOnAxis(idc[0:M, e % 4:e % 4 + 1], 0),
                                            in_=ysc[e % 2][0:M], in_offset=None, compute_op=ALU.add).then_inc(s_sct, 16)
                for n in rows:
                    if n > 0:
                        pool.wait_ge(s_yu, n)
                    inverse_root(st[:, 29:30], st[:, 28:29], D, 1, s_yss, s_yrs, n + 1)

        @block.tensor
        def _(pe):
            pe.wait_ge(s_const, 1)
            pe.wait_ge(s_cs, 1)
            for c in range(KC):
                mm = pe.transpose(pb(0)[:, 2 * c:2 * c + 2], crow2[:, P * c:P * c + P], ident[0:2, 0:2])
            mm.then_inc(s_csT, 1)
            for c in range(KC):
                mm = pe.transpose(pb(1)[:, 8 * c:8 * c + 8], grow[:, P * c:P * c + P], ident[0:8, 0:8])
            mm.then_inc(s_csT, 1)
            pe.wait_ge(s_cs, 2)

            def turn_piece(n):
                l, q = n // 12, n % 12
                pe.wait_ge(s_adar, n + 1)
                for j in range(4):
                    mm = pe.transpose(pb(4 + l)[:, 2 * (4 * q + j):2 * (4 * q + j) + 2],
                                      ada_row[n % 4][:, P * j:P * j + P], ident[0:2, 0:2])
                mm.then_inc(s_adat, 1)

            for n in range(24):
                pe.wait_ge(s_adaw[n % 3], 16 * (n // 3 + 1))
                if n >= 2:
                    pe.wait_ge(s_adar, n - 1)
                for c in range(KC):
                    mm = pe.matmul(pb(2 + n % 2)[0:2, :], cT[:, c, :], ada_ring[n % 3][:, c, :],
                                   start=(c == 0), stop=(c == KC - 1))
                mm.then_inc(s_adam, 1)
                if n:
                    turn_piece(n - 1)
            turn_piece(23)
            pe.wait_ge(s_mod, 1)

            gate_no = [0]

            def gate_rows():
                q = gate_no[0]
                pe.wait_ge(s_gd, q + 1)
                for h in range(2):
                    mm = pe.matmul(pb(6 + h), ones[:], diag[:, 4 * h:4 * h + 4, :].rearrange("p c n -> p (c n)"),
                                   start=True, stop=True)
                mm.then_inc(s_gm, 1)
                gate_no[0] += 1

            for l in range(DEPTH):
                def turn_rows(n):
                    pe.wait_ge(s_xn, n + 1)
                    if n:
                        pe.wait_ge(s_ht, n)
                    for c in range(KC):
                        mm = pe.transpose(pb(c // 4)[:, P * (c % 4):P * (c % 4) + P], xn[:, P * c:P * c + P], ident[:])
                    mm.then_inc(s_xt, 1)

                def turn_qk(n, only_kv):
                    pe.wait_ge(s_qk, n + 1)
                    if n:
                        pe.wait_ge(s_qkc, n)
                    for b in range(8 if only_kv else 0, 14):
                        o = b if b < 8 else b
                        mm = pe.transpose(pb(4 + o // 4)[:, P * (o % 4):P * (o % 4) + P], qk[:, P * b:P * b + P], ident[:])
                    mm.then_inc(s_qkt, 1)

                def only_kv(t):
                    return l == DEPTH - 1 and t < NC

                turn_rows(NT * l)
                for t in range(NT):
                    n = NT * l + t
                    pe.wait_ge(s_ht, n + 1)
                    for g in range(5):
                        G = 5 * n + g
                        lo, hi = KV_SPAN[g] if only_kv(t) else (0, 512)
                        if t == 0:
                            pe.wait_ge(s_win[g], 16 * (l + 1))
                        if G >= 2:
                            pe.wait_ge(s_raw, G - 1)
                        for c in range(KC):
                            mm = pe.matmul(pb(2 + G % 2)[:, lo:hi], hT[n % 2][:, c, :],
                                           win[:, c, 512 * g + lo:512 * g + hi], start=(c == 0), stop=(c == KC - 1))
                        mm.then_inc(s_prj, 1)
                        if g == 0 and t:
                            turn_qk(n - 1, only_kv(t - 1))
                        if g == 2 and t + 1 < NT:
                            turn_rows(n + 1)
                turn_qk(NT * l + NT - 1, False)
                pe.wait_ge(s_qkc, NT * (l + 1))
                pe.wait_ge(s_raw, 5 * NT * (l + 1))
                for step in STEPS[l]:
                    u = step["score"]
                    if u:
                        k = u["k"]
                        if k >= 2:
                            pe.wait_ge(s_ex, k - 1)
                        r0 = HD * u["half"] + (32 * u["c"] if u["mixer"] == "B" else 0)
                        r1 = r0 + (32 if u["mixer"] == "B" else HD)
                        for col, src, width in u["segs"]:
                            mm = pe.matmul(pb(2 * (k % 2), 2)[:, col:col + width],
                                           qT[r0:r1, u["qp"], P * u["t"]:P * u["t"] + P],
                                           kT[r0:r1, u["kp"], src:src + width], start=True, stop=True)
                        mm.then_inc(s_sc, 1)
                    for v in step["turn"]:
                        m, k = v["m"], v["k"]
                        if v["mixer"] == "B":
                            pe.wait_ge(s_cb, v["diffs"])
                        else:
                            pe.wait_ge(s_ex, k + 1)
                        if m:
                            pe.wait_ge(s_ta, m)
                            pe.wait_ge(s_tb, v["wide"] - (v["nk"] > 512))
                        src = Pb[(k - 1) % 4] if v["mixer"] == "B" else Pb[k % 4]
                        for j in range(v["nk"] // P):
                            mm = pe.transpose(pb(4 + j // 4)[:, P * (j % 4):P * (j % 4) + P], src[:, P * j:P * j + P], ident[:])
                        mm.then_inc(s_tn, 1)
                    for v in step["pv"]:
                        m = v["m"]
                        pe.wait_ge(s_ta, m + 1)
                        pe.wait_ge(s_tb, v["wide"])
                        if m >= 2:
                            pe.wait_ge(s_o, m - 1)
                        for j, vt in enumerate(v["vt"]):
                            mm = pe.matmul(pb(6 + m % 2)[:, 0:HD], PT[m % 2][:, P * j:P * j + P],
                                           V[:, vt, v["vcol"]:v["vcol"] + HD], start=(j == 0), stop=(j == len(v["vt"]) - 1))
                        mm.then_inc(s_pv, 1)
                rows = LAYER_ROWS[l]
                pe.wait_ge(s_o, LAYER_VALUES[l][-1] + 1)
                for _ in range(2):
                    gate_rows()
                    pe.wait_ge(s_gb, gate_no[0])

                def turn_out(n):
                    t = ROW_TILES[n][1]
                    pe.wait_ge(s_on, n + 1)
                    if n:
                        pe.wait_ge(s_oc, n)
                    for c in range(KC):
                        mm = pe.transpose(pb(c // 4)[:, P * (c % 4):P * (c % 4) + P], Ost[:, t, P * c:P * c + P], ident[:])
                    mm.then_inc(s_ot, 1)

                pe.wait_ge(s_wout, 16 * (l + 1))
                turn_out(rows[0])
                for n in rows:
                    if n < rows[-1]:
                        turn_out(n + 1)
                    pe.wait_ge(s_oc, n + 1)
                    if n >= 2:
                        pe.wait_ge(s_xu, n - 1)
                    for h in range(2):
                        for c in range(KC):
                            mm = pe.matmul(pb(2 + 2 * (n % 2) + h), OT[n % 2][:, c, :], wout[:, c, 512 * h:512 * h + 512],
                                           start=(c == 0), stop=(c == KC - 1))
                    mm.then_inc(s_om, 1)
                def turn_f(n):
                    pe.wait_ge(s_fxn, n + 1)
                    if n >= 2:
                        pe.wait_ge(s_fh, n - 1)
                        pe.wait_ge(s_fv, n - 1)
                    for c in range(KC):
                        mm = pe.transpose(pb(2 * (n % 2) + c // 4)[:, P * (c % 4):P * (c % 4) + P],
                                          fxn[n % 2][:, P * c:P * c + P], ident[:])
                    mm.then_inc(s_ft, 1)

                def turn_aff(n):
                    pe.wait_ge(s_lp, n + 1)
                    if n >= 2:
                        pe.wait_ge(s_lc, n - 1)
                    pe.transpose(pb(6 + n % 2)[0:NE, 0:P], lg[:, n % 2, :], ident[:]).then_inc(s_lt, 1)

                pe.wait_ge(s_xu, rows[-1] + 1)
                pe.wait_ge(s_wr, 16 * (l + 1))
                turn_f(rows[0])
                for n in rows:
                    if n < rows[-1]:
                        turn_f(n + 1)
                    pe.wait_ge(s_fh, n + 1)
                    pe.wait_ge(s_fv, n + 1)
                    if n >= 2:
                        pe.wait_ge(s_le, n - 1)
                    for c in range(KC):
                        mm = pe.matmul(pb(4 + n % 2)[:, 0:NE], fhT[n % 2][:, c, :], wr[:, c, :],
                                       start=(c == 0), stop=(c == KC - 1))
                    mm.then_inc(s_lg, 1)
                    if n > rows[0]:
                        turn_aff(n - 1)
                turn_aff(rows[-1])
                M = 96 if l < DEPTH - 1 else CAP_X
                pe.wait_ge(s_top, l + 1)
                pe.transpose(pb(4)[0:M, 0:NE], vals[:, 0:M], ident[0:NE, 0:NE])
                pe.transpose(pb(5)[0:M, 0:NE], idxf[:, 0:M], ident[0:NE, 0:NE]).then_inc(s_tt, 1)
                pe.wait_ge(s_tc, 2 * (l + 1))

                def turn_xe(e):
                    E = NE * l + e
                    pe.wait_ge(s_g[e % 2], 16 * (E // 2 + 1))
                    for half in range(2):
                        free = 2 * E if e == 0 else 2 * E - 3 + half
                        if free > 0:
                            pe.wait_ge(s_hsc, free)
                        for c in range(4 * half, 4 * half + 4):
                            mm = pe.transpose(pb(6 + half)[:, P * (c % 4):P * (c % 4) + M], xe[e % 2][0:M, P * c:P * c + P],
                                              ident[0:M, 0:M])
                        mm.then_inc(s_et, 1)

                def weights(e, part):
                    n = 6 * e + part
                    pe.wait_ge(s_w[(n + 5) % RING], 16 * (12 * l + n // RING + 1))
                    return unit[(n + 5) % RING]

                def gate_up(e, half, part):
                    w = weights(e, 2 * half + part).rearrange("p (c n) -> p c n", n=512)
                    E = NE * l + e
                    if E:
                        pe.wait_ge(s_hs, 2 * (E - 1) + half + 1)
                    for c in range(KC):
                        mm = pe.matmul(pb(2 * half + part)[0:M, :], xeT[e % 2][:, c, 0:M], w[:, c, :],
                                       start=(c == 0), stop=(c == KC - 1))
                    mm.then_inc(s_wf, 1)

                def turn_hs(e, half):
                    E = NE * l + e
                    pe.wait_ge(s_hs, 2 * E + half + 1)
                    if e + 1 < NE:
                        pe.wait_ge(s_ec, 2 * (E + 1) + half + 1)
                    for c in range(4 * half, 4 * half + 4):
                        mm = pe.transpose(pb(6 + half)[:, P * (c % 4):P * (c % 4) + M], hs[0:M, P * c:P * c + P],
                                          ident[0:M, 0:M])
                    mm.then_inc(s_hst, 1)

                def down(e, half):
                    E = NE * l + e
                    w = weights(e, 4 + half).rearrange("p (c n) -> p c n", n=D)
                    pe.wait_ge(s_hsc, 2 * E + half + 1)
                    if half == 0 and E:
                        pe.wait_ge(s_yc, E)
                    for c in range(4):
                        for h in range(2):
                            mm = pe.matmul(pb(4 + h)[0:M, :], hsT[:, 4 * half + c, 0:M], w[:, c, 512 * h:512 * h + 512],
                                           start=(half == 0 and c == 0), stop=(half == 1 and c == 3))
                    mm.then_inc(s_wf, 1)

                turn_xe(0)
                for e in range(NE):
                    pe.wait_ge(s_ec, 2 * (NE * l + e + 1))
                    gate_up(e, 0, 0)
                    gate_up(e, 0, 1)
                    if e + 1 < NE:
                        turn_xe(e + 1)
                    gate_up(e, 1, 0)
                    turn_hs(e, 0)
                    gate_up(e, 1, 1)
                    down(e, 0)
                    turn_hs(e, 1)
                    down(e, 1)
                pe.wait_ge(s_hsc, 2 * NE * (l + 1))
                for _ in range(2):
                    gate_rows()
                    pe.wait_ge(s_gb, gate_no[0])

        @block.scalar
        def _(act):
            act.wait_ge(s_in, 16 * n_small[0])
            act.activation(crow2, crow, ACT.Exp, scale=-1.0).then_inc(s_ach, 1)
            gate_no = [0]

            def gate_rows():
                q = gate_no[0]
                act.wait_ge(s_gm, q + 1)
                act.activation(GB[:, q % 2, :], pb(6, 2), ACT.Copy).then_inc(s_gb, 1)
                gate_no[0] += 1

            act.wait_ge(s_mod, 1)
            act.wait_ge(s_vlam, 1)
            act.activation(lams[:], lams[:], ACT.Exp).then_inc(s_ach, 1)
            for l in range(DEPTH):
                rows = LAYER_ROWS[l]
                def square_rows(n):
                    t = n - NT * l
                    if n:
                        act.wait_ge(s_rs, n)
                        act.wait_ge(s_xt, n)
                    act.activation(xn, X[:, t, :], ACT.Square, accum_out=st[:, 0:1]).then_inc(s_ss, 1)

                def modulate(n):
                    t = n - NT * l
                    act.wait_ge(s_xt, n + 1)
                    for c in range(KC):
                        ins = act.activation(hT[n % 2][:, c, :], pb(c // 4)[:, P * (c % 4):P * (c % 4) + P], ACT.Identity,
                                             scale=mscale[:, l, 0, kind(t), c:c + 1], bias=modcol[:, l, c, kind(t):kind(t) + 1])
                    ins.then_inc(s_ht, 1)

                if l == 0:
                    act.wait_ge(s_x, 32)
                else:
                    act.wait_ge(s_yu, LAYER_ROWS[l - 1][-1] + 1)
                square_rows(NT * l)
                modulate(NT * l)
                for t in range(NT):
                    n = NT * l + t
                    only_kv = l == DEPTH - 1 and t < NC
                    for g in range(5):
                        G = 5 * n + g
                        act.wait_ge(s_prj, G + 1)
                        if RAW_READ[G - 2] if G >= 2 else 0:
                            act.wait_ge(s_rawf, RAW_READ[G - 2])
                        for what, col, width, dst in GROUPS[g]:
                            if only_kv and what[0] == "q":
                                continue
                            src = pb(2 + G % 2)[:, col:col + width]
                            if what == "v":
                                ins = act.activation(V[:, t, dst:dst + width], src, ACT.Copy)
                            else:
                                ins = act.activation(raw[G % 2][:, col:col + width], src, ACT.Copy)
                        ins.then_inc(s_raw, 1)
                        if g == 1 and t + 1 < NT:
                            square_rows(n + 1)
                        if g == 2 and t + 1 < NT:
                            modulate(n + 1)
                for step in STEPS[l]:
                    u = step["score"]
                    if u:
                        k = u["k"]
                        act.wait_ge(s_mx, k + 1)
                        last = P_LAST[k]
                        if last:
                            act.wait_ge(s_tn, last)
                        act.activation(Pb[k % 4][:, 0:u["nk"]], pb(2 * (k % 2), 2)[:, 0:u["nk"]], ACT.Exp,
                                       bias=nmx[:, k % 8:k % 8 + 1], scale=SCALE_B if u["mixer"] == "B" else SCALE,
                                       accum_out=sumx[:, k % 8:k % 8 + 1]).then_inc(s_ex, 1)
                        if u["mixer"] == "C":
                            act.activation(skx[:, k % 8:k % 8 + 1], sink8[:, l, u["h"]:u["h"] + 1], ACT.Exp,
                                           bias=nmx[:, k % 8:k % 8 + 1], scale=SCALE).then_inc(s_sk, 1)
                    for v in step["turn"]:
                        m = v["m"]
                        act.wait_ge(s_tn, m + 1)
                        if m >= 2:
                            act.wait_ge(s_pv, m - 1)
                        w = min(v["nk"], 512)
                        act.activation(PT[m % 2][:, 0:w], pb(4)[:, 0:w], ACT.Copy).then_inc(s_ta, 1)
                for _ in range(2):
                    gate_rows()

                def store_out(n):
                    act.wait_ge(s_ot, n + 1)
                    if n >= 2:
                        act.wait_ge(s_om, n - 1)
                    act.activation(OT[n % 2].rearrange("p c n -> p (c n)"), pb(0, 2), ACT.Copy).then_inc(s_oc, 1)

                store_out(rows[0])
                for n in rows:
                    if n < rows[-1]:
                        store_out(n + 1)
                    act.wait_ge(s_om, n + 1)
                    if n:
                        act.wait_ge(s_ors, n)
                    act.activation(junk, pb(2 + 2 * (n % 2), 2), ACT.Square, accum_out=st[:, 24:25]).then_inc(s_oss, 1)
                def square_f(n):
                    act.wait_ge(s_xu, rows[-1] + 1)
                    if n:
                        act.wait_ge(s_frs, n)
                    act.activation(junk, X[:, ROW_TILES[n][1], :], ACT.Square, accum_out=st[:, 26:27]).then_inc(s_fss, 1)

                square_f(rows[0])
                for n in rows:
                    t = ROW_TILES[n][1]
                    if n < rows[-1]:
                        square_f(n + 1)
                    act.wait_ge(s_ft, n + 1)
                    if n >= 2:
                        act.wait_ge(s_lg, n - 1)
                    for c in range(4):
                        ins = act.activation(fhT[n % 2][:, c, :], pb(2 * (n % 2))[:, P * c:P * c + P], ACT.Identity,
                                             scale=mscale[:, l, 1, kind(t), c:c + 1],
                                             bias=modcol[:, l, 24 + c, kind(t):kind(t) + 1])
                    ins.then_inc(s_fh, 1)
                    act.wait_ge(s_lm, n + 1)
                    if n >= 2:
                        act.wait_ge(s_lt, n - 1)
                    act.activation(lg[:, n % 2, :], pb(4 + n % 2)[:, 0:NE], ACT.Exp, bias=st[:, 32 + n % 2:33 + n % 2],
                                   accum_out=st[:, 34 + n % 2:35 + n % 2]).then_inc(s_le, 1)
                M = 96 if l < DEPTH - 1 else CAP_X

                def modulate_xe(e):
                    E = NE * l + e
                    for half in range(2):
                        act.wait_ge(s_et, 2 * E + half + 1)
                        for c in range(4 * half, 4 * half + 4):
                            for kd, a, b in ((1, 0, CAP_X), (0, CAP_X, M)):
                                if a < b:
                                    ins = act.activation(xeT[e % 2][:, c, a:b],
                                                         pb(6 + half)[:, P * (c % 4) + a:P * (c % 4) + b], ACT.Identity,
                                                         scale=mscale[:, l, 1, kd, c:c + 1],
                                                         bias=modcol[:, l, 24 + c, kd:kd + 1])
                        ins.then_inc(s_ec, 1)

                def exp_gate(e, half):
                    E = NE * l + e
                    act.wait_ge(s_wf, 6 * E + 2 * half + 2)
                    if E:
                        act.wait_ge(s_hs, 2 * (E - 1) + half + 1)
                    act.activation(sg[0:M, half, :], pb(2 * half)[0:M, :], ACT.Exp, scale=-1.0).then_inc(s_eg, 1)

                modulate_xe(0)
                act.wait_ge(s_tc, 2 * (l + 1))
                for e in range(NE):
                    E = NE * l + e
                    exp_gate(e, 0)
                    if e + 1 < NE:
                        modulate_xe(e + 1)
                    exp_gate(e, 1)
                    act.wait_ge(s_wf, 6 * E + 6)
                    if e >= 2:
                        act.wait_ge(s_sct, 16 * (E - 1))
                    for h in range(2):
                        ins = act.activation(ysc[e % 2][0:M, 512 * h:512 * h + 512], pb(4 + h)[0:M, :], ACT.Copy,
                                             scale=gT[0:M, e:e + 1])
                    ins.then_inc(s_yc, 1)
                for _ in range(2):
                    gate_rows()
                for n in rows:
                    if n:
                        act.wait_ge(s_yrs, n)
                    act.wait_ge(s_yl[n % 2], 16 * (n // 2 + 1))
                    act.activation(junk, yrow[n % 2], ACT.Square, accum_out=st[:, 28:29]).then_inc(s_yss, 1)

        @block.vector
        def _(dve):
            chain = [0]

            def link(ins):
                chain[0] += 1
                ins.then_inc(s_vch, 1)
                dve.wait_ge(s_vch, chain[0])

            dve.wait_ge(s_ach, 1)
            link(dve.tensor_scalar(crow2, crow2, 1.0, None, ALU.add))
            link(dve.reciprocal(crow2, crow2))
            dve.tensor_tensor(crow2, crow2, crow, ALU.mult).then_inc(s_cs, 1)
            dve.wait_ge(s_csT, 1)
            dve.tensor_copy(cT[:].rearrange("p c k -> p (c k)"), pb(0)[:, 0:2 * KC]).then_inc(s_cs, 1)
            dve.wait_ge(s_csT, 2)
            dve.tensor_copy(gcol[:].rearrange("p c k -> p (c k)"), pb(1)[:, 0:8 * KC]).then_inc(s_cs, 1)
            for n in range(24):
                dve.wait_ge(s_adam, n + 1)
                dve.wait_ge(s_adab[n % 4], 16 * (n // 4 + 1))
                dve.tensor_tensor(ada_row[n % 4], ada_row[n % 4], pb(2 + n % 2)[0:2, :], ALU.add).then_inc(s_adar, 1)
            dve.wait_ge(s_adat, 24)
            dve.wait_ge(s_cs, 3)
            for l in range(DEPTH):
                link(dve.tensor_copy(modcol[:, l].rearrange("p f k -> p (f k)"), pb(4 + l)[:, 0:96]))
                for s in range(2):
                    for k in range(2):
                        dve.scalar_tensor_tensor(mscale[:, l, s, k, :], modcol[:, l, 24 * s + 8:24 * s + 16, k], 1.0,
                                                 gcol[:, :, 4 * s + l], ALU.add, ALU.mult)
                        ins = dve.tensor_tensor(gate[:, l, s, k, :], modcol[:, l, 24 * s + 16:24 * s + 24, k],
                                                gcol[:, :, 4 * s + 2 + l], ALU.mult)
            ins.then_inc(s_mod, 1)
            dve.wait_ge(s_in2, 16 * (1 + 6 * DEPTH + 2))
            link(dve.tensor_scalar(nsink8[:], sink8[:], -INV_SCALE, None, ALU.mult))
            link(dve.tensor_scalar(sink8[:], sink8[:], INV_SCALE, None, ALU.mult))
            for l in range(DEPTH):
                link(dve.tensor_scalar(subgain[:, l, :], subgain[:, l, :], 1.0 - lam_init(l), None, ALU.mult))
                link(dve.tensor_tensor(lamp[:, l], lamv[:, l, 0:2, :], lamv[:, l, 2:4, :], ALU.mult))
            dve.tensor_reduce(lams[:].rearrange("p l j -> p (l j)"), lamp[:].rearrange("p l j d -> p (l j) d"), AX_X,
                              ALU.add).then_inc(s_vlam, 1)
            dve.wait_ge(s_ach, 2)
            for l in range(DEPTH):
                link(dve.tensor_tensor(nlam[:, l:l + 1], lams[:, l, 1:2], lams[:, l, 0:1], ALU.subtract))
                link(dve.tensor_scalar(nlam[:, l:l + 1], nlam[:, l:l + 1], lam_init(l), None, ALU.subtract))
            dve.wait_ge(s_const, 2)
            dve.wait_ge(s_z, 16 * N_CLEAR)

            gate_no = [0]

            def gate_rows(l, s, k):
                q = gate_no[0]
                if q:
                    dve.wait_ge(s_gm, q)
                for c in range(KC):
                    ins = dve.tensor_scalar(diag[:, c, :], ident[:], gate[:, l, s, k, c:c + 1], None, ALU.mult)
                ins.then_inc(s_gd, 1)
                gate_no[0] += 1

            for l in range(DEPTH):
                rows = LAYER_ROWS[l]
                def normalise(n):
                    t = n - NT * l
                    dve.wait_ge(s_rs, n + 1)
                    if n:
                        dve.wait_ge(s_xt, n)
                    dve.tensor_scalar(xn, X[:, t, :], st[:, 1:2], None, ALU.mult).then_inc(s_xn, 1)

                def rotate(dst, src, t, heads, dim):
                    if t < NC:
                        link(dve.tensor_copy(dst, src))
                        return
                    off = 0 if dim == HD else 128
                    table = rope[:, t - NC, off:off + 2 * dim]
                    cos = table[:, 0:dim].unsqueeze(1).broadcast_to([P, heads, dim])
                    sin = table[:, dim:2 * dim].rearrange("p (j e) -> p e j", e=2)
                    w = heads * dim
                    a = tmp[1][:, 0:w].rearrange("p (h d) -> p h d", d=dim)
                    b = tmp[2][:, 0:w].rearrange("p (h d) -> p h d", d=dim)
                    s3 = src if len(src.shape) == 3 else src.rearrange("p (h d) -> p h d", d=dim)
                    dve.tensor_tensor(a, s3, cos, ALU.mult)
                    for e in range(2):
                        o = b.rearrange("p h (j e) -> p e h j", e=2)[:, e]
                        i = s3.rearrange("p h (j e) -> p e h j", e=2)[:, 1 - e]
                        ins = dve.tensor_tensor(o, i, sin[:, e].unsqueeze(1).broadcast_to([P, heads, dim // 2]), ALU.mult)
                    link(ins)
                    return a, b

                def place(what, col, width, dst, n, t, src):
                    dim = HD // 2 if what[1] == "b" else HD
                    out = qk[:, dst:dst + width]
                    swap = what in ("qa", "qc")
                    def order(v):
                        return v.rearrange("p (a b d) -> p a b d", a=2, b=2)
                    if swap:
                        out = out.rearrange("p (b a d) -> p a b d", b=2, a=2)
                    if what[1] == "d" or t < NC:
                        return dve.tensor_copy(out, order(src) if swap else src)
                    rotate(None, src, t, width // dim, dim)
                    a, b = tmp[1][:, 0:width], tmp[2][:, 0:width]
                    if swap:
                        a, b = order(a), order(b)
                    return dve.tensor_tensor(out, a, b, ALU.add)

                def store_qk(n, only_kv):
                    t = n - NT * l
                    dve.wait_ge(s_qkt, n + 1)
                    if not only_kv:
                        dve.tensor_copy(qT[:, :, P * t:P * t + P], pb(4, 2).rearrange("p (b n) -> p b n", n=P))
                    dve.tensor_copy(kT[:, :, P * t:P * t + P], pb(6, 2)[:, 0:768].rearrange("p (b n) -> p b n", n=P)
                                    ).then_inc(s_qkc, 1)

                normalise(NT * l)
                for t in range(NT):
                    n = NT * l + t
                    only_kv = l == DEPTH - 1 and t < NC
                    for g in range(5):
                        G = 5 * n + g
                        if g == 0 and t:
                            store_qk(n - 1, l == DEPTH - 1 and t - 1 < NC)
                        if g == 2 and t + 1 < NT:
                            normalise(n + 1)
                        work = [x for x in GROUPS[g] if x[0] != "v" and not (only_kv and x[0][0] == "q")]
                        if not work:
                            continue
                        dve.wait_ge(s_raw, G + 1)
                        r = raw[G % 2]
                        if g == 0:
                            lo = 256 if only_kv else 0
                            heads = slice(lo // HD, 6)
                            nh = 6 - lo // HD
                            r3 = r[:, lo:384].rearrange("p (h d) -> p h d", d=HD)
                            n3 = tmp[0][:, lo:384].rearrange("p (h d) -> p h d", d=HD)
                            if only_kv and n == NT * l:
                                link(dve.memset(st[:, 2:8], 1.0))
                            link(dve.tensor_tensor(n3, r3, r3, ALU.mult))
                            dve.tensor_reduce(st[:, 2 + heads.start:8], n3, AX_X, ALU.add).then_inc(s_hss, 1)
                            dve.wait_ge(s_hrs, n + 1)
                            link(dve.tensor_tensor(n3, r3, st[:, 8 + heads.start:14].unsqueeze(2).broadcast_to([P, nh, HD]),
                                                   ALU.mult))
                            for j, (a, b) in enumerate(((0, 256), (256, 384))):
                                if a >= lo:
                                    v3 = tmp[0][:, a:b].rearrange("p (h d) -> p h d", d=HD)
                                    link(dve.tensor_tensor(v3, v3, qkgain[:, l, j, :].unsqueeze(1).broadcast_to(
                                        [P, (b - a) // HD, HD]), ALU.mult))
                            r = tmp[0]
                        for j, (what, col, width, dst) in enumerate(work):
                            ins = place(what, col, width, dst, n, t, r[:, col:col + width])
                            if j < len(work) - 1:
                                link(ins)
                        if g < 4:
                            ins.then_inc(s_rawf, 1)
                            dve.wait_ge(s_rawf, RAW_READ[G])
                        else:
                            link(ins)
                            dve.tensor_copy(st[:, 40:41], st[:, 8:9]).then_inc(s_rawf, 1)
                            dve.tensor_copy(st[:, 41:42], st[:, 8:9]).then_inc(s_qk, 1)
                store_qk(NT * l + NT - 1, False)
                dve.wait_ge(s_rpl, 16 * 8 * (l + 1))
                bias = rpbT.rearrange("p h s c -> p (h s) c")
                mask = colmask[:].unsqueeze(1).broadcast_to([P, 56, GRID_W])
                link(dve.scalar_tensor_tensor(bias, bias, INV_SCALE, mask, ALU.mult, ALU.add))
                for step in STEPS[l]:
                    u = step["score"]
                    if u:
                        k, S = u["k"], pb(2 * (u["k"] % 2), 2)
                        dve.wait_ge(s_sc, k + 1)
                        if u["mixer"] == "C" and u["i"] >= 0:
                            if u["left"]:
                                link(dve.tensor_tensor(S[:, 256:384], S[:, 256:384], bandL[:], ALU.add))
                            if u["right"]:
                                e = u["nk"]
                                link(dve.tensor_tensor(S[:, e - P:e], S[:, e - P:e], bandR[:], ALU.add))
                        if u["mixer"] == "D" and u["i"] >= 0:
                            s0 = 6 - 2 * u["i"]
                            link(dve.tensor_tensor(S[:, 256:768], S[:, 256:768],
                                                   rpbT[:, u["h"], s0:s0 + 8, :].rearrange("p s c -> p (s c)"), ALU.add))
                        nm = nmx[:, k % 8:k % 8 + 1]
                        link(dve.tensor_reduce(nm, S[:, 0:u["nk"]], AX_X, ALU.max, negate=True))
                        if u["mixer"] == "C":
                            dve.tensor_scalar(nm, nm, nsink8[:, l, u["h"]:u["h"] + 1], SCALE, ALU.min, ALU.mult).then_inc(s_mx, 1)
                        else:
                            dve.tensor_scalar(nm, nm, SCALE_B if u["mixer"] == "B" else SCALE, None, ALU.mult).then_inc(s_mx, 1)
                    j = step["no"]
                    prev = STEPS[l][j - 1]["score"] if j else None
                    if prev and prev["mixer"] == "B" and prev["c"] == 1:
                        k = prev["k"]
                        dve.wait_ge(s_ex, k + 1)
                        a, b = (k - 1) % 8, k % 8
                        dve.reciprocal(rx[:, a:a + 1], sumx[:, a:a + 1])
                        link(dve.reciprocal(rx[:, b:b + 1], sumx[:, b:b + 1]))
                        link(dve.tensor_tensor(rx[:, b:b + 1], rx[:, b:b + 1], nlam[:, l:l + 1], ALU.mult))
                        p0, p1 = Pb[(k - 1) % 4][:, 0:prev["nk"]], Pb[k % 4][:, 0:prev["nk"]]
                        link(dve.tensor_scalar(p1, p1, rx[:, b:b + 1], None, ALU.mult))
                        dve.scalar_tensor_tensor(p0, p0, rx[:, a:a + 1], p1, ALU.mult, ALU.add).then_inc(s_cb, 1)
                    for v in step["turn"]:
                        if v["nk"] > 512:
                            m = v["m"]
                            dve.wait_ge(s_tn, m + 1)
                            if m >= 2:
                                dve.wait_ge(s_pv, m - 1)
                            dve.tensor_copy(PT[m % 2][:, 512:v["nk"]], pb(5)[:, 0:v["nk"] - 512]).then_inc(s_tb, 1)
                    for v in step["pv"]:
                        m, k = v["m"], v["k"]
                        dst = Ost[:, v["t"], v["ocol"]:v["ocol"] + HD]
                        if v["mixer"] == "B":
                            dve.wait_ge(s_pv, m + 1)
                            dve.tensor_copy(dst, pb(6 + m % 2)[:, 0:HD]).then_inc(s_o, 1)
                        else:
                            r = rx[:, k % 8:k % 8 + 1]
                            if v["mixer"] == "C":
                                dve.wait_ge(s_sk, SINKS[k])
                                link(dve.tensor_tensor(sumx[:, k % 8:k % 8 + 1], sumx[:, k % 8:k % 8 + 1],
                                                       skx[:, k % 8:k % 8 + 1], ALU.add))
                            link(dve.reciprocal(r, sumx[:, k % 8:k % 8 + 1]))
                            dve.wait_ge(s_pv, m + 1)
                            dve.tensor_scalar(dst, pb(6 + m % 2)[:, 0:HD], r, None, ALU.mult).then_inc(s_o, 1)
                dve.wait_ge(s_o, LAYER_VALUES[l][-1] + 1)
                dve.wait_ge(s_pv, LAYER_VALUES[l][-1] + 1)
                for k in range(2):
                    gate_rows(l, 0, k)

                def sub_norm(n):
                    t = ROW_TILES[n][1]
                    o = Ost[:, t, 256:512]
                    o3 = o.rearrange("p (h d) -> p h d", d=HD)
                    sq = upd[:, 0:256].rearrange("p (h d) -> p h d", d=HD)
                    if n >= 2:
                        dve.wait_ge(s_xu, n - 1)
                    link(dve.tensor_tensor(sq, o3, o3, ALU.mult))
                    dve.tensor_reduce(st[:, 16:20], sq, AX_X, ALU.add).then_inc(s_bss, 1)
                    dve.wait_ge(s_brs, n + 1)
                    link(dve.tensor_tensor(o3, o3, st[:, 20:24].unsqueeze(2).broadcast_to([P, 4, HD]), ALU.mult))
                    dve.tensor_tensor(o3, o3, subgain[:, l, :].unsqueeze(1).broadcast_to([P, 4, HD]), ALU.mult
                                      ).then_inc(s_on, 1)

                sub_norm(rows[0])
                dve.wait_ge(s_gb, gate_no[0])
                for n in rows:
                    t = ROW_TILES[n][1]
                    if n < rows[-1]:
                        sub_norm(n + 1)
                    dve.wait_ge(s_ors, n + 1)
                    link(dve.scalar_tensor_tensor(upd, pb(2 + 2 * (n % 2), 2), st[:, 25:26], GB[:, kind(t), :],
                                                  ALU.mult, ALU.mult))
                    dve.tensor_tensor(X[:, t, :], X[:, t, :], upd, ALU.add).then_inc(s_xu, 1)
                dve.wait_ge(s_xu, rows[-1] + 1)

                def normalise_f(n):
                    dve.wait_ge(s_frs, n + 1)
                    if n >= 2:
                        dve.wait_ge(s_ft, n - 1)
                        dve.wait_ge(s_fst[n % 2], 16 * (n // 2))
                    dve.tensor_scalar(fxn[n % 2], X[:, ROW_TILES[n][1], :], st[:, 27:28], None, ALU.mult).then_inc(s_fxn, 1)

                def store_aff(n):
                    t = ROW_TILES[n][1]
                    dve.wait_ge(s_lt, n + 1)
                    dve.tensor_copy(affT[:, P * t:P * t + P], pb(6 + n % 2)[0:NE, 0:P]).then_inc(s_lc, 1)

                normalise_f(rows[0])
                for n in rows:
                    t = ROW_TILES[n][1]
                    if n < rows[-1]:
                        normalise_f(n + 1)
                    dve.wait_ge(s_ft, n + 1)
                    if n >= 2:
                        dve.wait_ge(s_lg, n - 1)
                    for c in range(4, 8):
                        ins = dve.tensor_scalar(fhT[n % 2][:, c, :], pb(2 * (n % 2) + 1)[:, P * (c - 4):P * (c - 4) + P],
                                                mscale[:, l, 1, kind(t), c:c + 1], modcol[:, l, 24 + c, kind(t):kind(t) + 1],
                                                ALU.mult, ALU.add)
                    ins.then_inc(s_fv, 1)
                    dve.wait_ge(s_lg, n + 1)
                    dve.tensor_reduce(st[:, 32 + n % 2:33 + n % 2], pb(4 + n % 2)[:, 0:NE], AX_X, ALU.max, negate=True
                                      ).then_inc(s_lm, 1)
                    dve.wait_ge(s_le, n + 1)
                    link(dve.reciprocal(st[:, 36 + n % 2:37 + n % 2], st[:, 34 + n % 2:35 + n % 2]))
                    dve.tensor_scalar(lg[:, n % 2, :], lg[:, n % 2, :], st[:, 36 + n % 2:37 + n % 2], None, ALU.mult
                                      ).then_inc(s_lp, 1)
                    if n > rows[0]:
                        store_aff(n - 1)
                store_aff(rows[-1])
                dve.wait_ge(s_lc, rows[-1] + 1)
                for lo, hi, cap, col in ((CTX, CTX + SEQ, CAP_X, 0), (0, CTX, CAP_C, CAP_X)):
                    if lo == 0 and l == DEPTH - 1:
                        continue
                    src = affT[:, lo:hi]
                    for r in range(col, col + cap, 8):
                        link(dve.max(vals[:, r:r + 8], src))
                        ins = dve.max_index(idxu[:, r:r + 8], vals[:, r:r + 8], src)
                        if r + 8 < col + cap:
                            rest = aff2[:, 0:hi - lo]
                            ins = dve.match_replace(rest, vals[:, r:r + 8], src, -1.0)
                            src = rest
                        link(ins)
                    ins = dve.tensor_scalar(idxf[:, col:col + cap], idxu[:, col:col + cap], float(lo - P * first_tile(l)), None, ALU.add)
                    if lo == 0 or l == DEPTH - 1:
                        ins.then_inc(s_top, 1)
                M = 96 if l < DEPTH - 1 else CAP_X
                dve.wait_ge(s_tt, l + 1)
                dve.tensor_copy(gT[0:M, :], pb(4)[0:M, 0:NE]).then_inc(s_tc, 1)
                dve.tensor_copy(idxT[0:M, 0:NE], pb(5)[0:M, 0:NE]).then_inc(s_tc, 1)
                for e in range(NE):
                    E = NE * l + e
                    for half in range(2):
                        dve.wait_ge(s_eg, 2 * E + half + 1)
                        g = sg[0:M, half, :]
                        link(dve.tensor_scalar(g, g, 1.0, None, ALU.add))
                        link(dve.reciprocal(g, g))
                        link(dve.tensor_tensor(g, g, pb(2 * half)[0:M, :], ALU.mult))
                        if E:
                            dve.wait_ge(s_hst, 2 * (E - 1) + half + 1)
                        dve.tensor_tensor(hs[0:M, 512 * half:512 * half + 512], g, pb(2 * half + 1)[0:M, :], ALU.mult
                                          ).then_inc(s_hs, 1)
                        dve.wait_ge(s_hst, 2 * E + half + 1)
                        if E:
                            dve.wait_ge(s_wf, 6 * E)
                        dve.tensor_copy(hsT[:, 4 * half:4 * half + 4, 0:M],
                                        pb(6 + half).rearrange("p (c n) -> p c n", n=P)[:, :, 0:M]).then_inc(s_hsc, 1)
                dve.wait_ge(s_sct, 16 * NE * (l + 1))
                for k in range(2):
                    gate_rows(l, 1, k)
                dve.wait_ge(s_gb, gate_no[0])
                for n in rows:
                    t = ROW_TILES[n][1]
                    dve.wait_ge(s_yrs, n + 1)
                    if n:
                        dve.wait_ge(s_yu, n)
                    link(dve.scalar_tensor_tensor(yupd, yrow[n % 2], st[:, 29:30], GB[:, kind(t), :], ALU.mult, ALU.mult))
                    dve.tensor_tensor(X[:, t, :], X[:, t, :], yupd, ALU.add).then_inc(s_yu, 1)


_INS = ["x", "c", "ctx", "c_ctx", "w_ada", "b_ada", "g_pre_mix", "g_post_mix", "g_pre_ffn", "g_post_ffn", "w_in", "w_out",
        "q_gain_a", "k_gain_a", "lam_q1", "lam_k1", "lam_q2", "lam_k2", "subln_gain_b", "sink_c", "rpb_d", "w_router",
        "w_gate", "w_up", "w_down"]


def kernel(**inputs):
    import concourse.bacc as _bacc
    from concourse.bass_utils import run_bass_kernel_spmd as _run

    nc = _bacc.Bacc("TRN2", target_bir_lowering=False, num_devices=1)
    arrays = {"in_" + n: np.ascontiguousarray(inputs[n]) for n in _INS}
    arrays["in_rope"] = rope_table()
    aps = {n[3:]: nc.dram_tensor(n, a.shape, F32, kind="ExternalInput").ap() for n, a in arrays.items()}
    out = nc.dram_tensor("out_0", (1, SEQ, D), F32, kind="ExternalOutput").ap()

    def scratch(name, shape):
        return nc.dram_tensor(name, shape, F32, kind="Internal").ap()

    xn_dram = [scratch(f"xn_{l}", (SEQ + (CTX if l < DEPTH - 1 else 0), D)) for l in range(DEPTH)]
    y_dram = [scratch(f"y_{l}", (SEQ + (CTX if l < DEPTH - 1 else 0), D)) for l in range(DEPTH)]
    rp_dram = scratch("rp", (DEPTH, GRID_W, 60 * P))
    hybrid_dit(nc, aps, out, xn_dram, y_dram, rp_dram)
    r = _run(nc, [arrays], core_ids=[0])
    return r.results[0]["out_0"]
```

```python
from contextlib import ExitStack
import math

import numpy as np
import concourse.bass as bass
from concourse import mybir

F32 = mybir.dt.float32
F32R = mybir.dt.float32r
U32 = mybir.dt.uint32
ALU = mybir.AluOpType
ACT = mybir.ActivationFunctionType
AX_X = mybir.AxisListType.X

P = 128
D = 1024
KC = D // P
SEQ, CTX = 512, 256
NT, NC = (SEQ + CTX) // P, CTX // P
DEPTH = 2
HD = 64
GRID_W = 64
PROJ = 2560
NE = 16
CAP_X, CAP_C = 2 * SEQ // NE, 2 * CTX // NE
EPS = 1e-6
NEG = -1e30
SCALE = HD ** -0.5
SCALE_B = (HD // 2) ** -0.5
INV_SCALE = 1.0 / SCALE
KiB = 256

GROUPS = [
    [("qa", 0, 256, 0), ("ka", 256, 128, 0), ("v", 384, 128, 0)],
    [("qb", 0, 256, 256), ("kb", 256, 256, 128)],
    [("v", 0, 256, 128), ("qc", 256, 256, 512)],
    [("kc", 0, 128, 384), ("v", 128, 128, 384), ("qd", 256, 256, 768)],
    [("kd", 0, 256, 512), ("v", 256, 256, 512)],
]
KV_SPAN = [(256, 512), (256, 512), (0, 256), (0, 256), (0, 512)]


def lam_init(l):
    return 0.8 - 0.6 * math.exp(-0.3 * l)


def rope_table():
    t = np.arange(SEQ)
    parts = []
    for dim in (HD, HD // 2):
        n = dim // 4
        inv = (np.float32(10000.0) ** (-np.arange(n, dtype=np.float32) / np.float32(n))).astype(np.float32)
        rows = (t // GRID_W).astype(np.float32)
        cols = (t % GRID_W).astype(np.float32)
        ang = np.concatenate([rows[:, None] * inv, cols[:, None] * inv], axis=-1).astype(np.float32)
        cos, sin = np.cos(ang), np.sin(ang)
        parts += [np.repeat(cos, 2, axis=1), np.stack([-sin, sin], axis=-1).reshape(SEQ, dim)]
    return np.concatenate(parts, axis=1).astype(np.float32)


def attention_plan():
    entries, scores, values, steps = [], [], [], []
    turned = 0

    def turn(l, t, x):
        nonlocal turned
        entries.append(dict(turn=True, l=l, t=t, mixer="ABCD"[x], x=x, no=turned, slot=len(entries),
                            before=len(scores)))
        turned += 1
        part.append(entries[-1])

    for l in range(DEPTH):
        part = []
        tiles = range(0 if l < DEPTH - 1 else NC, NT)
        order = [(t, x) for t in tiles for x in range(4)]
        turn(l, *order[0])
        for at, (t, x) in enumerate(order):
            i = t - NC
            mixer, no = "ABCD"[x], turned - 1
            for h in range(4):
                for c in range(2 if mixer == "B" else 1):
                    u = dict(turn=False, l=l, t=t, i=i, mixer=mixer, h=h, c=c, k=len(scores), slot=len(entries),
                             q=no)
                    if i < 0:
                        u["segs"], u["vt"] = [(0, 0, 256)], [0, 1]
                    elif mixer == "C":
                        first, n = max(i - 1, 0), 3 if 0 < i < NT - NC - 1 else 2
                        u["segs"] = [(0, 0, 256), (256, CTX + P * first, 256)]
                        if n == 3:
                            u["segs"].append((512, CTX + P * (first + 2), P))
                        u["vt"] = [0, 1] + [NC + first + j for j in range(n)]
                        u["left"] = i > 0
                        u["right"] = i < NT - NC - 1
                    else:
                        u["segs"], u["vt"] = [(0, 0, 512), (512, 512, 256)], list(range(NT))
                    u["nk"] = len(u["vt"]) * P
                    u["kv"] = (0, 2, 6, 8)[x] + (h // 2 if mixer in "AC" else h)
                    u["ocol"] = 256 * x + HD * h
                    scores.append(u)
                    entries.append(u)
                    part.append(u)
                    if mixer != "B" or c == 1:
                        u["m"] = len(values)
                        values.append(u)
                    if (h, c) == (1, 0) and at + 1 < len(order):
                        turn(l, *order[at + 1])
        steps.append(part)
    wide = diffs = 0
    for v in values:
        wide += v["nk"] > 512
        v["wide"] = wide
        diffs += v["mixer"] == "B"
        v["diffs"] = diffs
    out = []
    for l, part in enumerate(steps):
        rows = [dict(entry=u, turn=[], pv=[]) for u in part] + [dict(entry=None, turn=[], pv=[]) for _ in range(4)]
        base = part[0]["slot"]
        for v in values:
            if v["l"] == l:
                lag = 3 if v["mixer"] == "B" else 2
                rows[v["slot"] - base + lag]["turn"].append(v)
                rows[v["slot"] - base + lag + 1]["pv"].append(v)
        for no, row in enumerate(rows):
            row["no"] = no
        out.append(rows)
    return entries, scores, values, out


ENTRIES, SCORES, VALUES, STEPS = attention_plan()
TURNS = [e for e in ENTRIES if e["turn"]]


def _counts():
    raw_read, done = [], 0
    for l in range(DEPTH):
        for t in range(NT):
            for g in range(5):
                reads = not (g == 2 and l == DEPTH - 1 and t < NC)
                done += reads
                raw_read.append(done if reads else 0)
    p_last = []
    for u in SCORES:
        k = u["k"] - 4
        p_last.append(0 if k < 0 else min(v["m"] for v in VALUES if v["k"] >= k) + 1)
    sinks, done = [], 0
    for u in SCORES:
        done += u["mixer"] == "C"
        sinks.append(done)
    return raw_read, p_last, sinks


RAW_READ, P_LAST, SINKS = _counts()
ROW_TILES = [(l, t) for l in range(DEPTH) for t in range(0 if l < DEPTH - 1 else NC, NT)]
LAYER_ROWS = [[n for n, (l, _) in enumerate(ROW_TILES) if l == k] for k in range(DEPTH)]
LAYER_SCORES = [[u["k"] for u in SCORES if u["l"] == k] for k in range(DEPTH)]
LAYER_VALUES = [[v["m"] for v in VALUES if v["l"] == k] for k in range(DEPTH)]



def hybrid_dit(nc, I, out, xn_dram, y_dram, rp_dram):
    with ExitStack() as ctx:
        def sb(name, shape, dt=F32):
            return ctx.enter_context(nc.sbuf_tensor(name, shape, dt))

        def sem(name):
            return ctx.enter_context(nc.semaphore(name))

        X = sb("X", [P, NT, D])
        ident = sb("ident", [P, P])
        ones = sb("ones", [P, P])
        bandL = sb("bandL", [P, P])
        bandR = sb("bandR", [P, P])
        colmask = sb("colmask", [P, GRID_W])
        rope = sb("rope", [P, NT - NC, 192])
        modcol = sb("modcol", [P, DEPTH, 48, 2])
        gcol = sb("gcol", [P, KC, 8])
        mscale = sb("mscale", [P, DEPTH, 2, 2, KC])
        gate = sb("gate", [P, DEPTH, 2, 2, KC])
        cT = sb("cT", [P, KC, 2])
        qkgain = sb("qkgain", [P, DEPTH, 2, HD])
        subgain = sb("subgain", [P, DEPTH, HD])
        sink8 = sb("sink8", [P, DEPTH, 4])
        nsink8 = sb("nsink8", [P, DEPTH, 4])
        lamv = sb("lamv", [P, DEPTH, 4, 32])
        lamp = sb("lamp", [P, DEPTH, 2, 32])
        lams = sb("lams", [P, DEPTH, 2])
        nlam = sb("nlam", [P, DEPTH])
        halfneg = sb("halfneg", [P, 8])
        st = sb("st", [P, 64])
        wr = sb("wr", [P, KC, NE])
        arena = sb("arena", [P, 170 * KiB])

        base = nc.lookup_mloc(arena).addr

        def at(kib, shape, parts=P, rounded=None):
            n = int(np.prod(shape))
            if rounded:
                v = nc.alloc_sbuf_tensor_at(rounded, [P, n], F32R, offset=base + int(kib * 1024))[0:parts, 0:n]
            else:
                v = arena[0:parts, int(kib * KiB):int(kib * KiB) + n]
            if len(shape) > 1:
                names = "abcd"[:len(shape)]
                v = v.rearrange(f"p ({' '.join(names)}) -> p {' '.join(names)}",
                                **{x: s for x, s in zip(names[1:], shape[1:])})
            return v

        ada_ring = [at(80 + 16 * s, [KC, 512]) for s in range(3)]
        ada_row = [at(128 + 2 * s, [512], parts=2) for s in range(4)]
        crow, crow2 = at(0, [D], parts=2), at(4, [D], parts=2)
        grow = at(8, [D], parts=8)
        win = at(0, [KC, PROJ])
        Qrows = at(80, [NT, D])
        Krows = at(104, [NT, 768])
        V = at(122, [NT, 768])
        xn = at(140, [D])
        hT = [at(144 + 4 * s, [KC, P]) for s in range(2)]
        raw = [at(152 + 2 * s, [512]) for s in range(2)]
        tmp = [at(156 + 2 * s, [512]) for s in range(3)]
        rpbT = at(0, [4, 14, GRID_W])
        Kst = at(14, [12, NT * P], rounded="Kst")
        Qst = [at(50 + 4 * s, [2, 4, P], rounded=f"Qst{s}") for s in range(2)]
        Qd_r = [at(58 + 4 * s, [2, 512], rounded=f"Qd{s}") for s in range(2)]
        Qd = [v.bitcast(F32) for v in Qd_r]
        Kd_r = [at(66 + 6 * s, [12, P], rounded=f"Kd{s}") for s in range(2)]
        Kd = [v.bitcast(F32) for v in Kd_r]
        wout = [at(x, [D]) for x in (104, 108, 112, 116, 66, 70, 74, 0)]
        Ost = Qrows
        Pb = [at(140 + 3 * s, [768]) for s in range(4)]
        PT = [at(152 + 3 * s, [768]) for s in range(2)]
        rp = at(169.5, [P], parts=60)
        OT = [at(140 + 4 * s, [KC, P]) for s in range(2)]
        junk = at(148, [D])
        upd = at(152, [D])
        diag = at(156, [KC, P])
        GB = at(160, [2, D])
        RING = 6
        SLOT = (1, 2, 3, 0, 4, 5)
        unit = [at(16 * s, [4096]) for s in range(RING)]
        PIECES = 4
        w_hi, w_lo = ([at(96 + 8 * s + 4 * k, [2, 512], rounded=f"w_{'hl'[k]}{s}") for s in range(PIECES)] for k in range(2))
        xe = [at(128 + 4 * s, [D], parts=96) for s in range(2)]
        xeT = at(136, [KC, 96])
        xeT_hi, xeT_lo = ([at(139 + 6 * s + 3 * k, [KC, 96], rounded=f"xeT_{'hl'[k]}{s}") for s in range(2)] for k in range(2))
        hs = at(151, [D], parts=96)
        hsT = at(155, [KC, 96])
        sg = at(158, [2, 512], parts=96)
        ysc = [at(162 + 4 * s, [D], parts=96) for s in range(2)]
        affT = at(161, [NT * P], parts=NE)
        aff2 = at(164, [SEQ], parts=NE)
        fxn = [at(128 + 4 * s, [D]) for s in range(2)]
        fhT = [at(136 + 4 * s, [KC, P]) for s in range(2)]
        yrow = [at(128 + 4 * s, [D]) for s in range(2)]
        yupd = at(136, [D])
        zero = at(165, [D])
        vals = sb("vals", [NE, 96])
        idxu = sb("idxu", [NE, 96], U32)
        idxf = sb("idxf", [NE, 96])
        gT = sb("gT", [96, NE])
        idxT = sb("idxT", [96, NE + 1], U32)
        idc = sb("idc", [96, 4], U32)
        nmx = sb("nmx", [P, 8])
        sumx = sb("sumx", [P, 8])
        skx = sb("skx", [P, 8])
        rx = sb("rx", [P, 8])
        lg = sb("lg", [P, 2, NE])

        ps = ctx.enter_context(nc.psum_tensor("ps", [P, 8, 512], F32))

        def pb(b, n=1):
            return ps[:, b:b + n, :].rearrange("p b n -> p (b n)")

        s_in = sem("s_in")
        s_in2 = sem("s_in2")
        s_x = sem("s_x")
        s_const = sem("s_const")
        s_adaw = [sem(f"s_adaw{s}") for s in range(3)]
        s_csT = sem("s_csT")
        s_cs = sem("s_cs")
        s_adam = sem("s_adam")
        s_adab = [sem(f"s_adab{s}") for s in range(4)]
        s_adar = sem("s_adar")
        s_adat = sem("s_adat")
        s_mod = sem("s_mod")
        s_win = [sem(f"s_win{g}") for g in range(5)]
        s_ss = sem("s_ss")
        s_rs = sem("s_rs")
        s_xn = sem("s_xn")
        s_xt = sem("s_xt")
        s_ht = sem("s_ht")
        s_prj = sem("s_prj")
        s_raw = sem("s_raw")
        s_rawf = sem("s_rawf")
        s_hss = sem("s_hss")
        s_hrs = sem("s_hrs")
        s_kd = sem("s_kd")
        s_kt = sem("s_kt")
        s_kc = sem("s_kc")
        s_qh = sem("s_qh")
        s_ql = sem("s_ql")
        s_rpi = sem("s_rpi")
        s_rpz = sem("s_rpz")
        s_rpw = sem("s_rpw")
        s_rpl = sem("s_rpl")
        s_bias = sem("s_bias")
        s_wout = sem("s_wout")
        s_sc = sem("s_sc")
        s_mx = sem("s_mx")
        s_ex = sem("s_ex")
        s_sk = sem("s_sk")
        s_cb = sem("s_cb")
        s_tn = sem("s_tn")
        s_ta = sem("s_ta")
        s_tb = sem("s_tb")
        s_pv = sem("s_pv")
        s_o = sem("s_o")
        s_gd = sem("s_gd")
        s_gm = sem("s_gm")
        s_gb = sem("s_gb")
        s_bss = sem("s_bss")
        s_brs = sem("s_brs")
        s_on = sem("s_on")
        s_ot = sem("s_ot")
        s_oc = sem("s_oc")
        s_om = sem("s_om")
        s_oss = sem("s_oss")
        s_ors = sem("s_ors")
        s_xu = sem("s_xu")
        s_wr = sem("s_wr")
        s_fss = sem("s_fss")
        s_frs = sem("s_frs")
        s_fxn = sem("s_fxn")
        s_fst = [sem("s_fst0"), sem("s_fst1")]
        s_ft = sem("s_ft")
        s_fh = sem("s_fh")
        s_fv = sem("s_fv")
        s_lg = sem("s_lg")
        s_lm = sem("s_lm")
        s_le = sem("s_le")
        s_lp = sem("s_lp")
        s_lt = sem("s_lt")
        s_lc = sem("s_lc")
        s_top = sem("s_top")
        s_tt = sem("s_tt")
        s_tc = sem("s_tc")
        s_w = [sem(f"s_w{s}") for s in range(RING)]
        s_wf = sem("s_wf")
        s_hi = sem("s_hi")
        s_lo = sem("s_lo")
        s_pr = sem("s_pr")
        s_idc = sem("s_idc")
        s_g = [sem("s_g0"), sem("s_g1")]
        s_et = sem("s_et")
        s_ec = sem("s_ec")
        s_xs = sem("s_xs")
        s_eg = sem("s_eg")
        s_hs = sem("s_hs")
        s_hst = sem("s_hst")
        s_hsc = sem("s_hsc")
        s_yd = sem("s_yd")
        s_yc = sem("s_yc")
        s_sct = sem("s_sct")
        s_z = sem("s_z")
        s_yl = [sem("s_yl0"), sem("s_yl1")]
        s_yss = sem("s_yss")
        s_yrs = sem("s_yrs")
        s_yu = sem("s_yu")
        s_out = sem("s_out")
        s_vch = sem("s_vch")
        s_vlam = sem("s_vlam")
        s_ach = sem("s_ach")
        s_pch = sem("s_pch")

        block = ctx.enter_context(nc.Block())
        n_small = [0]

        def paired(q, mixer):
            d = HD // 2 if mixer == "B" else HD
            q = q.rearrange("p (h d) -> p h d", d=d)
            return (q.unsqueeze(2).broadcast_to([P, 256 // d, 2, d]),
                    lambda v: v.rearrange("p (h r d) -> p h r d", r=2, d=d))

        def kind(t):
            return 0 if t < NC else 1

        def first_tile(l):
            return 0 if l < DEPTH - 1 else NC

        N_CLEAR = sum(NT - first_tile(l) for l in range(DEPTH))

        @block.sync
        def _(sp):
            def small(dst, src):
                sp.dma_start(dst, src).then_inc(s_in, 16)
                n_small[0] += 1

            small(crow[0:1, :], I["c_ctx"].rearrange("(a d) -> a d", a=1))
            small(crow[1:2, :], I["c"])
            for g, name in enumerate(("g_pre_mix", "g_post_mix", "g_pre_ffn", "g_post_ffn")):
                small(grow[2 * g:2 * g + 2, :], I[name])

            def ada_load(n):
                if n >= 4:
                    sp.wait_ge(s_adat, n - 3)
                sp.dma_start(ada_row[n % 4], bass.AP(I["b_ada"].tensor, 512 * n, [[0, 2], [1, 512]])
                             ).then_inc(s_adab[n % 4], 16)
                if n >= 3:
                    sp.wait_ge(s_adam, n - 2)
                sp.dma_start(ada_ring[n % 3],
                             I["w_ada"][n // 12].rearrange("(c p) n -> p c n", p=P)[:, :, 512 * (n % 12):512 * (n % 12) + 512]
                             ).then_inc(s_adaw[n % 3], 16)

            for n in range(12):
                ada_load(n)
            sp.dma_start(X[:, 0:NC, :], I["ctx"][0].rearrange("(t p) d -> p t d", p=P)).then_inc(s_x, 16)
            sp.dma_start(X[:, NC:NT, :], I["x"][0].rearrange("(t p) d -> p t d", p=P)).then_inc(s_x, 16)
            sp.wait_ge(s_cs, 3)
            for g in range(5):
                sp.dma_start(win[:, :, 512 * g:512 * g + 512],
                             I["w_in"][0].rearrange("(c p) n -> p c n", p=P)[:, :, 512 * g:512 * g + 512]
                             ).then_inc(s_win[g], 16)
            for n in range(12, 24):
                ada_load(n)

            def in2(dst, src):
                sp.dma_start(dst, src).then_inc(s_in2, 16)

            in2(rope[:], I["rope"].rearrange("(t p) n -> p t n", p=P))
            for l in range(DEPTH):
                in2(qkgain[:, l, 0, :], bass.AP(I["q_gain_a"].tensor, HD * l, [[0, P], [1, HD]]))
                in2(qkgain[:, l, 1, :], bass.AP(I["k_gain_a"].tensor, HD * l, [[0, P], [1, HD]]))
                for j, name in enumerate(("lam_q1", "lam_q2", "lam_k1", "lam_k2")):
                    in2(lamv[:, l, j, :], bass.AP(I[name].tensor, 32 * l, [[0, P], [1, 32]]))
            in2(subgain[:], bass.AP(I["subln_gain_b"].tensor, 0, [[0, P], [1, DEPTH * HD]]))
            in2(sink8[:], bass.AP(I["sink_c"].tensor, 0, [[0, P], [1, DEPTH * 4]]))

            sp.wait_ge(s_const, 2)
            for l in range(DEPTH):
                for t in range(NT - first_tile(l)):
                    sp.dma_start(y_dram[l][P * t:P * t + P, :], zero).then_inc(s_z, 16)

            for l in range(DEPTH):
                rows = LAYER_ROWS[l]
                if l == 0:
                    sp.wait_ge(s_z, 16 * N_CLEAR)
                sp.wait_ge(s_rpz, l + 1)
                sp.dma_start(rp[:, 48:79], I["rpb_d"][l].rearrange("h r c -> (h r) c")).then_inc(s_rpi, 16)
                sp.wait_ge(s_rpi, 16 * (l + 1))
                sp.dma_start(rp_dram[l].rearrange("c (r j) -> r c j", j=P),
                             rp.unsqueeze(1).broadcast_to([60, GRID_W, P])).then_inc(s_rpw, 16)
                sp.wait_ge(s_rpw, 16 * (l + 1))
                sp.wait_ge(s_prj, 5 * NT * (l + 1))
                for up in range(2):
                    for h in range(4):
                        src = bass.AP(rp_dram.tensor, l * GRID_W * 60 * P + 63 + P * (15 * h + 1 - up),
                                      [[60 * P - 1, GRID_W], [P, 14], [1, GRID_W]])
                        sp.dma_start(rpbT[64 * up:64 * up + 64, h], src).then_inc(s_rpl, 16)
                sp.wait_ge(s_kc, NT * (l + 1))
                for c in range(7):
                    sp.dma_start(wout[c], I["w_out"][l][P * c:P * c + P, :]).then_inc(s_wout, 16)
                sp.dma_start(wr[:], I["w_router"][l].rearrange("(c p) n -> p c n", p=P)).then_inc(s_wr, 16)

                wg = I["w_gate"][l].rearrange("e (c p) f -> e p c f", p=P)
                wu = I["w_up"][l].rearrange("e (c p) f -> e p c f", p=P)
                wd = I["w_down"][l].rearrange("e (c p) n -> e p c n", p=P)

                def load_unit(e, part, slot):
                    if part < 4:
                        src = (wg, wu)[part % 2][e, :, :, 512 * (part // 2):512 * (part // 2) + 512]
                        dst = unit[slot].rearrange("p (c n) -> p c n", n=512)
                    else:
                        src = wd[e, :, 4 * (part - 4):4 * (part - 4) + 4, :]
                        dst = unit[slot].rearrange("p (c n) -> p c n", n=D)
                    sp.dma_start(dst, src).then_inc(s_w[slot], 16)

                sp.wait_ge(s_pv, LAYER_VALUES[l][-1] + 1)
                sp.dma_start(wout[7], I["w_out"][l][7 * P:D, :]).then_inc(s_wout, 16)
                for n in range(3):
                    load_unit(0, n, SLOT[n % RING])
                sp.wait_ge(s_om, rows[-1] + 1)
                for n in range(3, RING):
                    load_unit(0, n, SLOT[n])
                for n in rows:
                    t = ROW_TILES[n][1] - first_tile(l)
                    sp.wait_ge(s_fxn, n + 1)
                    sp.dma_start(xn_dram[l][P * t:P * t + P, :], fxn[n % 2]).then_inc(s_fst[n % 2], 16)
                for n in range(RING, 6 * NE):
                    before, part = NE * l + n // 6 - 1, n % 6
                    if part < 4:
                        sp.wait_ge(s_lo, 16 * before + 4 * part + 4)
                    else:
                        sp.wait_ge(s_wf, 2 * before + part - 3)
                    load_unit(n // 6, part, SLOT[part])
                if l + 1 < DEPTH:
                    sp.wait_ge(s_wf, 2 * NE * (l + 1))
                    for g in range(5):
                        sp.dma_start(win[:, :, 512 * g:512 * g + 512],
                                     I["w_in"][l + 1].rearrange("(c p) n -> p c n", p=P)[:, :, 512 * g:512 * g + 512]
                                     ).then_inc(s_win[g], 16)
                sp.wait_ge(s_sct, 16 * NE * (l + 1))
                for n in rows:
                    t = ROW_TILES[n][1] - first_tile(l)
                    if n >= 2:
                        sp.wait_ge(s_yu, n - 1)
                    sp.dma_start(yrow[n % 2], y_dram[l][P * t:P * t + P, :]).then_inc(s_yl[n % 2], 16)
            for j, n in enumerate(LAYER_ROWS[DEPTH - 1]):
                sp.wait_ge(s_yu, n + 1)
                sp.dma_start(out[0, P * j:P * j + P, :], X[:, NC + j, :]).then_inc(s_out, 16)
            sp.wait_ge(s_out, 16 * (NT - NC))

        @block.gpsimd
        def _(pool):
            chain = [0]

            def link(ins):
                chain[0] += 1
                ins.then_inc(s_pch, 1)
                pool.wait_ge(s_pch, chain[0])

            link(pool.memset(ident[:], 0.0))
            link(pool.memset(ones[:], 1.0))
            link(pool.memset(halfneg[:], -0.5))
            pool.affine_select(out=ident[:], in_=ident[:], compare_op=ALU.not_equal, fill=1.0, base=0,
                               pattern=[[-1, P]], channel_multiplier=1).then_inc(s_const, 1)
            link(pool.memset(zero, 0.0))
            link(pool.memset(colmask[:], 0.0))
            for half in range(2):
                m = colmask[64 * half:64 * half + 64, :]
                link(pool.affine_select(out=m[:, 0:48], in_=m[:, 0:48], compare_op=ALU.is_ge, fill=NEG * INV_SCALE,
                                        base=8, pattern=[[1, 48]], channel_multiplier=-1))
                link(pool.affine_select(out=m[:, 16:64], in_=m[:, 16:64], compare_op=ALU.is_ge, fill=NEG * INV_SCALE,
                                        base=7 - 16, pattern=[[-1, 48]], channel_multiplier=1))
            link(pool.memset(bandL[:], 0.0))
            link(pool.memset(bandR[:], 0.0))
            link(pool.memset(idxT[:], 0))
            link(pool.affine_select(out=bandL[:], in_=bandL[:], compare_op=ALU.is_ge, fill=NEG, base=0,
                                    pattern=[[1, P]], channel_multiplier=-1))
            pool.affine_select(out=bandR[:], in_=bandR[:], compare_op=ALU.is_ge, fill=NEG, base=0,
                               pattern=[[-1, P]], channel_multiplier=1).then_inc(s_const, 1)

            def inverse_root(dst, src, width, n_el, wait, done, value):
                pool.wait_ge(wait, value)
                link(pool.tensor_scalar(dst, src, 1.0 / width, EPS, ALU.mult, ALU.add))
                pool.tensor_tensor(dst, dst, halfneg[:, 0:n_el], ALU.pow).then_inc(done, 1)

            for l in range(DEPTH):
                rows = LAYER_ROWS[l]
                if l > 0:
                    pool.wait_ge(s_yu, LAYER_ROWS[l - 1][-1] + 1)
                pool.memset(rp, 0.0).then_inc(s_rpz, 1)
                inverse_root(st[:, 1:2], st[:, 0:1], D, 1, s_ss, s_rs, NT * l + 1)
                for t in range(NT):
                    n = NT * l + t
                    inverse_root(st[:, 8:14], st[:, 2:8], HD, 6, s_hss, s_hrs, n + 1)
                    if t + 1 < NT:
                        pool.wait_ge(s_xn, n + 1)
                        inverse_root(st[:, 1:2], st[:, 0:1], D, 1, s_ss, s_rs, n + 2)
                for e in TURNS:
                    if e["l"] != l:
                        continue
                    pool.wait_ge(s_qh, e["no"] + 1)
                    q, dup = paired(Qrows[:, e["t"], 256 * e["x"]:256 * e["x"] + 256], e["mixer"])
                    pool.tensor_tensor(dup(Qd_r[e["no"] % 2][:, 1]), q, dup(Qd[e["no"] % 2][:, 0]), ALU.subtract
                                       ).then_inc(s_ql, 1)
                inverse_root(st[:, 20:24], st[:, 16:20], HD, 4, s_bss, s_brs, rows[0] + 1)
                pool.wait_ge(s_on, rows[0] + 1)
                inverse_root(st[:, 20:24], st[:, 16:20], HD, 4, s_bss, s_brs, rows[0] + 2)
                for n in rows:
                    if n + 2 <= rows[-1]:
                        pool.wait_ge(s_on, n + 2)
                        inverse_root(st[:, 20:24], st[:, 16:20], HD, 4, s_bss, s_brs, n + 3)
                    if n > 0:
                        pool.wait_ge(s_xu, n)
                    inverse_root(st[:, 25:26], st[:, 24:25], D, 1, s_oss, s_ors, n + 1)
                for n in rows:
                    if n > 0:
                        pool.wait_ge(s_fxn, n)
                    inverse_root(st[:, 27:28], st[:, 26:27], D, 1, s_fss, s_frs, n + 1)
                M = 96 if l < DEPTH - 1 else CAP_X
                pool.wait_ge(s_tc, 2 * (l + 1))
                pool.wait_ge(s_fst[0], 16 * (rows[-1] // 2 + 1))
                pool.wait_ge(s_fst[1], 16 * ((rows[-1] + 1) // 2))

                def gather(e):
                    E = NE * l + e
                    pool.tensor_copy(idc[0:M, e % 4:e % 4 + 1], idxT[0:M, e:e + 1]).then_inc(s_idc, 1)
                    pool.wait_ge(s_idc, E + 1)
                    if e >= 2:
                        pool.wait_ge(s_et, 2 * (E - 1))
                    pool.indirect_dma_start(out=xe[e % 2][0:M], out_offset=None, in_=xn_dram[l],
                                            in_offset=bass.IndirectOffsetOnAxis(idc[0:M, e % 4:e % 4 + 1], 0)
                                            ).then_inc(s_g[e % 2], 16)

                def split_xe(e):
                    E = NE * l + e
                    pool.wait_ge(s_ec, 2 * E + 2)
                    if e >= 2:
                        pool.wait_ge(s_pr, 16 * (E - 1))
                    full, hi, lo = xeT[:, :, 0:M], xeT_hi[e % 2][:, :, 0:M], xeT_lo[e % 2][:, :, 0:M]
                    link(pool.tensor_copy(hi, full))
                    pool.tensor_tensor(lo, full, hi.bitcast(F32), ALU.subtract).then_inc(s_xs, 1)

                gather(0)
                gather(1)
                split_xe(0)
                for e in range(NE):
                    E = NE * l + e
                    if e + 2 < NE:
                        gather(e + 2)
                    if e + 1 < NE:
                        split_xe(e + 1)
                    pool.wait_ge(s_yc, E + 1)
                    if e:
                        pool.wait_ge(s_sct, 16 * E)
                    elif l == 0:
                        pool.wait_ge(s_z, 16 * N_CLEAR)
                    pool.indirect_dma_start(out=y_dram[l],
                                            out_offset=bass.IndirectOffsetOnAxis(idc[0:M, e % 4:e % 4 + 1], 0),
                                            in_=ysc[e % 2][0:M], in_offset=None, compute_op=ALU.add).then_inc(s_sct, 16)
                for n in rows:
                    if n > 0:
                        pool.wait_ge(s_yu, n)
                    inverse_root(st[:, 29:30], st[:, 28:29], D, 1, s_yss, s_yrs, n + 1)

        @block.tensor
        def _(pe):
            pe.wait_ge(s_const, 1)
            pe.wait_ge(s_cs, 1)
            for c in range(KC):
                mm = pe.transpose(pb(0)[:, 2 * c:2 * c + 2], crow2[:, P * c:P * c + P], ident[0:2, 0:2])
            mm.then_inc(s_csT, 1)
            for c in range(KC):
                mm = pe.transpose(pb(1)[:, 8 * c:8 * c + 8], grow[:, P * c:P * c + P], ident[0:8, 0:8])
            mm.then_inc(s_csT, 1)
            pe.wait_ge(s_cs, 2)

            def turn_piece(n):
                l, q = n // 12, n % 12
                pe.wait_ge(s_adar, n + 1)
                for j in range(4):
                    mm = pe.transpose(pb(4 + l)[:, 2 * (4 * q + j):2 * (4 * q + j) + 2],
                                      ada_row[n % 4][:, P * j:P * j + P], ident[0:2, 0:2])
                mm.then_inc(s_adat, 1)

            for n in range(24):
                pe.wait_ge(s_adaw[n % 3], 16 * (n // 3 + 1))
                if n >= 2:
                    pe.wait_ge(s_adar, n - 1)
                for c in range(KC):
                    mm = pe.matmul(pb(2 + n % 2)[0:2, :], cT[:, c, :], ada_ring[n % 3][:, c, :],
                                   start=(c == 0), stop=(c == KC - 1))
                mm.then_inc(s_adam, 1)
                if n:
                    turn_piece(n - 1)
            turn_piece(23)
            pe.wait_ge(s_mod, 1)

            gate_no = [0]

            def gate_rows():
                q = gate_no[0]
                pe.wait_ge(s_gd, q + 1)
                for h in range(2):
                    mm = pe.matmul(pb(6 + h), ones[:], diag[:, 4 * h:4 * h + 4, :].rearrange("p c n -> p (c n)"),
                                   start=True, stop=True)
                mm.then_inc(s_gm, 1)
                gate_no[0] += 1

            for l in range(DEPTH):
                def turn_rows(n):
                    pe.wait_ge(s_xn, n + 1)
                    if n:
                        pe.wait_ge(s_ht, n)
                    for c in range(KC):
                        mm = pe.transpose(pb(c // 4)[:, P * (c % 4):P * (c % 4) + P], xn[:, P * c:P * c + P], ident[:])
                    mm.then_inc(s_xt, 1)

                def only_kv(t):
                    return l == DEPTH - 1 and t < NC

                turn_rows(NT * l)
                for t in range(NT):
                    n = NT * l + t
                    pe.wait_ge(s_ht, n + 1)
                    for g in range(5):
                        G = 5 * n + g
                        lo, hi = KV_SPAN[g] if only_kv(t) else (0, 512)
                        if t == 0:
                            pe.wait_ge(s_win[g], 16 * (l + 1))
                        if G >= 2:
                            pe.wait_ge(s_raw, G - 1)
                        for c in range(KC):
                            mm = pe.matmul(pb(2 + G % 2)[:, lo:hi], hT[n % 2][:, c, :],
                                           win[:, c, 512 * g + lo:512 * g + hi], start=(c == 0), stop=(c == KC - 1))
                        mm.then_inc(s_prj, 1)
                        if g == 2 and t + 1 < NT:
                            turn_rows(n + 1)
                for t in range(NT):
                    n = NT * l + t
                    pe.wait_ge(s_kd, n + 1)
                    if n >= 2:
                        pe.wait_ge(s_kc, n - 1)
                    for b in range(12):
                        mm = pe.transpose(pb(4 * (n % 2) + b // 4)[:, P * (b % 4):P * (b % 4) + P], Kd[n % 2][:, b, :], ident[:])
                    mm.then_inc(s_kt, 1)
                pe.wait_ge(s_kc, NT * (l + 1))
                for step in STEPS[l]:
                    u = step["entry"]
                    if u:
                        S = pb(2 * (u["slot"] % 2), 2)
                        if u["slot"] >= 2:
                            pe.wait_ge(s_ex, u["slot"] - 1)
                    if u and u["turn"]:
                        pe.wait_ge(s_ql, u["no"] + 1)
                        for b in range(8):
                            mm = pe.transpose(S[:, P * b:P * b + P], Qd[u["no"] % 2][:, b // 4, P * (b % 4):P * (b % 4) + P],
                                              ident[:])
                        mm.then_inc(s_sc, 1)
                    elif u:
                        r0, r1 = (HD * u["c"], HD * u["c"] + HD) if u["mixer"] == "B" else (0, P)
                        pe.wait_ge(s_ex, TURNS[u["q"]]["slot"] + 1)
                        for col, src, width in u["segs"]:
                            for part in range(2):
                                mm = pe.matmul(S[:, col:col + width], Qst[u["q"] % 2][r0:r1, part, u["h"], :],
                                               Kst[r0:r1, u["kv"], src:src + width], start=(part == 0), stop=(part == 1))
                        mm.then_inc(s_sc, 1)
                    for v in step["turn"]:
                        m, k = v["m"], v["k"]
                        if v["mixer"] == "B":
                            pe.wait_ge(s_cb, v["diffs"])
                        else:
                            pe.wait_ge(s_ex, v["slot"] + 1)
                        if m:
                            pe.wait_ge(s_ta, m)
                            pe.wait_ge(s_tb, v["wide"] - (v["nk"] > 512))
                        src = Pb[(k - 1) % 4] if v["mixer"] == "B" else Pb[k % 4]
                        for j in range(v["nk"] // P):
                            mm = pe.transpose(pb(4 + j // 4)[:, P * (j % 4):P * (j % 4) + P], src[:, P * j:P * j + P], ident[:])
                        mm.then_inc(s_tn, 1)
                    for v in step["pv"]:
                        m = v["m"]
                        pe.wait_ge(s_ta, m + 1)
                        pe.wait_ge(s_tb, v["wide"])
                        if m >= 2:
                            pe.wait_ge(s_o, m - 1)
                        for j, vt in enumerate(v["vt"]):
                            mm = pe.matmul(pb(6 + m % 2)[:, 0:HD], PT[m % 2][:, P * j:P * j + P],
                                           V[:, vt, HD * v["kv"]:HD * v["kv"] + HD], start=(j == 0), stop=(j == len(v["vt"]) - 1))
                        mm.then_inc(s_pv, 1)
                rows = LAYER_ROWS[l]
                pe.wait_ge(s_o, LAYER_VALUES[l][-1] + 1)
                for _ in range(2):
                    gate_rows()
                    pe.wait_ge(s_gb, gate_no[0])

                def turn_out(n):
                    t = ROW_TILES[n][1]
                    pe.wait_ge(s_on, n + 1)
                    if n:
                        pe.wait_ge(s_oc, n)
                    for c in range(KC):
                        mm = pe.transpose(pb(c // 4)[:, P * (c % 4):P * (c % 4) + P], Ost[:, t, P * c:P * c + P], ident[:])
                    mm.then_inc(s_ot, 1)

                turn_out(rows[0])
                turn_out(rows[1])
                pe.wait_ge(s_wout, 16 * KC * (l + 1))
                for n in rows:
                    pe.wait_ge(s_oc, n + 1)
                    if n >= 2:
                        pe.wait_ge(s_xu, n - 1)
                    for h in range(2):
                        for c in range(KC):
                            mm = pe.matmul(pb(2 + 2 * (n % 2) + h), OT[n % 2][:, c, :], wout[c][:, 512 * h:512 * h + 512],
                                           start=(c == 0), stop=(c == KC - 1))
                    mm.then_inc(s_om, 1)
                    if n + 2 <= rows[-1]:
                        turn_out(n + 2)
                def turn_f(n):
                    pe.wait_ge(s_fxn, n + 1)
                    if n >= 2:
                        pe.wait_ge(s_fh, n - 1)
                        pe.wait_ge(s_fv, n - 1)
                    for c in range(KC):
                        mm = pe.transpose(pb(2 * (n % 2) + c // 4)[:, P * (c % 4):P * (c % 4) + P],
                                          fxn[n % 2][:, P * c:P * c + P], ident[:])
                    mm.then_inc(s_ft, 1)

                def turn_aff(n):
                    pe.wait_ge(s_lp, n + 1)
                    if n >= 2:
                        pe.wait_ge(s_lc, n - 1)
                    pe.transpose(pb(6 + n % 2)[0:NE, 0:P], lg[:, n % 2, :], ident[:]).then_inc(s_lt, 1)

                pe.wait_ge(s_xu, rows[-1] + 1)
                pe.wait_ge(s_wr, 16 * (l + 1))
                turn_f(rows[0])
                for n in rows:
                    if n < rows[-1]:
                        turn_f(n + 1)
                    pe.wait_ge(s_fh, n + 1)
                    pe.wait_ge(s_fv, n + 1)
                    if n >= 2:
                        pe.wait_ge(s_le, n - 1)
                    for c in range(KC):
                        mm = pe.matmul(pb(4 + n % 2)[:, 0:NE], fhT[n % 2][:, c, :], wr[:, c, :],
                                       start=(c == 0), stop=(c == KC - 1))
                    mm.then_inc(s_lg, 1)
                    if n > rows[0]:
                        turn_aff(n - 1)
                turn_aff(rows[-1])
                M = 96 if l < DEPTH - 1 else CAP_X
                pe.wait_ge(s_top, l + 1)
                pe.transpose(pb(4)[0:M, 0:NE], vals[:, 0:M], ident[0:NE, 0:NE])
                pe.transpose(pb(5)[0:M, 0:NE], idxf[:, 0:M], ident[0:NE, 0:NE]).then_inc(s_tt, 1)
                pe.wait_ge(s_tc, 2 * (l + 1))

                def turn_xe(e):
                    E = NE * l + e
                    pe.wait_ge(s_g[e % 2], 16 * (E // 2 + 1))
                    for half in range(2):
                        free = 2 * E if e == 0 else 2 * E - 3 + half
                        if free > 0:
                            pe.wait_ge(s_hsc, free)
                        for c in range(4 * half, 4 * half + 4):
                            mm = pe.transpose(pb(6 + half)[:, P * (c % 4):P * (c % 4) + M], xe[e % 2][0:M, P * c:P * c + P],
                                              ident[0:M, 0:M])
                        mm.then_inc(s_et, 1)

                def gate_up(e, half, part):
                    E = NE * l + e
                    if E:
                        pe.wait_ge(s_hs, 2 * (E - 1) + half + 1)
                    out = pb(2 * half + part)[0:M, :]
                    for q in range(4):
                        piece = 16 * E + 4 * (2 * half + part) + q
                        pe.wait_ge(s_lo, piece + 1)
                        for j in range(2):
                            c = 2 * q + j
                            hi, lo = xeT_hi[e % 2][:, c, 0:M], xeT_lo[e % 2][:, c, 0:M]
                            wh, wl = w_hi[piece % PIECES][:, j, :], w_lo[piece % PIECES][:, j, :]
                            pe.matmul(out, hi, wh, start=(c == 0), stop=False)
                            pe.matmul(out, hi, wl, start=False, stop=False)
                            mm = pe.matmul(out, lo, wh, start=False, stop=(c == KC - 1))
                        mm.then_inc(s_pr, 1)

                def turn_hs(e, half):
                    E = NE * l + e
                    pe.wait_ge(s_hs, 2 * E + half + 1)
                    if e + 1 < NE:
                        pe.wait_ge(s_ec, 2 * (E + 1) + half + 1)
                    for c in range(4 * half, 4 * half + 4):
                        mm = pe.transpose(pb(6 + half)[:, P * (c % 4):P * (c % 4) + M], hs[0:M, P * c:P * c + P],
                                          ident[0:M, 0:M])
                    mm.then_inc(s_hst, 1)

                def down(e, half):
                    E = NE * l + e
                    pe.wait_ge(s_w[SLOT[4 + half]], 16 * (E + 1))
                    w = unit[SLOT[4 + half]].rearrange("p (c n) -> p c n", n=D)
                    pe.wait_ge(s_hsc, 2 * E + half + 1)
                    if half == 0 and E:
                        pe.wait_ge(s_yc, E)
                    for c in range(4):
                        for h in range(2):
                            mm = pe.matmul(pb(4 + h)[0:M, :], hsT[:, 4 * half + c, 0:M], w[:, c, 512 * h:512 * h + 512],
                                           start=(half == 0 and c == 0), stop=(half == 1 and c == 3))
                    mm.then_inc(s_wf, 1)

                turn_xe(0)
                for e in range(NE):
                    pe.wait_ge(s_xs, NE * l + e + 1)
                    gate_up(e, 0, 0)
                    gate_up(e, 0, 1)
                    if e + 1 < NE:
                        turn_xe(e + 1)
                    gate_up(e, 1, 0)
                    turn_hs(e, 0)
                    gate_up(e, 1, 1)
                    down(e, 0)
                    turn_hs(e, 1)
                    down(e, 1)
                pe.wait_ge(s_hsc, 2 * NE * (l + 1))
                for _ in range(2):
                    gate_rows()
                    pe.wait_ge(s_gb, gate_no[0])

        @block.scalar
        def _(act):
            act.wait_ge(s_in, 16 * n_small[0])
            act.activation(crow2, crow, ACT.Exp, scale=-1.0).then_inc(s_ach, 1)
            gate_no = [0]

            def gate_rows():
                q = gate_no[0]
                act.wait_ge(s_gm, q + 1)
                act.activation(GB[:, q % 2, :], pb(6, 2), ACT.Copy).then_inc(s_gb, 1)
                gate_no[0] += 1

            act.wait_ge(s_mod, 1)
            act.wait_ge(s_vlam, 1)
            act.activation(lams[:], lams[:], ACT.Exp).then_inc(s_ach, 1)
            for l in range(DEPTH):
                rows = LAYER_ROWS[l]
                def square_rows(n):
                    t = n - NT * l
                    if n:
                        act.wait_ge(s_rs, n)
                        act.wait_ge(s_xt, n)
                    act.activation(xn, X[:, t, :], ACT.Square, accum_out=st[:, 0:1]).then_inc(s_ss, 1)

                def modulate(n):
                    t = n - NT * l
                    act.wait_ge(s_xt, n + 1)
                    for c in range(KC):
                        ins = act.activation(hT[n % 2][:, c, :], pb(c // 4)[:, P * (c % 4):P * (c % 4) + P], ACT.Identity,
                                             scale=mscale[:, l, 0, kind(t), c:c + 1], bias=modcol[:, l, c, kind(t):kind(t) + 1])
                    ins.then_inc(s_ht, 1)

                if l == 0:
                    act.wait_ge(s_x, 32)
                else:
                    act.wait_ge(s_yu, LAYER_ROWS[l - 1][-1] + 1)
                square_rows(NT * l)
                modulate(NT * l)
                for t in range(NT):
                    n = NT * l + t
                    only_kv = l == DEPTH - 1 and t < NC
                    for g in range(5):
                        G = 5 * n + g
                        act.wait_ge(s_prj, G + 1)
                        if RAW_READ[G - 2] if G >= 2 else 0:
                            act.wait_ge(s_rawf, RAW_READ[G - 2])
                        for what, col, width, dst in GROUPS[g]:
                            if only_kv and what[0] == "q":
                                continue
                            src = pb(2 + G % 2)[:, col:col + width]
                            if what == "v":
                                ins = act.activation(V[:, t, dst:dst + width], src, ACT.Copy)
                            else:
                                ins = act.activation(raw[G % 2][:, col:col + width], src, ACT.Copy)
                        ins.then_inc(s_raw, 1)
                        if g == 1 and t + 1 < NT:
                            square_rows(n + 1)
                        if g == 2 and t + 1 < NT:
                            modulate(n + 1)
                def high_parts(no):
                    e = TURNS[no]
                    q, dup = paired(Qrows[:, e["t"], 256 * e["x"]:256 * e["x"] + 256], e["mixer"])
                    if no >= 2:
                        act.wait_ge(s_sc, TURNS[no - 2]["slot"] + 1)
                    act.activation(dup(Qd_r[no % 2][:, 0]), q, ACT.Copy).then_inc(s_qh, 1)

                first = [e["no"] for e in TURNS if e["l"] == l]
                act.wait_ge(s_rawf, RAW_READ[5 * NT * (l + 1) - 1])
                high_parts(first[0])
                high_parts(first[1])
                for t in range(NT):
                    n = NT * l + t
                    act.wait_ge(s_kt, n + 1)
                    act.activation(Kst[:, :, P * t:P * t + P], pb(4 * (n % 2), 3).rearrange("p (b n) -> p b n", n=P),
                                   ACT.Copy).then_inc(s_kc, 1)
                for step in STEPS[l]:
                    u = step["entry"]
                    if u and u["turn"]:
                        act.wait_ge(s_sc, u["slot"] + 1)
                        act.activation(Qst[u["no"] % 2].rearrange("p s h n -> p (s h n)"), pb(2 * (u["slot"] % 2), 2),
                                       ACT.Copy).then_inc(s_ex, 1)
                        if u["no"] + 2 <= first[-1]:
                            high_parts(u["no"] + 2)
                    elif u:
                        k = u["k"]
                        act.wait_ge(s_mx, k + 1)
                        last = P_LAST[k]
                        if last:
                            act.wait_ge(s_tn, last)
                        act.activation(Pb[k % 4][:, 0:u["nk"]], pb(2 * (u["slot"] % 2), 2)[:, 0:u["nk"]], ACT.Exp,
                                       bias=nmx[:, k % 8:k % 8 + 1], scale=SCALE_B if u["mixer"] == "B" else SCALE,
                                       accum_out=sumx[:, k % 8:k % 8 + 1]).then_inc(s_ex, 1)
                        if u["mixer"] == "C":
                            act.activation(skx[:, k % 8:k % 8 + 1], sink8[:, l, u["h"]:u["h"] + 1], ACT.Exp,
                                           bias=nmx[:, k % 8:k % 8 + 1], scale=SCALE).then_inc(s_sk, 1)
                    for v in step["turn"]:
                        m = v["m"]
                        act.wait_ge(s_tn, m + 1)
                        if m >= 2:
                            act.wait_ge(s_pv, m - 1)
                        w = min(v["nk"], 512)
                        act.activation(PT[m % 2][:, 0:w], pb(4)[:, 0:w], ACT.Copy).then_inc(s_ta, 1)
                for _ in range(2):
                    gate_rows()

                def store_out(n):
                    act.wait_ge(s_ot, n + 1)
                    if n >= 2:
                        act.wait_ge(s_om, n - 1)
                    act.activation(OT[n % 2].rearrange("p c n -> p (c n)"), pb(0, 2), ACT.Copy).then_inc(s_oc, 1)

                store_out(rows[0])
                store_out(rows[1])
                for n in rows:
                    act.wait_ge(s_om, n + 1)
                    if n:
                        act.wait_ge(s_ors, n)
                    act.activation(junk, pb(2 + 2 * (n % 2), 2), ACT.Square, accum_out=st[:, 24:25]).then_inc(s_oss, 1)
                    if n + 2 <= rows[-1]:
                        store_out(n + 2)
                def square_f(n):
                    act.wait_ge(s_xu, rows[-1] + 1)
                    if n:
                        act.wait_ge(s_frs, n)
                    act.activation(junk, X[:, ROW_TILES[n][1], :], ACT.Square, accum_out=st[:, 26:27]).then_inc(s_fss, 1)

                square_f(rows[0])
                for n in rows:
                    t = ROW_TILES[n][1]
                    if n < rows[-1]:
                        square_f(n + 1)
                    act.wait_ge(s_ft, n + 1)
                    if n >= 2:
                        act.wait_ge(s_lg, n - 1)
                    for c in range(4):
                        ins = act.activation(fhT[n % 2][:, c, :], pb(2 * (n % 2))[:, P * c:P * c + P], ACT.Identity,
                                             scale=mscale[:, l, 1, kind(t), c:c + 1],
                                             bias=modcol[:, l, 24 + c, kind(t):kind(t) + 1])
                    ins.then_inc(s_fh, 1)
                    act.wait_ge(s_lm, n + 1)
                    if n >= 2:
                        act.wait_ge(s_lt, n - 1)
                    act.activation(lg[:, n % 2, :], pb(4 + n % 2)[:, 0:NE], ACT.Exp, bias=st[:, 32 + n % 2:33 + n % 2],
                                   accum_out=st[:, 34 + n % 2:35 + n % 2]).then_inc(s_le, 1)
                M = 96 if l < DEPTH - 1 else CAP_X

                def modulate_xe(e):
                    E = NE * l + e
                    if e:
                        act.wait_ge(s_xs, E)
                    for half in range(2):
                        act.wait_ge(s_et, 2 * E + half + 1)
                        for c in range(4 * half, 4 * half + 4):
                            for kd, a, b in ((1, 0, CAP_X), (0, CAP_X, M)):
                                if a < b:
                                    ins = act.activation(xeT[:, c, a:b],
                                                         pb(6 + half)[:, P * (c % 4) + a:P * (c % 4) + b], ACT.Identity,
                                                         scale=mscale[:, l, 1, kd, c:c + 1],
                                                         bias=modcol[:, l, 24 + c, kd:kd + 1])
                        ins.then_inc(s_ec, 1)

                def exp_gate(e, half):
                    E = NE * l + e
                    act.wait_ge(s_pr, 16 * E + 8 * half + 8)
                    if E:
                        act.wait_ge(s_hs, 2 * (E - 1) + half + 1)
                    act.activation(sg[0:M, half, :], pb(2 * half)[0:M, :], ACT.Exp, scale=-1.0).then_inc(s_eg, 1)

                def high_pieces(e, first, last):
                    if e == NE:
                        return
                    for q in range(first, last):
                        part, piece = q // 4, 16 * (NE * l + e) + q
                        if q % 4 == 0:
                            act.wait_ge(s_w[SLOT[part]], 16 * (NE * l + e + 1))
                        if piece >= PIECES:
                            act.wait_ge(s_pr, piece - PIECES + 1)
                        act.activation(w_hi[piece % PIECES].rearrange("p c n -> p (c n)"),
                                       unit[SLOT[part]][:, D * (q % 4):D * (q % 4) + D], ACT.Copy).then_inc(s_hi, 1)

                act.wait_ge(s_tc, 2 * (l + 1))
                high_pieces(0, 0, 4)
                modulate_xe(0)
                for e in range(NE):
                    E = NE * l + e
                    high_pieces(e, 4, 12)
                    exp_gate(e, 0)
                    if e + 1 < NE:
                        modulate_xe(e + 1)
                    high_pieces(e, 12, 16)
                    high_pieces(e + 1, 0, 3)
                    exp_gate(e, 1)
                    high_pieces(e + 1, 3, 4)
                    act.wait_ge(s_wf, 2 * E + 2)
                    if e >= 2:
                        act.wait_ge(s_sct, 16 * (E - 1))
                    for h in range(2):
                        ins = act.activation(ysc[e % 2][0:M, 512 * h:512 * h + 512], pb(4 + h)[0:M, :], ACT.Copy,
                                             scale=gT[0:M, e:e + 1])
                    ins.then_inc(s_yc, 1)
                for _ in range(2):
                    gate_rows()
                for n in rows:
                    if n:
                        act.wait_ge(s_yrs, n)
                    act.wait_ge(s_yl[n % 2], 16 * (n // 2 + 1))
                    act.activation(junk, yrow[n % 2], ACT.Square, accum_out=st[:, 28:29]).then_inc(s_yss, 1)

        @block.vector
        def _(dve):
            chain = [0]

            def link(ins):
                chain[0] += 1
                ins.then_inc(s_vch, 1)
                dve.wait_ge(s_vch, chain[0])

            dve.wait_ge(s_ach, 1)
            link(dve.tensor_scalar(crow2, crow2, 1.0, None, ALU.add))
            link(dve.reciprocal(crow2, crow2))
            dve.tensor_tensor(crow2, crow2, crow, ALU.mult).then_inc(s_cs, 1)
            dve.wait_ge(s_csT, 1)
            dve.tensor_copy(cT[:].rearrange("p c k -> p (c k)"), pb(0)[:, 0:2 * KC]).then_inc(s_cs, 1)
            dve.wait_ge(s_csT, 2)
            dve.tensor_copy(gcol[:].rearrange("p c k -> p (c k)"), pb(1)[:, 0:8 * KC]).then_inc(s_cs, 1)
            for n in range(24):
                dve.wait_ge(s_adam, n + 1)
                dve.wait_ge(s_adab[n % 4], 16 * (n // 4 + 1))
                dve.tensor_tensor(ada_row[n % 4], ada_row[n % 4], pb(2 + n % 2)[0:2, :], ALU.add).then_inc(s_adar, 1)
            dve.wait_ge(s_adat, 24)
            dve.wait_ge(s_cs, 3)
            for l in range(DEPTH):
                link(dve.tensor_copy(modcol[:, l].rearrange("p f k -> p (f k)"), pb(4 + l)[:, 0:96]))
                for s in range(2):
                    for k in range(2):
                        dve.scalar_tensor_tensor(mscale[:, l, s, k, :], modcol[:, l, 24 * s + 8:24 * s + 16, k], 1.0,
                                                 gcol[:, :, 4 * s + l], ALU.add, ALU.mult)
                        ins = dve.tensor_tensor(gate[:, l, s, k, :], modcol[:, l, 24 * s + 16:24 * s + 24, k],
                                                gcol[:, :, 4 * s + 2 + l], ALU.mult)
            ins.then_inc(s_mod, 1)
            dve.wait_ge(s_in2, 16 * (1 + 6 * DEPTH + 2))
            link(dve.tensor_scalar(nsink8[:], sink8[:], -INV_SCALE, None, ALU.mult))
            link(dve.tensor_scalar(sink8[:], sink8[:], INV_SCALE, None, ALU.mult))
            for l in range(DEPTH):
                link(dve.tensor_scalar(subgain[:, l, :], subgain[:, l, :], 1.0 - lam_init(l), None, ALU.mult))
                link(dve.tensor_tensor(lamp[:, l], lamv[:, l, 0:2, :], lamv[:, l, 2:4, :], ALU.mult))
            dve.tensor_reduce(lams[:].rearrange("p l j -> p (l j)"), lamp[:].rearrange("p l j d -> p (l j) d"), AX_X,
                              ALU.add).then_inc(s_vlam, 1)
            dve.wait_ge(s_ach, 2)
            for l in range(DEPTH):
                link(dve.tensor_tensor(nlam[:, l:l + 1], lams[:, l, 1:2], lams[:, l, 0:1], ALU.subtract))
                link(dve.tensor_scalar(nlam[:, l:l + 1], nlam[:, l:l + 1], lam_init(l), None, ALU.subtract))
            dve.wait_ge(s_const, 2)

            gate_no = [0]

            def gate_rows(l, s, k):
                q = gate_no[0]
                if q:
                    dve.wait_ge(s_gm, q)
                for c in range(KC):
                    ins = dve.tensor_scalar(diag[:, c, :], ident[:], gate[:, l, s, k, c:c + 1], None, ALU.mult)
                ins.then_inc(s_gd, 1)
                gate_no[0] += 1

            for l in range(DEPTH):
                rows = LAYER_ROWS[l]
                def normalise(n):
                    t = n - NT * l
                    dve.wait_ge(s_rs, n + 1)
                    if n:
                        dve.wait_ge(s_xt, n)
                    dve.tensor_scalar(xn, X[:, t, :], st[:, 1:2], None, ALU.mult).then_inc(s_xn, 1)

                def rotate(src, t, heads, dim):
                    off = 0 if dim == HD else 128
                    table = rope[:, t - NC, off:off + 2 * dim]
                    cos = table[:, 0:dim].unsqueeze(1).broadcast_to([P, heads, dim])
                    sin = table[:, dim:2 * dim].rearrange("p (j e) -> p e j", e=2)
                    a = tmp[1][:, 0:heads * dim].rearrange("p (h d) -> p h d", d=dim)
                    b = tmp[2][:, 0:heads * dim].rearrange("p (h j e) -> p e h j", e=2, j=dim // 2)
                    s3 = src.rearrange("p (h d) -> p h d", d=dim)
                    s4 = src.rearrange("p (h j e) -> p e h j", e=2, j=dim // 2)
                    dve.tensor_tensor(a, s3, cos, ALU.mult)
                    for e in range(2):
                        ins = dve.tensor_tensor(b[:, e], s4[:, 1 - e],
                                                sin[:, e].unsqueeze(1).broadcast_to([P, heads, dim // 2]), ALU.mult)
                    link(ins)

                def place(what, width, dst, t, src):
                    dim = HD // 2 if what[1] == "b" else HD
                    out = (Qrows if what[0] == "q" else Krows)[:, t, dst:dst + width]
                    if what[1] == "d" or t < NC:
                        return dve.tensor_copy(out, src)
                    rotate(src, t, width // dim, dim)
                    return dve.tensor_tensor(out, tmp[1][:, 0:width], tmp[2][:, 0:width], ALU.add)

                normalise(NT * l)
                for t in range(NT):
                    n = NT * l + t
                    only_kv = l == DEPTH - 1 and t < NC
                    for g in range(5):
                        G = 5 * n + g
                        if g == 2 and t + 1 < NT:
                            normalise(n + 1)
                        work = [x for x in GROUPS[g] if x[0] != "v" and not (only_kv and x[0][0] == "q")]
                        if not work:
                            continue
                        dve.wait_ge(s_raw, G + 1)
                        r = raw[G % 2]
                        if g == 0:
                            lo = 256 if only_kv else 0
                            heads = slice(lo // HD, 6)
                            nh = 6 - lo // HD
                            r3 = r[:, lo:384].rearrange("p (h d) -> p h d", d=HD)
                            n3 = tmp[0][:, lo:384].rearrange("p (h d) -> p h d", d=HD)
                            if only_kv and n == NT * l:
                                link(dve.memset(st[:, 2:8], 1.0))
                            link(dve.tensor_tensor(n3, r3, r3, ALU.mult))
                            dve.tensor_reduce(st[:, 2 + heads.start:8], n3, AX_X, ALU.add).then_inc(s_hss, 1)
                            dve.wait_ge(s_hrs, n + 1)
                            link(dve.tensor_tensor(n3, r3, st[:, 8 + heads.start:14].unsqueeze(2).broadcast_to([P, nh, HD]),
                                                   ALU.mult))
                            for j, (a, b) in enumerate(((0, 256), (256, 384))):
                                if a >= lo:
                                    v3 = tmp[0][:, a:b].rearrange("p (h d) -> p h d", d=HD)
                                    link(dve.tensor_tensor(v3, v3, qkgain[:, l, j, :].unsqueeze(1).broadcast_to(
                                        [P, (b - a) // HD, HD]), ALU.mult))
                            r = tmp[0]
                        for j, (what, col, width, dst) in enumerate(work):
                            ins = place(what, width, dst, t, r[:, col:col + width])
                            if j < len(work) - 1:
                                link(ins)
                        ins.then_inc(s_rawf, 1)
                        dve.wait_ge(s_rawf, RAW_READ[G])
                for t in range(NT):
                    n = NT * l + t
                    if n >= 2:
                        dve.wait_ge(s_kt, n - 1)
                    spans = [(b0, b1, d) for b0, b1, d in ((0, 2, HD), (2, 6, HD // 2), (6, 12, HD))]
                    for part in range(2):
                        for b0, b1, d in spans:
                            src = Krows[:, t, HD * b0:HD * b1].rearrange("p (h d) -> p h d", d=d)
                            hi, lo = (v[n % 2][:, b0:b1, :].rearrange("p b n -> p (b n)")
                                      .rearrange("p (h s d) -> p s h d", s=2, d=d) for v in (Kd, Kd_r))
                            if part == 0:
                                ins = dve.tensor_copy(lo[:, 0], src)
                            else:
                                ins = dve.tensor_tensor(lo[:, 1], src, hi[:, 0], ALU.subtract)
                        if part == 0:
                            link(ins)
                    ins.then_inc(s_kd, 1)
                dve.wait_ge(s_rpl, 16 * 8 * (l + 1))
                bias = rpbT.rearrange("p h s c -> p (h s) c")
                mask = colmask[:].unsqueeze(1).broadcast_to([P, 56, GRID_W])
                link(dve.scalar_tensor_tensor(bias, bias, INV_SCALE, mask, ALU.mult, ALU.add))
                for step in STEPS[l]:
                    u = step["entry"]
                    if u and not u["turn"]:
                        k, S = u["k"], pb(2 * (u["slot"] % 2), 2)
                        dve.wait_ge(s_sc, u["slot"] + 1)
                        if u["mixer"] == "C" and u["i"] >= 0:
                            if u["left"]:
                                link(dve.tensor_tensor(S[:, 256:384], S[:, 256:384], bandL[:], ALU.add))
                            if u["right"]:
                                e = u["nk"]
                                link(dve.tensor_tensor(S[:, e - P:e], S[:, e - P:e], bandR[:], ALU.add))
                        if u["mixer"] == "D" and u["i"] >= 0:
                            s0 = 6 - 2 * u["i"]
                            link(dve.tensor_tensor(S[:, 256:768], S[:, 256:768],
                                                   rpbT[:, u["h"], s0:s0 + 8, :].rearrange("p s c -> p (s c)"), ALU.add))
                        nm = nmx[:, k % 8:k % 8 + 1]
                        link(dve.tensor_reduce(nm, S[:, 0:u["nk"]], AX_X, ALU.max, negate=True))
                        if u["mixer"] == "C":
                            dve.tensor_scalar(nm, nm, nsink8[:, l, u["h"]:u["h"] + 1], SCALE, ALU.min, ALU.mult).then_inc(s_mx, 1)
                        else:
                            dve.tensor_scalar(nm, nm, SCALE_B if u["mixer"] == "B" else SCALE, None, ALU.mult).then_inc(s_mx, 1)
                    j = step["no"]
                    prev = STEPS[l][j - 1]["entry"] if j else None
                    if prev and not prev["turn"] and prev["mixer"] == "B" and prev["c"] == 1:
                        k = prev["k"]
                        dve.wait_ge(s_ex, prev["slot"] + 1)
                        a, b = (k - 1) % 8, k % 8
                        dve.reciprocal(rx[:, a:a + 1], sumx[:, a:a + 1])
                        link(dve.reciprocal(rx[:, b:b + 1], sumx[:, b:b + 1]))
                        link(dve.tensor_tensor(rx[:, b:b + 1], rx[:, b:b + 1], nlam[:, l:l + 1], ALU.mult))
                        p0, p1 = Pb[(k - 1) % 4][:, 0:prev["nk"]], Pb[k % 4][:, 0:prev["nk"]]
                        link(dve.tensor_scalar(p1, p1, rx[:, b:b + 1], None, ALU.mult))
                        dve.scalar_tensor_tensor(p0, p0, rx[:, a:a + 1], p1, ALU.mult, ALU.add).then_inc(s_cb, 1)
                    for v in step["turn"]:
                        if v["nk"] > 512:
                            m = v["m"]
                            dve.wait_ge(s_tn, m + 1)
                            if m >= 2:
                                dve.wait_ge(s_pv, m - 1)
                            dve.tensor_copy(PT[m % 2][:, 512:v["nk"]], pb(5)[:, 0:v["nk"] - 512]).then_inc(s_tb, 1)
                    for v in step["pv"]:
                        m, k = v["m"], v["k"]
                        dst = Ost[:, v["t"], v["ocol"]:v["ocol"] + HD]
                        if v["mixer"] == "B":
                            dve.wait_ge(s_pv, m + 1)
                            dve.tensor_copy(dst, pb(6 + m % 2)[:, 0:HD]).then_inc(s_o, 1)
                        else:
                            r = rx[:, k % 8:k % 8 + 1]
                            if v["mixer"] == "C":
                                dve.wait_ge(s_sk, SINKS[k])
                                link(dve.tensor_tensor(sumx[:, k % 8:k % 8 + 1], sumx[:, k % 8:k % 8 + 1],
                                                       skx[:, k % 8:k % 8 + 1], ALU.add))
                            link(dve.reciprocal(r, sumx[:, k % 8:k % 8 + 1]))
                            dve.wait_ge(s_pv, m + 1)
                            dve.tensor_scalar(dst, pb(6 + m % 2)[:, 0:HD], r, None, ALU.mult).then_inc(s_o, 1)
                dve.wait_ge(s_o, LAYER_VALUES[l][-1] + 1)
                dve.wait_ge(s_pv, LAYER_VALUES[l][-1] + 1)
                for k in range(2):
                    gate_rows(l, 0, k)

                def sub_norm(n):
                    t = ROW_TILES[n][1]
                    o = Ost[:, t, 256:512]
                    o3 = o.rearrange("p (h d) -> p h d", d=HD)
                    sq = upd[:, 0:256].rearrange("p (h d) -> p h d", d=HD)
                    if n >= 3:
                        dve.wait_ge(s_xu, n - 2)
                    link(dve.tensor_tensor(sq, o3, o3, ALU.mult))
                    dve.tensor_reduce(st[:, 16:20], sq, AX_X, ALU.add).then_inc(s_bss, 1)
                    dve.wait_ge(s_brs, n + 1)
                    link(dve.tensor_tensor(o3, o3, st[:, 20:24].unsqueeze(2).broadcast_to([P, 4, HD]), ALU.mult))
                    dve.tensor_tensor(o3, o3, subgain[:, l, :].unsqueeze(1).broadcast_to([P, 4, HD]), ALU.mult
                                      ).then_inc(s_on, 1)

                sub_norm(rows[0])
                sub_norm(rows[1])
                dve.wait_ge(s_gb, gate_no[0])
                for n in rows:
                    t = ROW_TILES[n][1]
                    if n + 2 <= rows[-1]:
                        sub_norm(n + 2)
                    dve.wait_ge(s_ors, n + 1)
                    link(dve.scalar_tensor_tensor(upd, pb(2 + 2 * (n % 2), 2), st[:, 25:26], GB[:, kind(t), :],
                                                  ALU.mult, ALU.mult))
                    dve.tensor_tensor(X[:, t, :], X[:, t, :], upd, ALU.add).then_inc(s_xu, 1)
                dve.wait_ge(s_xu, rows[-1] + 1)

                def normalise_f(n):
                    dve.wait_ge(s_frs, n + 1)
                    if n >= 2:
                        dve.wait_ge(s_ft, n - 1)
                        dve.wait_ge(s_fst[n % 2], 16 * (n // 2))
                    dve.tensor_scalar(fxn[n % 2], X[:, ROW_TILES[n][1], :], st[:, 27:28], None, ALU.mult).then_inc(s_fxn, 1)

                def store_aff(n):
                    t = ROW_TILES[n][1]
                    dve.wait_ge(s_lt, n + 1)
                    dve.tensor_copy(affT[:, P * t:P * t + P], pb(6 + n % 2)[0:NE, 0:P]).then_inc(s_lc, 1)

                normalise_f(rows[0])
                for n in rows:
                    t = ROW_TILES[n][1]
                    if n < rows[-1]:
                        normalise_f(n + 1)
                    dve.wait_ge(s_ft, n + 1)
                    if n >= 2:
                        dve.wait_ge(s_lg, n - 1)
                    for c in range(4, 8):
                        ins = dve.tensor_scalar(fhT[n % 2][:, c, :], pb(2 * (n % 2) + 1)[:, P * (c - 4):P * (c - 4) + P],
                                                mscale[:, l, 1, kind(t), c:c + 1], modcol[:, l, 24 + c, kind(t):kind(t) + 1],
                                                ALU.mult, ALU.add)
                    ins.then_inc(s_fv, 1)
                    dve.wait_ge(s_lg, n + 1)
                    dve.tensor_reduce(st[:, 32 + n % 2:33 + n % 2], pb(4 + n % 2)[:, 0:NE], AX_X, ALU.max, negate=True
                                      ).then_inc(s_lm, 1)
                    dve.wait_ge(s_le, n + 1)
                    link(dve.reciprocal(st[:, 36 + n % 2:37 + n % 2], st[:, 34 + n % 2:35 + n % 2]))
                    dve.tensor_scalar(lg[:, n % 2, :], lg[:, n % 2, :], st[:, 36 + n % 2:37 + n % 2], None, ALU.mult
                                      ).then_inc(s_lp, 1)
                    if n > rows[0]:
                        store_aff(n - 1)
                store_aff(rows[-1])
                dve.wait_ge(s_lc, rows[-1] + 1)
                for lo, hi, cap, col in ((CTX, CTX + SEQ, CAP_X, 0), (0, CTX, CAP_C, CAP_X)):
                    if lo == 0 and l == DEPTH - 1:
                        continue
                    src = affT[:, lo:hi]
                    for r in range(col, col + cap, 8):
                        link(dve.max(vals[:, r:r + 8], src))
                        ins = dve.max_index(idxu[:, r:r + 8], vals[:, r:r + 8], src)
                        if r + 8 < col + cap:
                            rest = aff2[:, 0:hi - lo]
                            ins = dve.match_replace(rest, vals[:, r:r + 8], src, -1.0)
                            src = rest
                        link(ins)
                    ins = dve.tensor_scalar(idxf[:, col:col + cap], idxu[:, col:col + cap], float(lo - P * first_tile(l)), None, ALU.add)
                    if lo == 0 or l == DEPTH - 1:
                        ins.then_inc(s_top, 1)
                M = 96 if l < DEPTH - 1 else CAP_X
                dve.wait_ge(s_tt, l + 1)
                dve.tensor_copy(gT[0:M, :], pb(4)[0:M, 0:NE]).then_inc(s_tc, 1)
                dve.tensor_copy(idxT[0:M, 0:NE], pb(5)[0:M, 0:NE]).then_inc(s_tc, 1)
                def low_pieces(e, first, last):
                    if e == NE:
                        return
                    for q in range(first, last):
                        part, piece = q // 4, 16 * (NE * l + e) + q
                        dve.wait_ge(s_hi, piece + 1)
                        hi, lo = (v[piece % PIECES].rearrange("p c n -> p (c n)") for v in (w_hi, w_lo))
                        dve.tensor_tensor(lo, unit[SLOT[part]][:, D * (q % 4):D * (q % 4) + D], hi.bitcast(F32),
                                          ALU.subtract).then_inc(s_lo, 1)

                def hidden(e, half):
                    E = NE * l + e
                    dve.wait_ge(s_eg, 2 * E + half + 1)
                    g = sg[0:M, half, :]
                    link(dve.tensor_scalar(g, g, 1.0, None, ALU.add))
                    link(dve.reciprocal(g, g))
                    link(dve.tensor_tensor(g, g, pb(2 * half)[0:M, :], ALU.mult))
                    if E:
                        dve.wait_ge(s_hst, 2 * (E - 1) + half + 1)
                    dve.tensor_tensor(hs[0:M, 512 * half:512 * half + 512], g, pb(2 * half + 1)[0:M, :], ALU.mult
                                      ).then_inc(s_hs, 1)

                def store_hidden(e, half):
                    E = NE * l + e
                    dve.wait_ge(s_hst, 2 * E + half + 1)
                    if E:
                        dve.wait_ge(s_wf, 2 * E)
                    dve.tensor_copy(hsT[:, 4 * half:4 * half + 4, 0:M],
                                    pb(6 + half).rearrange("p (c n) -> p c n", n=P)[:, :, 0:M]).then_inc(s_hsc, 1)

                low_pieces(0, 0, 4)
                for e in range(NE):
                    low_pieces(e, 4, 12)
                    hidden(e, 0)
                    low_pieces(e, 12, 16)
                    store_hidden(e, 0)
                    low_pieces(e + 1, 0, 3)
                    hidden(e, 1)
                    low_pieces(e + 1, 3, 4)
                    store_hidden(e, 1)
                dve.wait_ge(s_sct, 16 * NE * (l + 1))
                for k in range(2):
                    gate_rows(l, 1, k)
                dve.wait_ge(s_gb, gate_no[0])
                for n in rows:
                    t = ROW_TILES[n][1]
                    dve.wait_ge(s_yrs, n + 1)
                    if n:
                        dve.wait_ge(s_yu, n)
                    link(dve.scalar_tensor_tensor(yupd, yrow[n % 2], st[:, 29:30], GB[:, kind(t), :], ALU.mult, ALU.mult))
                    dve.tensor_tensor(X[:, t, :], X[:, t, :], yupd, ALU.add).then_inc(s_yu, 1)


_INS = ["x", "c", "ctx", "c_ctx", "w_ada", "b_ada", "g_pre_mix", "g_post_mix", "g_pre_ffn", "g_post_ffn", "w_in", "w_out",
        "q_gain_a", "k_gain_a", "lam_q1", "lam_k1", "lam_q2", "lam_k2", "subln_gain_b", "sink_c", "rpb_d", "w_router",
        "w_gate", "w_up", "w_down"]


def kernel(**inputs):
    import concourse.bacc as _bacc
    from concourse.bass_utils import run_bass_kernel_spmd as _run

    nc = _bacc.Bacc("TRN2", target_bir_lowering=False, num_devices=1)
    arrays = {"in_" + n: np.ascontiguousarray(inputs[n]) for n in _INS}
    arrays["in_rope"] = rope_table()
    aps = {n[3:]: nc.dram_tensor(n, a.shape, F32, kind="ExternalInput").ap() for n, a in arrays.items()}
    out = nc.dram_tensor("out_0", (1, SEQ, D), F32, kind="ExternalOutput").ap()

    def scratch(name, shape):
        return nc.dram_tensor(name, shape, F32, kind="Internal").ap()

    xn_dram = [scratch(f"xn_{l}", (SEQ + (CTX if l < DEPTH - 1 else 0), D)) for l in range(DEPTH)]
    y_dram = [scratch(f"y_{l}", (SEQ + (CTX if l < DEPTH - 1 else 0), D)) for l in range(DEPTH)]
    rp_dram = scratch("rp", (DEPTH, GRID_W, 60 * P))
    hybrid_dit(nc, aps, out, xn_dram, y_dram, rp_dram)
    r = _run(nc, [arrays], core_ids=[0])
    return r.results[0]["out_0"]
```

```python
from contextlib import ExitStack
import math

import numpy as np
import concourse.bass as bass
from concourse import mybir

F32 = mybir.dt.float32
F32R = mybir.dt.float32r
U32 = mybir.dt.uint32
ALU = mybir.AluOpType
ACT = mybir.ActivationFunctionType
AX_X = mybir.AxisListType.X

P = 128
D = 1024
KC = D // P
SEQ, CTX = 512, 256
NT, NC = (SEQ + CTX) // P, CTX // P
DEPTH = 2
HD = 64
GRID_W = 64
PROJ = 2560
NE = 16
CAP_X, CAP_C = 2 * SEQ // NE, 2 * CTX // NE
EPS = 1e-6
NEG = -1e30
SCALE = HD ** -0.5
SCALE_B = (HD // 2) ** -0.5
INV_SCALE = 1.0 / SCALE
KiB = 256

GROUPS = [
    [("qa", 0, 256, 0), ("ka", 256, 128, 0), ("v", 384, 128, 0)],
    [("qb", 0, 256, 256), ("kb", 256, 256, 128)],
    [("v", 0, 256, 128), ("qc", 256, 256, 512)],
    [("kc", 0, 128, 384), ("v", 128, 128, 384), ("qd", 256, 256, 768)],
    [("kd", 0, 256, 512), ("v", 256, 256, 512)],
]
KV_SPAN = [(256, 512), (256, 512), (0, 256), (0, 256), (0, 512)]


def lam_init(l):
    return 0.8 - 0.6 * math.exp(-0.3 * l)


def rope_table():
    t = np.arange(SEQ)
    parts = []
    for dim in (HD, HD // 2):
        n = dim // 4
        inv = (np.float32(10000.0) ** (-np.arange(n, dtype=np.float32) / np.float32(n))).astype(np.float32)
        rows = (t // GRID_W).astype(np.float32)
        cols = (t % GRID_W).astype(np.float32)
        ang = np.concatenate([rows[:, None] * inv, cols[:, None] * inv], axis=-1).astype(np.float32)
        cos, sin = np.cos(ang), np.sin(ang)
        parts += [np.repeat(cos, 2, axis=1), np.stack([-sin, sin], axis=-1).reshape(SEQ, dim)]
    return np.concatenate(parts, axis=1).astype(np.float32)


def attention_plan():
    entries, scores, values, steps = [], [], [], []
    turned = 0

    def turn(l, t, x):
        nonlocal turned
        entries.append(dict(turn=True, l=l, t=t, mixer="ABCD"[x], x=x, no=turned, slot=len(entries),
                            before=len(scores)))
        turned += 1
        part.append(entries[-1])

    for l in range(DEPTH):
        part = []
        tiles = range(0 if l < DEPTH - 1 else NC, NT)
        order = [(t, x) for t in tiles for x in range(4)]
        turn(l, *order[0])
        for at, (t, x) in enumerate(order):
            i = t - NC
            mixer, no = "ABCD"[x], turned - 1
            for h in range(4):
                for c in range(2 if mixer == "B" else 1):
                    u = dict(turn=False, l=l, t=t, i=i, mixer=mixer, h=h, c=c, k=len(scores), slot=len(entries),
                             q=no)
                    if i < 0:
                        u["segs"], u["vt"] = [(0, 0, 256)], [0, 1]
                    elif mixer == "C":
                        first, n = max(i - 1, 0), 3 if 0 < i < NT - NC - 1 else 2
                        u["segs"] = [(0, 0, 256), (256, CTX + P * first, 256)]
                        if n == 3:
                            u["segs"].append((512, CTX + P * (first + 2), P))
                        u["vt"] = [0, 1] + [NC + first + j for j in range(n)]
                        u["left"] = i > 0
                        u["right"] = i < NT - NC - 1
                    else:
                        u["segs"], u["vt"] = [(0, 0, 512), (512, 512, 256)], list(range(NT))
                    u["nk"] = len(u["vt"]) * P
                    u["kv"] = (0, 2, 6, 8)[x] + (h // 2 if mixer in "AC" else h)
                    u["ocol"] = 256 * x + HD * h
                    scores.append(u)
                    entries.append(u)
                    part.append(u)
                    if mixer != "B" or c == 1:
                        u["m"] = len(values)
                        values.append(u)
                    if (h, c) == (1, 0) and at + 1 < len(order):
                        turn(l, *order[at + 1])
        steps.append(part)
    wide = diffs = 0
    for v in values:
        wide += v["nk"] > 512
        v["wide"] = wide
        diffs += v["mixer"] == "B"
        v["diffs"] = diffs
    out = []
    for l, part in enumerate(steps):
        rows = [dict(entry=u, turn=[], pv=[]) for u in part] + [dict(entry=None, turn=[], pv=[]) for _ in range(4)]
        base = part[0]["slot"]
        for v in values:
            if v["l"] == l:
                lag = 3
                rows[v["slot"] - base + lag]["turn"].append(v)
                rows[v["slot"] - base + lag + 1]["pv"].append(v)
        for no, row in enumerate(rows):
            row["no"] = no
        out.append(rows)
    return entries, scores, values, out


ENTRIES, SCORES, VALUES, STEPS = attention_plan()
TURNS = [e for e in ENTRIES if e["turn"]]


def _counts():
    raw_read, done = [], 0
    for l in range(DEPTH):
        for t in range(NT):
            for g in range(5):
                reads = not (g == 2 and l == DEPTH - 1 and t < NC)
                done += reads
                raw_read.append(done if reads else 0)
    p_last = []
    for u in SCORES:
        k = u["k"] - 4
        p_last.append(0 if k < 0 else min(v["m"] for v in VALUES if v["k"] >= k) + 1)
    sinks, done = [], 0
    for u in SCORES:
        done += u["mixer"] == "C"
        sinks.append(done)
    return raw_read, p_last, sinks


RAW_READ, P_LAST, SINKS = _counts()
ADA_ORDER = [q for i in range(8) for q in (8 + 2 * i, 9 + 2 * i, i)]
ROW_TILES = [(l, t) for l in range(DEPTH) for t in range(0 if l < DEPTH - 1 else NC, NT)]
LAYER_ROWS = [[n for n, (l, _) in enumerate(ROW_TILES) if l == k] for k in range(DEPTH)]
LAYER_SCORES = [[u["k"] for u in SCORES if u["l"] == k] for k in range(DEPTH)]
LAYER_VALUES = [[v["m"] for v in VALUES if v["l"] == k] for k in range(DEPTH)]



def hybrid_dit(nc, I, out, xn_dram, y_dram, rp_dram):
    with ExitStack() as ctx:
        def sb(name, shape, dt=F32):
            return ctx.enter_context(nc.sbuf_tensor(name, shape, dt))

        def sem(name):
            return ctx.enter_context(nc.semaphore(name))

        X = sb("X", [P, NT, D])
        ident = sb("ident", [P, P])
        ones = sb("ones", [P, P])
        bandL = sb("bandL", [P, P])
        bandR = sb("bandR", [P, P])
        colmask = sb("colmask", [P, GRID_W])
        rope = sb("rope", [P, NT - NC, 192])
        modcol = sb("modcol", [P, DEPTH, 48, 2])
        gcol = sb("gcol", [P, KC, 8])
        mscale = sb("mscale", [P, DEPTH, 2, 2, KC])
        gate = sb("gate", [P, DEPTH, 2, 2, KC])
        cT = sb("cT", [P, KC, 2])
        qkgain = sb("qkgain", [P, DEPTH, 2, HD])
        subgain = sb("subgain", [P, DEPTH, HD])
        sink8 = sb("sink8", [P, DEPTH, 4])
        nsink8 = sb("nsink8", [P, DEPTH, 4])
        lamv = sb("lamv", [P, DEPTH, 4, 32])
        lamp = sb("lamp", [P, DEPTH, 2, 32])
        lams = sb("lams", [P, DEPTH, 2])
        nlam = sb("nlam", [P, DEPTH])
        halfneg = sb("halfneg", [P, 8])
        st = sb("st", [P, 64])
        wr = sb("wr", [P, KC, NE])
        arena = sb("arena", [P, 170 * KiB])

        base = nc.lookup_mloc(arena).addr

        def at(kib, shape, parts=P, rounded=None):
            n = int(np.prod(shape))
            if rounded:
                v = nc.alloc_sbuf_tensor_at(rounded, [P, n], F32R, offset=base + int(kib * 1024))[0:parts, 0:n]
            else:
                v = arena[0:parts, int(kib * KiB):int(kib * KiB) + n]
            if len(shape) > 1:
                names = "abcd"[:len(shape)]
                v = v.rearrange(f"p ({' '.join(names)}) -> p {' '.join(names)}",
                                **{x: s for x, s in zip(names[1:], shape[1:])})
            return v

        ada_ring = [at(80 + 16 * s, [KC, 512]) for s in range(3)]
        ada_row = [at(128 + 2 * s, [512], parts=2) for s in range(4)]
        crow, crow2 = at(0, [D], parts=2), at(4, [D], parts=2)
        grow = at(8, [D], parts=8)
        win = [at(16 * g, [KC, 512]) for g in range(5)]
        Qrows = at(80, [NT, D])
        Krows = at(104, [NT, 768])
        V = at(122, [NT, 768])
        xn = at(140, [D])
        hT = [at(144 + 4 * s, [KC, P]) for s in range(2)]
        raw = [at(152 + 2 * s, [512]) for s in range(2)]
        tmp = [at(156, [384]), at(158, [256]), at(159, [256])]
        ada_piece = [at(160 + 4 * s, [4, 256]) for s in range(2)]
        ada_acc = [[at(100 + 2 * s + k, [256]) for k in range(2)] for s in range(2)]
        ada_bias = at(121, [P], parts=48)
        rpbT = at(0, [4, 14, GRID_W])
        Kst = at(14, [12, NT * P], rounded="Kst")
        Qst = [at(50 + 4 * s, [2, 4, P], rounded=f"Qst{s}") for s in range(2)]
        Qd_r = [at(58 + 4 * s, [2, 512], rounded=f"Qd{s}") for s in range(2)]
        Qd = [v.bitcast(F32) for v in Qd_r]
        Kd_r = [at(66 + 6 * s, [12, P], rounded=f"Kd{s}") for s in range(2)]
        Kd = [v.bitcast(F32) for v in Kd_r]
        wout = [at(x, [D]) for x in (104, 108, 112, 116, 66, 70, 74, 0)]
        Ost = Qrows
        Pb = [at(140 + 3 * s, [768]) for s in range(4)]
        PT = [at(152 + 3 * s, [768]) for s in range(2)]
        rp = at(169.5, [P], parts=60)
        OT = [at(140 + 4 * s, [KC, P]) for s in range(2)]
        junk = at(148, [D])
        upd = at(152, [D])
        diag = [at(152, [KC, P]), at(96, [KC, P])]
        GB = [at(160, [2, D]), at(104, [2, D])]
        RING = 6
        SLOT = (1, 2, 3, 0, 4, 5)
        unit = [at(16 * s, [4096]) for s in range(RING)]
        PIECES = 4
        w_hi, w_lo = ([at(96 + 8 * s + 4 * k, [2, 512], rounded=f"w_{'hl'[k]}{s}") for s in range(PIECES)] for k in range(2))
        xe = [at(128 + 4 * s, [D], parts=96) for s in range(2)]
        xeT = at(136, [KC, 96])
        xeT_hi, xeT_lo = ([at(139 + 6 * s + 3 * k, [KC, 96], rounded=f"xeT_{'hl'[k]}{s}") for s in range(2)] for k in range(2))
        hs = at(151, [D], parts=96)
        hsT = at(155, [KC, 96])
        sg = at(158, [2, 512], parts=96)
        ysc = [at(162 + 4 * s, [D], parts=96) for s in range(2)]
        affT = at(136, [NT * P], parts=NE)
        aff_rest = {0: at(139, [CTX], parts=NE), CTX: at(164, [SEQ], parts=NE)}
        fxn = [at(128 + 4 * s, [D]) for s in range(2)]
        fhT = [at(120 + 4 * s, [KC, P]) for s in range(2)]
        yrow = [at(128 + 4 * s, [D]) for s in range(2)]
        yupd = at(136, [D])
        zero = at(119, [512])
        vals = sb("vals", [NE, 96])
        idxu = sb("idxu", [NE, 96], U32)
        idxf = sb("idxf", [NE, 96])
        gT = sb("gT", [96, NE])
        idxT = sb("idxT", [96, NE + 1], U32)
        idc = sb("idc", [96, 4], U32)
        nmx = sb("nmx", [P, 8])
        sumx = sb("sumx", [P, 8])
        skx = sb("skx", [P, 8])
        rx = sb("rx", [P, 8])
        lg = sb("lg", [P, 2, NE])

        ps = ctx.enter_context(nc.psum_tensor("ps", [P, 8, 512], F32))

        def pb(b, n=1):
            return ps[:, b:b + n, :].rearrange("p b n -> p (b n)")

        s_in = sem("s_in")
        s_in2 = sem("s_in2")
        s_x = [sem("s_x0"), sem("s_x1")]
        s_const = sem("s_const")
        s_adaw = [sem(f"s_adaw{s}") for s in range(3)]
        s_csT = sem("s_csT")
        s_cs = sem("s_cs")
        s_adam = sem("s_adam")
        s_adab = [sem(f"s_adab{s}") for s in range(4)]
        s_adar = sem("s_adar")
        s_adat = sem("s_adat")
        s_mod = sem("s_mod")
        s_aw = [sem("s_aw0"), sem("s_aw1")]
        s_ap = sem("s_ap")
        s_ar = sem("s_ar")
        s_bl = sem("s_bl")
        s_zero = sem("s_zero")
        s_win = [sem(f"s_win{g}") for g in range(5)]
        s_ss = sem("s_ss")
        s_rs = sem("s_rs")
        s_xn = sem("s_xn")
        s_xt = sem("s_xt")
        s_ht = sem("s_ht")
        s_prj = sem("s_prj")
        s_raw = sem("s_raw")
        s_rawf = sem("s_rawf")
        s_hss = sem("s_hss")
        s_hrs = sem("s_hrs")
        s_kd = sem("s_kd")
        s_kt = sem("s_kt")
        s_kc = sem("s_kc")
        s_qh = sem("s_qh")
        s_ql = sem("s_ql")
        s_rpi = sem("s_rpi")
        s_rpz = sem("s_rpz")
        s_rpw = sem("s_rpw")
        s_rpl = sem("s_rpl")
        s_wout = sem("s_wout")
        s_sc = sem("s_sc")
        s_mx = sem("s_mx")
        s_ex = sem("s_ex")
        s_sk = sem("s_sk")
        s_cb = sem("s_cb")
        s_tn = sem("s_tn")
        s_ta = sem("s_ta")
        s_tb = sem("s_tb")
        s_pv = sem("s_pv")
        s_o = sem("s_o")
        s_gd = sem("s_gd")
        s_gm = sem("s_gm")
        s_gb = sem("s_gb")
        s_bss = sem("s_bss")
        s_brs = sem("s_brs")
        s_on = sem("s_on")
        s_ot = sem("s_ot")
        s_oc = sem("s_oc")
        s_om = sem("s_om")
        s_oss = sem("s_oss")
        s_ors = sem("s_ors")
        s_xu = sem("s_xu")
        s_wr = sem("s_wr")
        s_fss = sem("s_fss")
        s_frs = sem("s_frs")
        s_fxn = sem("s_fxn")
        s_fst = [sem("s_fst0"), sem("s_fst1")]
        s_ft = sem("s_ft")
        s_fh = sem("s_fh")
        s_fv = sem("s_fv")
        s_lg = sem("s_lg")
        s_lm = sem("s_lm")
        s_le = sem("s_le")
        s_lp = sem("s_lp")
        s_lt = sem("s_lt")
        s_lc = sem("s_lc")
        s_top = sem("s_top")
        s_tt = sem("s_tt")
        s_tc = sem("s_tc")
        s_w = [sem(f"s_w{s}") for s in range(RING)]
        s_wf = sem("s_wf")
        s_hi = sem("s_hi")
        s_lo = sem("s_lo")
        s_pr = sem("s_pr")
        s_idc = sem("s_idc")
        s_g = [sem("s_g0"), sem("s_g1")]
        s_et = sem("s_et")
        s_ec = sem("s_ec")
        s_xs = sem("s_xs")
        s_eg = sem("s_eg")
        s_hs = sem("s_hs")
        s_hst = sem("s_hst")
        s_hsc = sem("s_hsc")
        s_yc = sem("s_yc")
        s_sct = sem("s_sct")
        s_z = sem("s_z")
        s_yl = [sem("s_yl0"), sem("s_yl1")]
        s_yss = sem("s_yss")
        s_yrs = sem("s_yrs")
        s_yu = sem("s_yu")
        s_out = sem("s_out")
        s_vch = sem("s_vch")
        s_vlam = sem("s_vlam")
        s_ach = sem("s_ach")
        s_pch = sem("s_pch")

        block = ctx.enter_context(nc.Block())
        n_small = [0]

        def paired(q, mixer):
            d = HD // 2 if mixer == "B" else HD
            q = q.rearrange("p (h d) -> p h d", d=d)
            return (q.unsqueeze(2).broadcast_to([P, 256 // d, 2, d]),
                    lambda v: v.rearrange("p (h r d) -> p h r d", r=2, d=d))

        def kind(t):
            return 0 if t < NC else 1

        def first_tile(l):
            return 0 if l < DEPTH - 1 else NC

        N_CLEAR = sum(NT - first_tile(l) for l in range(DEPTH))

        @block.sync
        def _(sp):
            def small(dst, src):
                sp.dma_start(dst, src).then_inc(s_in, 16)
                n_small[0] += 1

            small(crow[0:1, :], I["c_ctx"].rearrange("(a d) -> a d", a=1))
            small(crow[1:2, :], I["c"])
            for g, name in enumerate(("g_pre_mix", "g_post_mix", "g_pre_ffn", "g_post_ffn")):
                small(grow[2 * g:2 * g + 2, :], I[name])

            def ada_load(n):
                if n >= 4:
                    sp.wait_ge(s_adat, n - 3)
                sp.dma_start(ada_row[n % 4], bass.AP(I["b_ada"].tensor, 512 * n, [[0, 2], [1, 512]])
                             ).then_inc(s_adab[n % 4], 16)
                if n >= 3:
                    sp.wait_ge(s_adam, n - 2)
                sp.dma_start(ada_ring[n % 3],
                             I["w_ada"][n // 12].rearrange("(c p) n -> p c n", p=P)[:, :, 512 * (n % 12):512 * (n % 12) + 512]
                             ).then_inc(s_adaw[n % 3], 16)

            def in2(dst, src):
                sp.dma_start(dst, src).then_inc(s_in2, 16)

            for n in range(12):
                ada_load(n)
                if n == 6:
                    in2(rope[:], I["rope"].rearrange("(t p) n -> p t n", p=P))
                    for l in range(DEPTH):
                        in2(qkgain[:, l, 0, :], bass.AP(I["q_gain_a"].tensor, HD * l, [[0, P], [1, HD]]))
                        in2(qkgain[:, l, 1, :], bass.AP(I["k_gain_a"].tensor, HD * l, [[0, P], [1, HD]]))
                        for j, name in enumerate(("lam_q1", "lam_q2", "lam_k1", "lam_k2")):
                            in2(lamv[:, l, j, :], bass.AP(I[name].tensor, 32 * l, [[0, P], [1, 32]]))
                    in2(subgain[:], bass.AP(I["subln_gain_b"].tensor, 0, [[0, P], [1, DEPTH * HD]]))
                    in2(sink8[:], bass.AP(I["sink_c"].tensor, 0, [[0, P], [1, DEPTH * 4]]))
                if n == 8:
                    sp.dma_start(X[:, 0:NC, :], I["ctx"][0].rearrange("(t p) d -> p t d", p=P)).then_inc(s_x[0], 16)
            sp.wait_ge(s_cs, 3)
            for g in range(5):
                sp.dma_start(win[g],
                             I["w_in"][0].rearrange("(c p) n -> p c n", p=P)[:, :, 512 * g:512 * g + 512]
                             ).then_inc(s_win[g], 16)
            sp.dma_start(X[:, NC:NT, :], I["x"][0].rearrange("(t p) d -> p t d", p=P)).then_inc(s_x[1], 16)

            sp.wait_ge(s_adam, 12)
            sp.dma_start(ada_bias, I["b_ada"][1].rearrange("(f p) -> f p", p=P)).then_inc(s_bl, 16)
            clears = [(l, t) for l in range(DEPTH) for t in range(NT - first_tile(l))]
            wa = I["w_ada"][1].rearrange("(c p) n -> p c n", p=P)
            for n in range(48):
                if n >= 2:
                    sp.wait_ge(s_ap, n - 1)
                q, half = ADA_ORDER[n // 2], n % 2
                sp.dma_start(ada_piece[n % 2], wa[:, 4 * half:4 * half + 4, 256 * q:256 * q + 256]).then_inc(s_aw[n % 2], 16)
                if n % 4 == 3 and n // 4 < len(clears):
                    sp.wait_ge(s_zero, 1)
                    l, t = clears[n // 4]
                    sp.dma_start(y_dram[l][P * t:P * t + P, :].rearrange("p (a n) -> p a n", a=2),
                                 zero.unsqueeze(1).broadcast_to([P, 2, 512])).then_inc(s_z, 16)

            for l in range(DEPTH):
                rows = LAYER_ROWS[l]
                if l == 0:
                    sp.wait_ge(s_z, 16 * N_CLEAR)
                sp.wait_ge(s_rpz, l + 1)
                sp.dma_start(rp[:, 48:79], I["rpb_d"][l].rearrange("h r c -> (h r) c")).then_inc(s_rpi, 16)
                sp.wait_ge(s_rpi, 16 * (l + 1))
                sp.dma_start(rp_dram[l].rearrange("c (r j) -> r c j", j=P),
                             rp.unsqueeze(1).broadcast_to([60, GRID_W, P])).then_inc(s_rpw, 16)
                sp.wait_ge(s_rpw, 16 * (l + 1))
                sp.wait_ge(s_prj, 5 * NT * (l + 1))
                for up in range(2):
                    for h in range(4):
                        src = bass.AP(rp_dram.tensor, l * GRID_W * 60 * P + 63 + P * (15 * h + 1 - up),
                                      [[60 * P - 1, GRID_W], [P, 14], [1, GRID_W]])
                        sp.dma_start(rpbT[64 * up:64 * up + 64, h], src).then_inc(s_rpl, 16)
                sp.wait_ge(s_kc, NT * (l + 1))
                for c in range(7):
                    sp.dma_start(wout[c], I["w_out"][l][P * c:P * c + P, :]).then_inc(s_wout, 16)
                sp.dma_start(wr[:], I["w_router"][l].rearrange("(c p) n -> p c n", p=P)).then_inc(s_wr, 16)

                wg = I["w_gate"][l].rearrange("e (c p) f -> e p c f", p=P)
                wu = I["w_up"][l].rearrange("e (c p) f -> e p c f", p=P)
                wd = I["w_down"][l].rearrange("e (c p) n -> e p c n", p=P)

                def load_unit(e, part, slot):
                    if part < 4:
                        src = (wg, wu)[part % 2][e, :, :, 512 * (part // 2):512 * (part // 2) + 512]
                        dst = unit[slot].rearrange("p (c n) -> p c n", n=512)
                    else:
                        src = wd[e, :, 4 * (part - 4):4 * (part - 4) + 4, :]
                        dst = unit[slot].rearrange("p (c n) -> p c n", n=D)
                    sp.dma_start(dst, src).then_inc(s_w[slot], 16)

                sp.wait_ge(s_pv, LAYER_VALUES[l][-1] + 1)
                sp.dma_start(wout[7], I["w_out"][l][7 * P:D, :]).then_inc(s_wout, 16)
                for n in range(3):
                    load_unit(0, n, SLOT[n % RING])
                for n in rows:
                    if n == rows[-1]:
                        sp.wait_ge(s_om, n + 1)
                        for m in range(3, RING):
                            load_unit(0, m, SLOT[m])
                    t = ROW_TILES[n][1] - first_tile(l)
                    sp.wait_ge(s_fxn, n + 1)
                    sp.dma_start(xn_dram[l][P * t:P * t + P, :], fxn[n % 2]).then_inc(s_fst[n % 2], 16)
                for e in range(NE):
                    E = NE * l + e
                    for part in (0, 1, 5, 2, 3, 4):
                        if part == 5:
                            if e > 0:
                                sp.wait_ge(s_wf, 2 * E)
                                load_unit(e, 5, SLOT[5])
                            continue
                        if part < 4:
                            sp.wait_ge(s_lo, 16 * E + 4 * part + 4)
                        else:
                            sp.wait_ge(s_wf, 2 * E + 1)
                        if e + 1 < NE:
                            load_unit(e + 1, part, SLOT[part])
                        elif l + 1 < DEPTH:
                            g = SLOT[part]
                            sp.dma_start(win[g], I["w_in"][l + 1].rearrange("(c p) n -> p c n", p=P)[:, :, 512 * g:512 * g + 512]
                                         ).then_inc(s_win[g], 16)
                sp.wait_ge(s_sct, 16 * NE * (l + 1))
                for n in rows:
                    t = ROW_TILES[n][1] - first_tile(l)
                    if n >= 2:
                        sp.wait_ge(s_yu, n - 1)
                    sp.dma_start(yrow[n % 2], y_dram[l][P * t:P * t + P, :]).then_inc(s_yl[n % 2], 16)
            for j, n in enumerate(LAYER_ROWS[DEPTH - 1]):
                sp.wait_ge(s_yu, n + 1)
                sp.dma_start(out[0, P * j:P * j + P, :], X[:, NC + j, :]).then_inc(s_out, 16)
            sp.wait_ge(s_out, 16 * (NT - NC))

        @block.gpsimd
        def _(pool):
            chain = [0]

            def link(ins):
                chain[0] += 1
                ins.then_inc(s_pch, 1)
                pool.wait_ge(s_pch, chain[0])

            link(pool.memset(ident[:], 0.0))
            link(pool.memset(ones[:], 1.0))
            link(pool.memset(halfneg[:], -0.5))
            pool.affine_select(out=ident[:], in_=ident[:], compare_op=ALU.not_equal, fill=1.0, base=0,
                               pattern=[[-1, P]], channel_multiplier=1).then_inc(s_const, 1)
            link(pool.memset(colmask[:], 0.0))
            for half in range(2):
                m = colmask[64 * half:64 * half + 64, :]
                link(pool.affine_select(out=m[:, 0:48], in_=m[:, 0:48], compare_op=ALU.is_ge, fill=NEG * INV_SCALE,
                                        base=8, pattern=[[1, 48]], channel_multiplier=-1))
                link(pool.affine_select(out=m[:, 16:64], in_=m[:, 16:64], compare_op=ALU.is_ge, fill=NEG * INV_SCALE,
                                        base=7 - 16, pattern=[[-1, 48]], channel_multiplier=1))
            link(pool.memset(bandL[:], 0.0))
            link(pool.memset(bandR[:], 0.0))
            link(pool.memset(idxT[:], 0))
            link(pool.affine_select(out=bandL[:], in_=bandL[:], compare_op=ALU.is_ge, fill=NEG, base=0,
                                    pattern=[[1, P]], channel_multiplier=-1))
            pool.affine_select(out=bandR[:], in_=bandR[:], compare_op=ALU.is_ge, fill=NEG, base=0,
                               pattern=[[-1, P]], channel_multiplier=1).then_inc(s_const, 1)

            def inverse_root(dst, src, width, n_el, wait, done, value):
                pool.wait_ge(wait, value)
                link(pool.tensor_scalar(dst, src, 1.0 / width, EPS, ALU.mult, ALU.add))
                pool.tensor_tensor(dst, dst, halfneg[:, 0:n_el], ALU.pow).then_inc(done, 1)

            for l in range(DEPTH):
                rows = LAYER_ROWS[l]
                if l > 0:
                    pool.wait_ge(s_yu, LAYER_ROWS[l - 1][-1] + 1)
                pool.memset(rp, 0.0).then_inc(s_rpz, 1)
                inverse_root(st[:, 1:2], st[:, 0:1], D, 1, s_ss, s_rs, NT * l + 1)
                if l == 0:
                    pool.wait_ge(s_adam, 12)
                    pool.memset(zero, 0.0).then_inc(s_zero, 1)
                for t in range(NT):
                    n = NT * l + t
                    inverse_root(st[:, 8:14], st[:, 2:8], HD, 6, s_hss, s_hrs, n + 1)
                    if t + 1 < NT:
                        pool.wait_ge(s_xn, n + 1)
                        inverse_root(st[:, 1:2], st[:, 0:1], D, 1, s_ss, s_rs, n + 2)
                for e in TURNS:
                    if e["l"] != l:
                        continue
                    pool.wait_ge(s_qh, e["no"] + 1)
                    q, dup = paired(Qrows[:, e["t"], 256 * e["x"]:256 * e["x"] + 256], e["mixer"])
                    pool.tensor_tensor(dup(Qd_r[e["no"] % 2][:, 1]), q, dup(Qd[e["no"] % 2][:, 0]), ALU.subtract
                                       ).then_inc(s_ql, 1)
                inverse_root(st[:, 20:24], st[:, 16:20], HD, 4, s_bss, s_brs, rows[0] + 1)
                pool.wait_ge(s_on, rows[0] + 1)
                inverse_root(st[:, 20:24], st[:, 16:20], HD, 4, s_bss, s_brs, rows[0] + 2)
                for n in range(rows[0], rows[-1] + 2):
                    if n > rows[0]:
                        if n > 1:
                            pool.wait_ge(s_xu, n - 1)
                        inverse_root(st[:, 25:26], st[:, 24:25], D, 1, s_oss, s_ors, n)
                        if n > 1:
                            pool.wait_ge(s_fxn, n - 1)
                        inverse_root(st[:, 27:28], st[:, 26:27], D, 1, s_fss, s_frs, n)
                    if n + 2 <= rows[-1]:
                        pool.wait_ge(s_on, n + 2)
                        inverse_root(st[:, 20:24], st[:, 16:20], HD, 4, s_bss, s_brs, n + 3)
                M = 96 if l < DEPTH - 1 else CAP_X
                pool.wait_ge(s_tc, 2 * (l + 1))
                pool.wait_ge(s_fst[0], 16 * (rows[-1] // 2 + 1))
                pool.wait_ge(s_fst[1], 16 * ((rows[-1] + 1) // 2))

                def gather(e):
                    E = NE * l + e
                    pool.tensor_copy(idc[0:M, e % 4:e % 4 + 1], idxT[0:M, e:e + 1]).then_inc(s_idc, 1)
                    pool.wait_ge(s_idc, E + 1)
                    if e >= 2:
                        pool.wait_ge(s_et, 2 * (E - 1))
                    pool.indirect_dma_start(out=xe[e % 2][0:M], out_offset=None, in_=xn_dram[l],
                                            in_offset=bass.IndirectOffsetOnAxis(idc[0:M, e % 4:e % 4 + 1], 0)
                                            ).then_inc(s_g[e % 2], 16)

                def split_xe(e):
                    E = NE * l + e
                    pool.wait_ge(s_ec, 2 * E + 2)
                    if e >= 2:
                        pool.wait_ge(s_pr, 16 * (E - 1))
                    full, hi, lo = xeT[:, :, 0:M], xeT_hi[e % 2][:, :, 0:M], xeT_lo[e % 2][:, :, 0:M]
                    link(pool.tensor_copy(hi, full))
                    pool.tensor_tensor(lo, full, hi.bitcast(F32), ALU.subtract).then_inc(s_xs, 1)

                gather(0)
                gather(1)
                split_xe(0)
                for e in range(NE):
                    E = NE * l + e
                    if e + 2 < NE:
                        gather(e + 2)
                    if e + 1 < NE:
                        split_xe(e + 1)
                    pool.wait_ge(s_yc, E + 1)
                    if e:
                        pool.wait_ge(s_sct, 16 * E)
                    elif l == 0:
                        pool.wait_ge(s_z, 16 * N_CLEAR)
                    pool.indirect_dma_start(out=y_dram[l],
                                            out_offset=bass.IndirectOffsetOnAxis(idc[0:M, e % 4:e % 4 + 1], 0),
                                            in_=ysc[e % 2][0:M], in_offset=None, compute_op=ALU.add).then_inc(s_sct, 16)
                for n in rows:
                    if n > 0:
                        pool.wait_ge(s_yu, n)
                    inverse_root(st[:, 29:30], st[:, 28:29], D, 1, s_yss, s_yrs, n + 1)

        @block.tensor
        def _(pe):
            pe.wait_ge(s_const, 1)
            pe.wait_ge(s_cs, 1)
            for c in range(KC):
                mm = pe.transpose(pb(0)[:, 2 * c:2 * c + 2], crow2[:, P * c:P * c + P], ident[0:2, 0:2])
            mm.then_inc(s_csT, 1)
            for c in range(KC):
                mm = pe.transpose(pb(1)[:, 8 * c:8 * c + 8], grow[:, P * c:P * c + P], ident[0:8, 0:8])
            mm.then_inc(s_csT, 1)
            pe.wait_ge(s_cs, 2)

            def turn_piece(n):
                l, q = n // 12, n % 12
                pe.wait_ge(s_adar, n + 1)
                for j in range(4):
                    mm = pe.transpose(pb(4 + l)[:, 2 * (4 * q + j):2 * (4 * q + j) + 2],
                                      ada_row[n % 4][:, P * j:P * j + P], ident[0:2, 0:2])
                mm.then_inc(s_adat, 1)

            def turn_rows(n):
                pe.wait_ge(s_xn, n + 1)
                if n:
                    pe.wait_ge(s_ht, n)
                for c in range(KC):
                    mm = pe.transpose(pb(c // 4)[:, P * (c % 4):P * (c % 4) + P], xn[:, P * c:P * c + P], ident[:])
                mm.then_inc(s_xt, 1)

            for n in range(12):
                pe.wait_ge(s_adaw[n % 3], 16 * (n // 3 + 1))
                if n >= 2:
                    pe.wait_ge(s_adar, n - 1)
                for c in range(KC):
                    mm = pe.matmul(pb(2 + n % 2)[0:2, :], cT[:, c, :], ada_ring[n % 3][:, c, :],
                                   start=(c == 0), stop=(c == KC - 1))
                mm.then_inc(s_adam, 1)
                if n:
                    turn_piece(n - 1)
            pe.wait_ge(s_cs, 3)
            turn_rows(0)
            turn_piece(11)
            pe.wait_ge(s_mod, 1)

            def sum_ada(no):
                q = ADA_ORDER[no]
                if no == 23:
                    pe.wait_ge(s_bl, 16)
                    pe.transpose(pb(7)[:, 0:48], ada_bias, ident[0:48, 0:48])
                pe.wait_ge(s_ap, 2 * no + 2)
                for j in range(2):
                    col = 2 * (2 * q + j)
                    if q < 8:
                        for k in range(2):
                            mm = pe.matmul(pb(6)[:, col + k:col + k + 1], ada_acc[no % 2][k][:, P * j:P * j + P],
                                           ones[:, 0:1], start=True, stop=True)
                    else:
                        for k in range(2):
                            mm = pe.matmul(pb(6)[:, col + 1:col + 2], ada_acc[no % 2][k][:, P * j:P * j + P],
                                           ones[:, 0:1], start=(k == 0), stop=(k == 1))
                mm.then_inc(s_ar, 1)

            gate_no = [0]

            def gate_rows(s, banks):
                q = gate_no[0]
                pe.wait_ge(s_gd, q + 1)
                if q:
                    pe.wait_ge(s_gb, q)
                for h in range(2):
                    mm = pe.matmul(pb(banks[h]), ones[:], diag[s][:, 4 * h:4 * h + 4, :].rearrange("p c n -> p (c n)"),
                                   start=True, stop=True)
                mm.then_inc(s_gm, 1)
                gate_no[0] += 1

            for l in range(DEPTH):
                def only_kv(t):
                    return l == DEPTH - 1 and t < NC

                if l:
                    turn_rows(NT * l)
                for t in range(NT):
                    n = NT * l + t
                    pe.wait_ge(s_ht, n + 1)
                    for g in range(5):
                        G = 5 * n + g
                        lo, hi = KV_SPAN[g] if only_kv(t) else (0, 512)
                        if t == 0:
                            pe.wait_ge(s_win[g], 16 * (l + 1))
                        if G >= 2:
                            pe.wait_ge(s_raw, G - 1)
                        for c in range(KC):
                            mm = pe.matmul(pb(2 + G % 2)[:, lo:hi], hT[n % 2][:, c, :],
                                           win[g][:, c, lo:hi], start=(c == 0), stop=(c == KC - 1))
                        mm.then_inc(s_prj, 1)
                        if l == 0 and 1 <= G <= 24:
                            sum_ada(G - 1)
                        if g == 2 and t + 1 < NT:
                            turn_rows(n + 1)
                for t in range(NT):
                    n = NT * l + t
                    pe.wait_ge(s_kd, n + 1)
                    if n >= 2:
                        pe.wait_ge(s_kc, n - 1)
                    for b in range(12):
                        mm = pe.transpose(pb(4 * (n % 2) + b // 4)[:, P * (b % 4):P * (b % 4) + P], Kd[n % 2][:, b, :], ident[:])
                    mm.then_inc(s_kt, 1)
                    if t in (2, 4):
                        gate_rows(0, (3, 7))
                pe.wait_ge(s_kc, NT * (l + 1))
                for step in STEPS[l]:
                    u = step["entry"]
                    if u:
                        S = pb(2 * (u["slot"] % 2), 2)
                        if u["slot"] >= 2:
                            pe.wait_ge(s_ex, u["slot"] - 1)
                    if u and u["turn"]:
                        pe.wait_ge(s_ql, u["no"] + 1)
                        for b in range(8):
                            mm = pe.transpose(S[:, P * b:P * b + P], Qd[u["no"] % 2][:, b // 4, P * (b % 4):P * (b % 4) + P],
                                              ident[:])
                        mm.then_inc(s_sc, 1)
                    elif u:
                        r0, r1 = (HD * u["c"], HD * u["c"] + HD) if u["mixer"] == "B" else (0, P)
                        pe.wait_ge(s_ex, TURNS[u["q"]]["slot"] + 1)
                        for col, src, width in u["segs"]:
                            for part in range(2):
                                mm = pe.matmul(S[:, col:col + width], Qst[u["q"] % 2][r0:r1, part, u["h"], :],
                                               Kst[r0:r1, u["kv"], src:src + width], start=(part == 0), stop=(part == 1))
                        mm.then_inc(s_sc, 1)
                    for v in step["turn"]:
                        m, k = v["m"], v["k"]
                        if v["mixer"] == "B":
                            pe.wait_ge(s_cb, v["diffs"])
                        else:
                            pe.wait_ge(s_ex, v["slot"] + 1)
                        if m:
                            pe.wait_ge(s_ta, m)
                            pe.wait_ge(s_tb, v["wide"] - (v["nk"] > 512))
                        src = Pb[(k - 1) % 4] if v["mixer"] == "B" else Pb[k % 4]
                        for j in range(v["nk"] // P):
                            mm = pe.transpose(pb(4 + j // 4)[:, P * (j % 4):P * (j % 4) + P], src[:, P * j:P * j + P], ident[:])
                        mm.then_inc(s_tn, 1)
                    for v in step["pv"]:
                        m = v["m"]
                        pe.wait_ge(s_ta, m + 1)
                        pe.wait_ge(s_tb, v["wide"])
                        if m >= 2:
                            pe.wait_ge(s_o, m - 1)
                        for j, vt in enumerate(v["vt"]):
                            mm = pe.matmul(pb(6 + m % 2)[:, 0:HD], PT[m % 2][:, P * j:P * j + P],
                                           V[:, vt, HD * v["kv"]:HD * v["kv"] + HD], start=(j == 0), stop=(j == len(v["vt"]) - 1))
                        mm.then_inc(s_pv, 1)
                rows = LAYER_ROWS[l]
                pe.wait_ge(s_o, LAYER_VALUES[l][-1] + 1)

                def turn_out(n):
                    t = ROW_TILES[n][1]
                    pe.wait_ge(s_on, n + 1)
                    if n:
                        pe.wait_ge(s_oc, n)
                    for c in range(KC):
                        mm = pe.transpose(pb(c // 4)[:, P * (c % 4):P * (c % 4) + P], Ost[:, t, P * c:P * c + P], ident[:])
                    mm.then_inc(s_ot, 1)

                def turn_f(n):
                    pe.wait_ge(s_fxn, n + 1)
                    if n:
                        pe.wait_ge(s_lc, n)
                    for c in range(KC):
                        mm = pe.transpose(pb(6 + c // 4)[:, P * (c % 4):P * (c % 4) + P],
                                          fxn[n % 2][:, P * c:P * c + P], ident[:])
                    mm.then_inc(s_ft, 1)

                def logits(n):
                    pe.wait_ge(s_fh, n + 1)
                    pe.wait_ge(s_fv, n + 1)
                    for c in range(KC):
                        mm = pe.matmul(pb(6)[:, 0:NE], fhT[n % 2][:, c, :], wr[:, c, :],
                                       start=(c == 0), stop=(c == KC - 1))
                    mm.then_inc(s_lg, 1)

                def turn_aff(n):
                    pe.wait_ge(s_lp, n + 1)
                    pe.transpose(pb(7)[0:NE, 0:P], lg[:, n % 2, :], ident[:]).then_inc(s_lt, 1)

                def project(n, h):
                    if n >= 2:
                        pe.wait_ge(s_xu, n - 1)
                    pe.wait_ge(s_oc, n + 1)
                    for c in range(KC):
                        mm = pe.matmul(pb(2 + 2 * (n % 2) + h), OT[n % 2][:, c, :], wout[c][:, 512 * h:512 * h + 512],
                                       start=(c == 0), stop=(c == KC - 1))
                    if h == 1:
                        mm.then_inc(s_om, 1)

                turn_out(rows[0])
                turn_out(rows[1])
                pe.wait_ge(s_wout, 16 * KC * (l + 1))
                pe.wait_ge(s_wr, 16 * (l + 1))
                for n in range(rows[0], rows[-1] + 3):
                    if n <= rows[-1]:
                        project(n, 0)
                    if n - 2 >= rows[0]:
                        logits(n - 2)
                    if n <= rows[-1]:
                        project(n, 1)
                    if n - 2 >= rows[0]:
                        turn_aff(n - 2)
                    if n + 2 <= rows[-1]:
                        turn_out(n + 2)
                    if rows[0] <= n - 1 <= rows[-1]:
                        turn_f(n - 1)
                M = 96 if l < DEPTH - 1 else CAP_X
                pe.wait_ge(s_top, l + 1)
                pe.transpose(pb(4)[0:M, 0:NE], vals[:, 0:M], ident[0:NE, 0:NE])
                pe.transpose(pb(5)[0:M, 0:NE], idxf[:, 0:M], ident[0:NE, 0:NE]).then_inc(s_tt, 1)
                pe.wait_ge(s_tc, 2 * (l + 1))

                def turn_xe(e):
                    E = NE * l + e
                    pe.wait_ge(s_g[e % 2], 16 * (E // 2 + 1))
                    for half in range(2):
                        free = 2 * E if e == 0 else 2 * E - 3 + half
                        if free > 0:
                            pe.wait_ge(s_hsc, free)
                        for c in range(4 * half, 4 * half + 4):
                            mm = pe.transpose(pb(6 + half)[:, P * (c % 4):P * (c % 4) + M], xe[e % 2][0:M, P * c:P * c + P],
                                              ident[0:M, 0:M])
                        mm.then_inc(s_et, 1)

                def gate_up(e, half, part):
                    E = NE * l + e
                    if E:
                        pe.wait_ge(s_hs, 2 * (E - 1) + half + 1)
                    out = pb(2 * half + part)[0:M, :]
                    for q in range(4):
                        piece = 16 * E + 4 * (2 * half + part) + q
                        pe.wait_ge(s_lo, piece + 1)
                        for j in range(2):
                            c = 2 * q + j
                            hi, lo = xeT_hi[e % 2][:, c, 0:M], xeT_lo[e % 2][:, c, 0:M]
                            wh, wl = w_hi[piece % PIECES][:, j, :], w_lo[piece % PIECES][:, j, :]
                            pe.matmul(out, hi, wh, start=(c == 0), stop=False)
                            pe.matmul(out, hi, wl, start=False, stop=False)
                            mm = pe.matmul(out, lo, wh, start=False, stop=(c == KC - 1))
                        mm.then_inc(s_pr, 1)

                def turn_hs(e, half):
                    E = NE * l + e
                    pe.wait_ge(s_hs, 2 * E + half + 1)
                    if e + 1 < NE:
                        pe.wait_ge(s_ec, 2 * (E + 1) + half + 1)
                    for c in range(4 * half, 4 * half + 4):
                        mm = pe.transpose(pb(6 + half)[:, P * (c % 4):P * (c % 4) + M], hs[0:M, P * c:P * c + P],
                                          ident[0:M, 0:M])
                    mm.then_inc(s_hst, 1)

                def down(e, half):
                    E = NE * l + e
                    pe.wait_ge(s_w[SLOT[4 + half]], 16 * (E + 1))
                    w = unit[SLOT[4 + half]].rearrange("p (c n) -> p c n", n=D)
                    pe.wait_ge(s_hsc, 2 * E + half + 1)
                    if half == 0 and E:
                        pe.wait_ge(s_yc, E)
                    for c in range(4):
                        for h in range(2):
                            mm = pe.matmul(pb(4 + h)[0:M, :], hsT[:, 4 * half + c, 0:M], w[:, c, 512 * h:512 * h + 512],
                                           start=(half == 0 and c == 0), stop=(half == 1 and c == 3))
                    mm.then_inc(s_wf, 1)

                turn_xe(0)
                for e in range(NE):
                    pe.wait_ge(s_xs, NE * l + e + 1)
                    gate_up(e, 0, 0)
                    if e:
                        turn_hs(e - 1, 1)
                    gate_up(e, 0, 1)
                    if e:
                        down(e - 1, 1)
                    if e + 1 < NE:
                        turn_xe(e + 1)
                    gate_up(e, 1, 0)
                    turn_hs(e, 0)
                    gate_up(e, 1, 1)
                    down(e, 0)
                turn_hs(NE - 1, 1)
                down(NE - 1, 1)
                pe.wait_ge(s_hsc, 2 * NE * (l + 1))
                for _ in range(2):
                    gate_rows(1, (6, 7))
                pe.wait_ge(s_gb, gate_no[0])

        @block.scalar
        def _(act):
            act.wait_ge(s_in, 16 * n_small[0])
            act.activation(crow2, crow, ACT.Exp, scale=-1.0).then_inc(s_ach, 1)
            gate_no = [0]

            def gate_rows(s, banks):
                q = gate_no[0]
                act.wait_ge(s_gm, q + 1)
                for h in range(2):
                    ins = act.activation(GB[s][:, q % 2, 512 * h:512 * h + 512], pb(banks[h]), ACT.Copy)
                ins.then_inc(s_gb, 1)
                gate_no[0] += 1

            for l in range(DEPTH):
                rows = LAYER_ROWS[l]
                def square_rows(n):
                    t = n - NT * l
                    if n == NC:
                        act.wait_ge(s_x[1], 16)
                    if n:
                        act.wait_ge(s_rs, n)
                        act.wait_ge(s_xt, n)
                    act.activation(xn, X[:, t, :], ACT.Square, accum_out=st[:, 0:1]).then_inc(s_ss, 1)

                def modulate(n):
                    t = n - NT * l
                    act.wait_ge(s_xt, n + 1)
                    for c in range(KC):
                        ins = act.activation(hT[n % 2][:, c, :], pb(c // 4)[:, P * (c % 4):P * (c % 4) + P], ACT.Identity,
                                             scale=mscale[:, l, 0, kind(t), c:c + 1], bias=modcol[:, l, c, kind(t):kind(t) + 1])
                    ins.then_inc(s_ht, 1)

                if l == 0:
                    act.wait_ge(s_x[0], 16)
                else:
                    act.wait_ge(s_yu, LAYER_ROWS[l - 1][-1] + 1)
                square_rows(NT * l)
                act.wait_ge(s_mod, l + 1)
                modulate(NT * l)
                for t in range(NT):
                    n = NT * l + t
                    only_kv = l == DEPTH - 1 and t < NC
                    for g in range(5):
                        G = 5 * n + g
                        act.wait_ge(s_prj, G + 1)
                        if RAW_READ[G - 2] if G >= 2 else 0:
                            act.wait_ge(s_rawf, RAW_READ[G - 2])
                        for what, col, width, dst in GROUPS[g]:
                            if only_kv and what[0] == "q":
                                continue
                            src = pb(2 + G % 2)[:, col:col + width]
                            if what == "v":
                                ins = act.activation(V[:, t, dst:dst + width], src, ACT.Copy)
                            else:
                                ins = act.activation(raw[G % 2][:, col:col + width], src, ACT.Copy)
                        ins.then_inc(s_raw, 1)
                        if g == 1 and t + 1 < NT:
                            square_rows(n + 1)
                        if g == 2 and t + 1 < NT:
                            modulate(n + 1)
                        if G == 0:
                            act.wait_ge(s_vlam, 1)
                            act.activation(lams[:], lams[:], ACT.Exp).then_inc(s_ach, 1)
                def high_parts(no):
                    e = TURNS[no]
                    q, dup = paired(Qrows[:, e["t"], 256 * e["x"]:256 * e["x"] + 256], e["mixer"])
                    if no >= 2:
                        act.wait_ge(s_sc, TURNS[no - 2]["slot"] + 1)
                    act.activation(dup(Qd_r[no % 2][:, 0]), q, ACT.Copy).then_inc(s_qh, 1)

                first = [e["no"] for e in TURNS if e["l"] == l]
                act.wait_ge(s_rawf, RAW_READ[5 * NT * (l + 1) - 1])
                high_parts(first[0])
                high_parts(first[1])
                for t in range(NT):
                    n = NT * l + t
                    act.wait_ge(s_kt, n + 1)
                    act.activation(Kst[:, :, P * t:P * t + P], pb(4 * (n % 2), 3).rearrange("p (b n) -> p b n", n=P),
                                   ACT.Copy).then_inc(s_kc, 1)
                    if t in (2, 4):
                        gate_rows(0, (3, 7))
                for step in STEPS[l]:
                    for v in step["turn"]:
                        m = v["m"]
                        act.wait_ge(s_tn, m + 1)
                        if m >= 2:
                            act.wait_ge(s_pv, m - 1)
                        w = min(v["nk"], 512)
                        act.activation(PT[m % 2][:, 0:w], pb(4)[:, 0:w], ACT.Copy).then_inc(s_ta, 1)
                    u = step["entry"]
                    if u and u["turn"]:
                        act.wait_ge(s_sc, u["slot"] + 1)
                        act.activation(Qst[u["no"] % 2].rearrange("p s h n -> p (s h n)"), pb(2 * (u["slot"] % 2), 2),
                                       ACT.Copy).then_inc(s_ex, 1)
                        if u["no"] + 2 <= first[-1]:
                            high_parts(u["no"] + 2)
                    elif u:
                        k = u["k"]
                        act.wait_ge(s_mx, k + 1)
                        last = P_LAST[k]
                        if last:
                            act.wait_ge(s_tn, last)
                        act.activation(Pb[k % 4][:, 0:u["nk"]], pb(2 * (u["slot"] % 2), 2)[:, 0:u["nk"]], ACT.Exp,
                                       bias=nmx[:, k % 8:k % 8 + 1], scale=SCALE_B if u["mixer"] == "B" else SCALE,
                                       accum_out=sumx[:, k % 8:k % 8 + 1]).then_inc(s_ex, 1)
                        if u["mixer"] == "C":
                            act.activation(skx[:, k % 8:k % 8 + 1], sink8[:, l, u["h"]:u["h"] + 1], ACT.Exp,
                                           bias=nmx[:, k % 8:k % 8 + 1], scale=SCALE).then_inc(s_sk, 1)

                def store_out(n):
                    act.wait_ge(s_ot, n + 1)
                    if n >= 2:
                        act.wait_ge(s_om, n - 1)
                    act.activation(OT[n % 2].rearrange("p c n -> p (c n)"), pb(0, 2), ACT.Copy).then_inc(s_oc, 1)

                def square_out(n):
                    act.wait_ge(s_om, n + 1)
                    if n:
                        act.wait_ge(s_ors, n)
                        act.wait_ge(s_fss, n)
                    act.activation(junk, pb(2 + 2 * (n % 2), 2), ACT.Square, accum_out=st[:, 24:25]).then_inc(s_oss, 1)

                def store_f(n):
                    t = ROW_TILES[n][1]
                    act.wait_ge(s_ft, n + 1)
                    if n >= 2:
                        act.wait_ge(s_lg, n - 1)
                    for c in range(4):
                        ins = act.activation(fhT[n % 2][:, c, :], pb(6)[:, P * c:P * c + P], ACT.Identity,
                                             scale=mscale[:, l, 1, kind(t), c:c + 1],
                                             bias=modcol[:, l, 24 + c, kind(t):kind(t) + 1])
                    ins.then_inc(s_fh, 1)

                def square_f(n):
                    act.wait_ge(s_xu, n + 1)
                    if n:
                        act.wait_ge(s_frs, n)
                    act.activation(junk, X[:, ROW_TILES[n][1], :], ACT.Square, accum_out=st[:, 26:27]).then_inc(s_fss, 1)

                def exp_logits(n):
                    act.wait_ge(s_lm, n + 1)
                    if n >= 2:
                        act.wait_ge(s_lt, n - 1)
                    act.activation(lg[:, n % 2, :], pb(6)[:, 0:NE], ACT.Exp, bias=st[:, 32 + n % 2:33 + n % 2],
                                   accum_out=st[:, 34 + n % 2:35 + n % 2]).then_inc(s_le, 1)

                store_out(rows[0])
                store_out(rows[1])
                for n in range(rows[0], rows[-1] + 3):
                    if rows[0] <= n - 1 <= rows[-1]:
                        square_out(n - 1)
                        if n + 1 >= rows[2] and n + 1 <= rows[-1]:
                            store_out(n + 1)
                    if n - 2 >= rows[0]:
                        store_f(n - 2)
                    if rows[0] <= n - 1 <= rows[-1]:
                        square_f(n - 1)
                    if n - 2 >= rows[0]:
                        exp_logits(n - 2)
                M = 96 if l < DEPTH - 1 else CAP_X

                def modulate_xe(e):
                    E = NE * l + e
                    if e:
                        act.wait_ge(s_xs, E)
                    for half in range(2):
                        act.wait_ge(s_et, 2 * E + half + 1)
                        for c in range(4 * half, 4 * half + 4):
                            for kd, a, b in ((1, 0, CAP_X), (0, CAP_X, M)):
                                if a < b:
                                    ins = act.activation(xeT[:, c, a:b],
                                                         pb(6 + half)[:, P * (c % 4) + a:P * (c % 4) + b], ACT.Identity,
                                                         scale=mscale[:, l, 1, kd, c:c + 1],
                                                         bias=modcol[:, l, 24 + c, kd:kd + 1])
                        ins.then_inc(s_ec, 1)

                def exp_gate(e, half):
                    E = NE * l + e
                    act.wait_ge(s_pr, 16 * E + 8 * half + 8)
                    if E:
                        act.wait_ge(s_hs, 2 * (E - 1) + half + 1)
                    act.activation(sg[0:M, half, :], pb(2 * half)[0:M, :], ACT.Exp, scale=-1.0).then_inc(s_eg, 1)

                def high_pieces(e, first, last):
                    if e == NE:
                        return
                    for q in range(first, last):
                        part, piece = q // 4, 16 * (NE * l + e) + q
                        if q % 4 == 0:
                            act.wait_ge(s_w[SLOT[part]], 16 * (NE * l + e + 1))
                        if piece >= PIECES:
                            act.wait_ge(s_pr, piece - PIECES + 1)
                        act.activation(w_hi[piece % PIECES].rearrange("p c n -> p (c n)"),
                                       unit[SLOT[part]][:, D * (q % 4):D * (q % 4) + D], ACT.Copy).then_inc(s_hi, 1)

                act.wait_ge(s_tc, 2 * (l + 1))
                high_pieces(0, 0, 4)
                modulate_xe(0)
                def store_y(e):
                    E = NE * l + e
                    act.wait_ge(s_wf, 2 * E + 2)
                    if e >= 2:
                        act.wait_ge(s_sct, 16 * (E - 1))
                    for h in range(2):
                        ins = act.activation(ysc[e % 2][0:M, 512 * h:512 * h + 512], pb(4 + h)[0:M, :], ACT.Copy,
                                             scale=gT[0:M, e:e + 1])
                    ins.then_inc(s_yc, 1)

                for e in range(NE):
                    high_pieces(e, 4, 11)
                    exp_gate(e, 0)
                    high_pieces(e, 11, 12)
                    if e:
                        store_y(e - 1)
                    if e + 1 < NE:
                        modulate_xe(e + 1)
                    high_pieces(e, 12, 16)
                    high_pieces(e + 1, 0, 3)
                    exp_gate(e, 1)
                    high_pieces(e + 1, 3, 4)
                store_y(NE - 1)
                for _ in range(2):
                    gate_rows(1, (6, 7))
                for n in rows:
                    if n:
                        act.wait_ge(s_yrs, n)
                    act.wait_ge(s_yl[n % 2], 16 * (n // 2 + 1))
                    act.activation(junk, yrow[n % 2], ACT.Square, accum_out=st[:, 28:29]).then_inc(s_yss, 1)

        @block.vector
        def _(dve):
            chain = [0]

            def link(ins):
                chain[0] += 1
                ins.then_inc(s_vch, 1)
                dve.wait_ge(s_vch, chain[0])

            dve.wait_ge(s_ach, 1)
            link(dve.tensor_scalar(crow2, crow2, 1.0, None, ALU.add))
            link(dve.reciprocal(crow2, crow2))
            dve.tensor_tensor(crow2, crow2, crow, ALU.mult).then_inc(s_cs, 1)
            dve.wait_ge(s_csT, 1)
            dve.tensor_copy(cT[:].rearrange("p c k -> p (c k)"), pb(0)[:, 0:2 * KC]).then_inc(s_cs, 1)
            dve.wait_ge(s_csT, 2)
            dve.tensor_copy(gcol[:].rearrange("p c k -> p (c k)"), pb(1)[:, 0:8 * KC]).then_inc(s_cs, 1)
            def normalise(n):
                dve.wait_ge(s_rs, n + 1)
                if n:
                    dve.wait_ge(s_xt, n)
                dve.tensor_scalar(xn, X[:, n % NT, :], st[:, 1:2], None, ALU.mult).then_inc(s_xn, 1)

            def modulation(l):
                for s in range(2):
                    for k in range(2):
                        dve.scalar_tensor_tensor(mscale[:, l, s, k, :], modcol[:, l, 24 * s + 8:24 * s + 16, k], 1.0,
                                                 gcol[:, :, 4 * s + l], ALU.add, ALU.mult)
                        ins = dve.tensor_tensor(gate[:, l, s, k, :], modcol[:, l, 24 * s + 16:24 * s + 24, k],
                                                gcol[:, :, 4 * s + 2 + l], ALU.mult)
                ins.then_inc(s_mod, 1)

            dve.wait_ge(s_cs, 3)
            for n in range(12):
                dve.wait_ge(s_adam, n + 1)
                dve.wait_ge(s_adab[n % 4], 16 * (n // 4 + 1))
                dve.tensor_tensor(ada_row[n % 4], ada_row[n % 4], pb(2 + n % 2)[0:2, :], ALU.add).then_inc(s_adar, 1)
            normalise(0)
            dve.wait_ge(s_adat, 12)
            link(dve.tensor_copy(modcol[:, 0].rearrange("p f k -> p (f k)"), pb(4)[:, 0:96]))
            modulation(0)

            def multiply_ada(n):
                no, q = n // 2, ADA_ORDER[n // 2]
                dve.wait_ge(s_aw[n % 2], 16 * (n // 2 + 1))
                if n % 2 == 0 and no >= 2:
                    dve.wait_ge(s_ar, no - 1)
                for j in range(4):
                    c, w = 4 * (n % 2) + j, ada_piece[n % 2][:, j, :]
                    for k in ((0, 1) if q < 8 else (c % 2,)):
                        acc, factor = ada_acc[no % 2][k], cT[:, c, (k if q < 8 else 1):(k if q < 8 else 1) + 1]
                        if c == 0 or (q >= 8 and c == 1):
                            ins = dve.tensor_scalar(acc, w, factor, None, ALU.mult)
                        else:
                            ins = dve.scalar_tensor_tensor(acc, w, factor, acc, ALU.mult, ALU.add)
                    if j < 3 and (q < 8 or j % 2 == 1):
                        link(ins)
                ins.then_inc(s_ap, 1)
                dve.wait_ge(s_ap, n + 1)

            dve.wait_ge(s_in2, 16 * (1 + 6 * DEPTH + 2))
            link(dve.tensor_scalar(nsink8[:], sink8[:], -INV_SCALE, None, ALU.mult))
            link(dve.tensor_scalar(sink8[:], sink8[:], INV_SCALE, None, ALU.mult))
            for l in range(DEPTH):
                link(dve.tensor_scalar(subgain[:, l, :], subgain[:, l, :], 1.0 - lam_init(l), None, ALU.mult))
                link(dve.tensor_tensor(lamp[:, l], lamv[:, l, 0:2, :], lamv[:, l, 2:4, :], ALU.mult))
            dve.tensor_reduce(lams[:].rearrange("p l j -> p (l j)"), lamp[:].rearrange("p l j d -> p (l j) d"), AX_X,
                              ALU.add).then_inc(s_vlam, 1)
            dve.wait_ge(s_ach, 2)
            for l in range(DEPTH):
                link(dve.tensor_tensor(nlam[:, l:l + 1], lams[:, l, 1:2], lams[:, l, 0:1], ALU.subtract))
                link(dve.tensor_scalar(nlam[:, l:l + 1], nlam[:, l:l + 1], lam_init(l), None, ALU.subtract))
            dve.wait_ge(s_const, 2)

            gate_no = [0]

            def gate_rows(l, s, k):
                q = gate_no[0]
                if q:
                    dve.wait_ge(s_gm, q)
                for c in range(KC):
                    ins = dve.tensor_scalar(diag[s][:, c, :], ident[:], gate[:, l, s, k, c:c + 1], None, ALU.mult)
                ins.then_inc(s_gd, 1)
                gate_no[0] += 1

            for l in range(DEPTH):
                rows = LAYER_ROWS[l]
                def rotate(src, t, heads, dim):
                    off = 0 if dim == HD else 128
                    table = rope[:, t - NC, off:off + 2 * dim]
                    cos = table[:, 0:dim].unsqueeze(1).broadcast_to([P, heads, dim])
                    sin = table[:, dim:2 * dim].rearrange("p (j e) -> p e j", e=2)
                    a = tmp[1][:, 0:heads * dim].rearrange("p (h d) -> p h d", d=dim)
                    b = tmp[2][:, 0:heads * dim].rearrange("p (h j e) -> p e h j", e=2, j=dim // 2)
                    s3 = src.rearrange("p (h d) -> p h d", d=dim)
                    s4 = src.rearrange("p (h j e) -> p e h j", e=2, j=dim // 2)
                    dve.tensor_tensor(a, s3, cos, ALU.mult)
                    for e in range(2):
                        ins = dve.tensor_tensor(b[:, e], s4[:, 1 - e],
                                                sin[:, e].unsqueeze(1).broadcast_to([P, heads, dim // 2]), ALU.mult)
                    link(ins)

                def place(what, width, dst, t, src):
                    dim = HD // 2 if what[1] == "b" else HD
                    out = (Qrows if what[0] == "q" else Krows)[:, t, dst:dst + width]
                    if what[1] == "d" or t < NC:
                        return dve.tensor_copy(out, src)
                    rotate(src, t, width // dim, dim)
                    return dve.tensor_tensor(out, tmp[1][:, 0:width], tmp[2][:, 0:width], ALU.add)

                if l:
                    normalise(NT * l)
                for t in range(NT):
                    n = NT * l + t
                    only_kv = l == DEPTH - 1 and t < NC
                    for g in range(5):
                        G = 5 * n + g
                        if g == 2 and t + 1 < NT:
                            normalise(n + 1)
                        if l == 0 and G < 24:
                            multiply_ada(2 * G)
                            multiply_ada(2 * G + 1)
                        if l == 0 and G == 25:
                            dve.wait_ge(s_ar, 24)
                            dve.wait_ge(s_z, 16 * N_CLEAR)
                            other, bias, sums = modcol[:, 1], pb(7)[:, 0:48], pb(6)[:, 0:96].rearrange("p (f k) -> p f k", k=2)
                            link(dve.memset(other, 0.0))
                            dve.tensor_copy(other[:, 0:16, 0], bias[:, 0:16])
                            link(dve.tensor_copy(other[:, :, 1], bias))
                            dve.tensor_tensor(other[:, 0:16, 0], other[:, 0:16, 0], sums[:, 0:16, 0], ALU.add)
                            link(dve.tensor_tensor(other[:, :, 1], other[:, :, 1], sums[:, :, 1], ALU.add))
                            modulation(1)
                        work = [x for x in GROUPS[g] if x[0] != "v" and not (only_kv and x[0][0] == "q")]
                        if not work:
                            continue
                        dve.wait_ge(s_raw, G + 1)
                        r = raw[G % 2]
                        if g == 0:
                            lo = 256 if only_kv else 0
                            heads = slice(lo // HD, 6)
                            nh = 6 - lo // HD
                            r3 = r[:, lo:384].rearrange("p (h d) -> p h d", d=HD)
                            n3 = tmp[0][:, lo:384].rearrange("p (h d) -> p h d", d=HD)
                            if only_kv and n == NT * l:
                                link(dve.memset(st[:, 2:8], 1.0))
                            link(dve.tensor_tensor(n3, r3, r3, ALU.mult))
                            dve.tensor_reduce(st[:, 2 + heads.start:8], n3, AX_X, ALU.add).then_inc(s_hss, 1)
                            dve.wait_ge(s_hrs, n + 1)
                            link(dve.tensor_tensor(n3, r3, st[:, 8 + heads.start:14].unsqueeze(2).broadcast_to([P, nh, HD]),
                                                   ALU.mult))
                            for j, (a, b) in enumerate(((0, 256), (256, 384))):
                                if a >= lo:
                                    v3 = tmp[0][:, a:b].rearrange("p (h d) -> p h d", d=HD)
                                    link(dve.tensor_tensor(v3, v3, qkgain[:, l, j, :].unsqueeze(1).broadcast_to(
                                        [P, (b - a) // HD, HD]), ALU.mult))
                            r = tmp[0]
                        for j, (what, col, width, dst) in enumerate(work):
                            ins = place(what, width, dst, t, r[:, col:col + width])
                            if j < len(work) - 1:
                                link(ins)
                        ins.then_inc(s_rawf, 1)
                        dve.wait_ge(s_rawf, RAW_READ[G])
                for t in range(NT):
                    n = NT * l + t
                    if n >= 2:
                        dve.wait_ge(s_kt, n - 1)
                    spans = [(b0, b1, d) for b0, b1, d in ((0, 2, HD), (2, 6, HD // 2), (6, 12, HD))]
                    for part in range(2):
                        for b0, b1, d in spans:
                            src = Krows[:, t, HD * b0:HD * b1].rearrange("p (h d) -> p h d", d=d)
                            hi, lo = (v[n % 2][:, b0:b1, :].rearrange("p b n -> p (b n)")
                                      .rearrange("p (h s d) -> p s h d", s=2, d=d) for v in (Kd, Kd_r))
                            if part == 0:
                                ins = dve.tensor_copy(lo[:, 0], src)
                            else:
                                ins = dve.tensor_tensor(lo[:, 1], src, hi[:, 0], ALU.subtract)
                        if part == 0:
                            link(ins)
                    ins.then_inc(s_kd, 1)
                    if t in (1, 3):
                        gate_rows(l, 0, t // 2)
                dve.wait_ge(s_rpl, 16 * 8 * (l + 1))
                bias = rpbT.rearrange("p h s c -> p (h s) c")
                mask = colmask[:].unsqueeze(1).broadcast_to([P, 56, GRID_W])
                link(dve.scalar_tensor_tensor(bias, bias, INV_SCALE, mask, ALU.mult, ALU.add))
                for step in STEPS[l]:
                    for v in step["turn"]:
                        if v["nk"] > 512:
                            m = v["m"]
                            dve.wait_ge(s_tn, m + 1)
                            if m >= 2:
                                dve.wait_ge(s_pv, m - 1)
                            dve.tensor_copy(PT[m % 2][:, 512:v["nk"]], pb(5)[:, 0:v["nk"] - 512]).then_inc(s_tb, 1)
                    u = step["entry"]
                    if u and not u["turn"]:
                        k, S = u["k"], pb(2 * (u["slot"] % 2), 2)
                        dve.wait_ge(s_sc, u["slot"] + 1)
                        if u["mixer"] == "C" and u["i"] >= 0:
                            if u["left"]:
                                link(dve.tensor_tensor(S[:, 256:384], S[:, 256:384], bandL[:], ALU.add))
                            if u["right"]:
                                e = u["nk"]
                                link(dve.tensor_tensor(S[:, e - P:e], S[:, e - P:e], bandR[:], ALU.add))
                        if u["mixer"] == "D" and u["i"] >= 0:
                            s0 = 6 - 2 * u["i"]
                            link(dve.tensor_tensor(S[:, 256:768], S[:, 256:768],
                                                   rpbT[:, u["h"], s0:s0 + 8, :].rearrange("p s c -> p (s c)"), ALU.add))
                        nm = nmx[:, k % 8:k % 8 + 1]
                        link(dve.tensor_reduce(nm, S[:, 0:u["nk"]], AX_X, ALU.max, negate=True))
                        if u["mixer"] == "C":
                            dve.tensor_scalar(nm, nm, nsink8[:, l, u["h"]:u["h"] + 1], SCALE, ALU.min, ALU.mult).then_inc(s_mx, 1)
                        else:
                            dve.tensor_scalar(nm, nm, SCALE_B if u["mixer"] == "B" else SCALE, None, ALU.mult).then_inc(s_mx, 1)
                    j = step["no"]
                    prev = STEPS[l][j - 1]["entry"] if j else None
                    if prev and not prev["turn"] and prev["mixer"] == "B" and prev["c"] == 1:
                        k = prev["k"]
                        dve.wait_ge(s_ex, prev["slot"] + 1)
                        a, b = (k - 1) % 8, k % 8
                        dve.reciprocal(rx[:, a:a + 1], sumx[:, a:a + 1])
                        link(dve.reciprocal(rx[:, b:b + 1], sumx[:, b:b + 1]))
                        link(dve.tensor_tensor(rx[:, b:b + 1], rx[:, b:b + 1], nlam[:, l:l + 1], ALU.mult))
                        p0, p1 = Pb[(k - 1) % 4][:, 0:prev["nk"]], Pb[k % 4][:, 0:prev["nk"]]
                        link(dve.tensor_scalar(p1, p1, rx[:, b:b + 1], None, ALU.mult))
                        dve.scalar_tensor_tensor(p0, p0, rx[:, a:a + 1], p1, ALU.mult, ALU.add).then_inc(s_cb, 1)
                    for v in step["pv"]:
                        m, k = v["m"], v["k"]
                        dst = Ost[:, v["t"], v["ocol"]:v["ocol"] + HD]
                        if v["mixer"] == "B":
                            dve.wait_ge(s_pv, m + 1)
                            dve.tensor_copy(dst, pb(6 + m % 2)[:, 0:HD]).then_inc(s_o, 1)
                        else:
                            r = rx[:, k % 8:k % 8 + 1]
                            if v["mixer"] == "C":
                                dve.wait_ge(s_sk, SINKS[k])
                                link(dve.tensor_tensor(sumx[:, k % 8:k % 8 + 1], sumx[:, k % 8:k % 8 + 1],
                                                       skx[:, k % 8:k % 8 + 1], ALU.add))
                            link(dve.reciprocal(r, sumx[:, k % 8:k % 8 + 1]))
                            dve.wait_ge(s_pv, m + 1)
                            dve.tensor_scalar(dst, pb(6 + m % 2)[:, 0:HD], r, None, ALU.mult).then_inc(s_o, 1)
                dve.wait_ge(s_o, LAYER_VALUES[l][-1] + 1)
                dve.wait_ge(s_pv, LAYER_VALUES[l][-1] + 1)

                def sub_norm(n):
                    t = ROW_TILES[n][1]
                    o = Ost[:, t, 256:512]
                    o3 = o.rearrange("p (h d) -> p h d", d=HD)
                    sq = upd[:, 0:256].rearrange("p (h d) -> p h d", d=HD)
                    if n >= 3:
                        dve.wait_ge(s_xu, n - 2)
                    link(dve.tensor_tensor(sq, o3, o3, ALU.mult))
                    dve.tensor_reduce(st[:, 16:20], sq, AX_X, ALU.add).then_inc(s_bss, 1)
                    dve.wait_ge(s_brs, n + 1)
                    link(dve.tensor_tensor(o3, o3, st[:, 20:24].unsqueeze(2).broadcast_to([P, 4, HD]), ALU.mult))
                    dve.tensor_tensor(o3, o3, subgain[:, l, :].unsqueeze(1).broadcast_to([P, 4, HD]), ALU.mult
                                      ).then_inc(s_on, 1)

                def update(n):
                    t = ROW_TILES[n][1]
                    dve.wait_ge(s_ors, n + 1)
                    link(dve.scalar_tensor_tensor(upd, pb(2 + 2 * (n % 2), 2), st[:, 25:26], GB[0][:, kind(t), :],
                                                  ALU.mult, ALU.mult))
                    dve.tensor_tensor(X[:, t, :], X[:, t, :], upd, ALU.add).then_inc(s_xu, 1)

                def normalise_f(n):
                    dve.wait_ge(s_frs, n + 1)
                    if n >= 2:
                        dve.wait_ge(s_ft, n - 1)
                        dve.wait_ge(s_fst[n % 2], 16 * (n // 2))
                    dve.tensor_scalar(fxn[n % 2], X[:, ROW_TILES[n][1], :], st[:, 27:28], None, ALU.mult).then_inc(s_fxn, 1)

                def store_f(n):
                    t = ROW_TILES[n][1]
                    dve.wait_ge(s_ft, n + 1)
                    if n >= 2:
                        dve.wait_ge(s_lg, n - 1)
                    for c in range(4, 8):
                        ins = dve.tensor_scalar(fhT[n % 2][:, c, :], pb(7)[:, P * (c - 4):P * (c - 4) + P],
                                                mscale[:, l, 1, kind(t), c:c + 1], modcol[:, l, 24 + c, kind(t):kind(t) + 1],
                                                ALU.mult, ALU.add)
                    ins.then_inc(s_fv, 1)

                def affinities(n):
                    dve.wait_ge(s_lg, n + 1)
                    dve.tensor_reduce(st[:, 32 + n % 2:33 + n % 2], pb(6)[:, 0:NE], AX_X, ALU.max, negate=True
                                      ).then_inc(s_lm, 1)
                    dve.wait_ge(s_le, n + 1)
                    link(dve.reciprocal(st[:, 36 + n % 2:37 + n % 2], st[:, 34 + n % 2:35 + n % 2]))
                    dve.tensor_scalar(lg[:, n % 2, :], lg[:, n % 2, :], st[:, 36 + n % 2:37 + n % 2], None, ALU.mult
                                      ).then_inc(s_lp, 1)

                def store_aff(n):
                    t = ROW_TILES[n][1]
                    dve.wait_ge(s_lt, n + 1)
                    dve.tensor_copy(affT[:, P * t:P * t + P], pb(7)[0:NE, 0:P]).then_inc(s_lc, 1)

                def top(lo, hi, cap, col):
                    src = affT[:, lo:hi]
                    for r in range(col, col + cap, 8):
                        link(dve.max(vals[:, r:r + 8], src))
                        ins = dve.max_index(idxu[:, r:r + 8], vals[:, r:r + 8], src)
                        if r + 8 < col + cap:
                            rest = aff_rest[lo]
                            ins = dve.match_replace(rest, vals[:, r:r + 8], src, -1.0)
                            src = rest
                        link(ins)
                    return dve.tensor_scalar(idxf[:, col:col + cap], idxu[:, col:col + cap],
                                             float(lo - P * first_tile(l)), None, ALU.add)

                sub_norm(rows[0])
                sub_norm(rows[1])
                dve.wait_ge(s_gb, gate_no[0])
                for n in range(rows[0], rows[-1] + 3):
                    if n - 2 >= rows[0]:
                        store_f(n - 2)
                    if rows[0] <= n - 1 <= rows[-1]:
                        update(n - 1)
                        normalise_f(n - 1)
                    if n - 2 >= rows[0]:
                        affinities(n - 2)
                    if n + 2 <= rows[-1]:
                        sub_norm(n + 2)
                    if n - 2 >= rows[0]:
                        store_aff(n - 2)
                    if rows[0] == 0 and n == 4:
                        dve.wait_ge(s_lc, NC)
                        link(top(0, CTX, CAP_C, CAP_X))
                dve.wait_ge(s_lc, rows[-1] + 1)
                dve.wait_ge(s_xu, rows[-1] + 1)
                top(CTX, CTX + SEQ, CAP_X, 0).then_inc(s_top, 1)
                M = 96 if l < DEPTH - 1 else CAP_X
                dve.wait_ge(s_tt, l + 1)
                dve.tensor_copy(gT[0:M, :], pb(4)[0:M, 0:NE]).then_inc(s_tc, 1)
                dve.tensor_copy(idxT[0:M, 0:NE], pb(5)[0:M, 0:NE]).then_inc(s_tc, 1)
                def low_pieces(e, first, last):
                    if e == NE:
                        return
                    for q in range(first, last):
                        part, piece = q // 4, 16 * (NE * l + e) + q
                        dve.wait_ge(s_hi, piece + 1)
                        hi, lo = (v[piece % PIECES].rearrange("p c n -> p (c n)") for v in (w_hi, w_lo))
                        dve.tensor_tensor(lo, unit[SLOT[part]][:, D * (q % 4):D * (q % 4) + D], hi.bitcast(F32),
                                          ALU.subtract).then_inc(s_lo, 1)

                def hidden(e, half):
                    E = NE * l + e
                    dve.wait_ge(s_eg, 2 * E + half + 1)
                    g = sg[0:M, half, :]
                    link(dve.tensor_scalar(g, g, 1.0, None, ALU.add))
                    link(dve.reciprocal(g, g))
                    link(dve.tensor_tensor(g, g, pb(2 * half)[0:M, :], ALU.mult))
                    if E:
                        dve.wait_ge(s_hst, 2 * (E - 1) + half + 1)
                    dve.tensor_tensor(hs[0:M, 512 * half:512 * half + 512], g, pb(2 * half + 1)[0:M, :], ALU.mult
                                      ).then_inc(s_hs, 1)

                def store_hidden(e, half):
                    E = NE * l + e
                    dve.wait_ge(s_hst, 2 * E + half + 1)
                    if E:
                        dve.wait_ge(s_wf, 2 * E)
                    dve.tensor_copy(hsT[:, 4 * half:4 * half + 4, 0:M],
                                    pb(6 + half).rearrange("p (c n) -> p c n", n=P)[:, :, 0:M]).then_inc(s_hsc, 1)

                low_pieces(0, 0, 4)
                for e in range(NE):
                    low_pieces(e, 4, 8)
                    if e:
                        store_hidden(e - 1, 1)
                    low_pieces(e, 8, 11)
                    hidden(e, 0)
                    low_pieces(e, 11, 16)
                    store_hidden(e, 0)
                    low_pieces(e + 1, 0, 3)
                    hidden(e, 1)
                    low_pieces(e + 1, 3, 4)
                store_hidden(NE - 1, 1)
                dve.wait_ge(s_pr, 16 * NE * (l + 1))
                for k in range(2):
                    gate_rows(l, 1, k)
                dve.wait_ge(s_gb, gate_no[0])
                for n in rows:
                    t = ROW_TILES[n][1]
                    dve.wait_ge(s_yrs, n + 1)
                    if n:
                        dve.wait_ge(s_yu, n)
                    link(dve.scalar_tensor_tensor(yupd, yrow[n % 2], st[:, 29:30], GB[1][:, kind(t), :], ALU.mult, ALU.mult))
                    dve.tensor_tensor(X[:, t, :], X[:, t, :], yupd, ALU.add).then_inc(s_yu, 1)


_INS = ["x", "c", "ctx", "c_ctx", "w_ada", "b_ada", "g_pre_mix", "g_post_mix", "g_pre_ffn", "g_post_ffn", "w_in", "w_out",
        "q_gain_a", "k_gain_a", "lam_q1", "lam_k1", "lam_q2", "lam_k2", "subln_gain_b", "sink_c", "rpb_d", "w_router",
        "w_gate", "w_up", "w_down"]


def kernel(**inputs):
    import concourse.bacc as _bacc
    from concourse.bass_utils import run_bass_kernel_spmd as _run

    nc = _bacc.Bacc("TRN2", target_bir_lowering=False, num_devices=1)
    arrays = {"in_" + n: np.ascontiguousarray(inputs[n]) for n in _INS}
    arrays["in_rope"] = rope_table()
    aps = {n[3:]: nc.dram_tensor(n, a.shape, F32, kind="ExternalInput").ap() for n, a in arrays.items()}
    out = nc.dram_tensor("out_0", (1, SEQ, D), F32, kind="ExternalOutput").ap()

    def scratch(name, shape):
        return nc.dram_tensor(name, shape, F32, kind="Internal").ap()

    xn_dram = [scratch(f"xn_{l}", (SEQ + (CTX if l < DEPTH - 1 else 0), D)) for l in range(DEPTH)]
    y_dram = [scratch(f"y_{l}", (SEQ + (CTX if l < DEPTH - 1 else 0), D)) for l in range(DEPTH)]
    rp_dram = scratch("rp", (DEPTH, GRID_W, 60 * P))
    hybrid_dit(nc, aps, out, xn_dram, y_dram, rp_dram)
    r = _run(nc, [arrays], core_ids=[0])
    return r.results[0]["out_0"]
```
